# Optimizing a Trainium2 kernel written in Bass

```python
import math
import jax, jax.numpy as jnp
from jax import lax
import numpy as np

D_MODEL = 1024
BATCH = 1
SEQ = 512
DEPTH = 1

ATTN_HEADS = 8
HEAD_DIM = 64
ATTN_WIDTH = ATTN_HEADS * HEAD_DIM
IDX_HEADS = 8
IDX_DIM = 64
TOPK_MAX = 256
Q_BLOCK = 128
POOL_WINDOWS = (2, 4, 8, 16)
POOL_GROUPS = len(POOL_WINDOWS)
POOL_WIDTH = D_MODEL - ATTN_WIDTH
POOL_GROUP_DIM = POOL_WIDTH // POOL_GROUPS
REL_BUCKETS = 32
REL_MAX_DIST = 128
N_GROUPS = 4
EXPERTS_PER_GROUP = 8
N_EXPERTS = N_GROUPS * EXPERTS_PER_GROUP
TOP_K_INNER = 2
D_EXPERT = 256
LN_EPS = 1e-5
DEEPNORM_ALPHA = (2 * DEPTH) ** 0.25
DEEPNORM_BETA = (8 * DEPTH) ** -0.25
Q_OFF = 0
K_OFF = Q_OFF + ATTN_WIDTH
V_OFF = K_OFF + ATTN_WIDTH
IQ_OFF = V_OFF + ATTN_WIDTH
IK_OFF = IQ_OFF + IDX_HEADS * IDX_DIM
IW_OFF = IK_OFF + IDX_DIM
P_OFF = IW_OFF + IDX_HEADS
IN_WIDTH = P_OFF + POOL_WIDTH

kernel_name = 'hybrid_dsa_pool_hmoe_deepnorm'

def layer_norm(x, g, b):
    xf = x.astype(jnp.float32)
    mu = jnp.mean(xf, axis=-1, keepdims=True)
    var = jnp.mean(jnp.square(xf - mu), axis=-1, keepdims=True)
    y = (xf - mu) * lax.rsqrt(var + LN_EPS) * g.astype(jnp.float32) + b.astype(jnp.float32)
    return y.astype(x.dtype)

def rel_bucket(dist):
    max_exact = REL_BUCKETS // 2
    n = jnp.maximum(dist, 0)
    nf = jnp.maximum(n, 1).astype(jnp.float32)
    large = max_exact + (jnp.log(nf / max_exact) / math.log(REL_MAX_DIST / max_exact)
                         * (REL_BUCKETS - max_exact)).astype(jnp.int32)
    large = jnp.minimum(large, REL_BUCKETS - 1)
    return jnp.where(n < max_exact, n, large)

def dsa_attention(q, k, v, iq, ik, iw, rel_bias):
    B, S = q.shape[0], q.shape[1]
    k_top = min(TOPK_MAX, S // 4)
    n_blocks = S // Q_BLOCK
    key_pos = jnp.arange(S)

    def block(i):
        start = i * Q_BLOCK
        qb = lax.dynamic_slice_in_dim(q, start, Q_BLOCK, axis=1)
        iqb = lax.dynamic_slice_in_dim(iq, start, Q_BLOCK, axis=1)
        iwb = lax.dynamic_slice_in_dim(iw, start, Q_BLOCK, axis=1)
        q_pos = start + jnp.arange(Q_BLOCK)
        dots = jnp.einsum('bqjd,bsd->bqjs', iqb, ik).astype(jnp.float32) * (IDX_DIM ** -0.5)
        score = jnp.einsum('bqj,bqjs->bqs', iwb.astype(jnp.float32), jax.nn.relu(dots))
        causal = key_pos[None, :] <= q_pos[:, None]
        score = jnp.where(causal[None], score, -jnp.inf)
        _, sel = lax.top_k(score, k_top)
        valid = sel <= q_pos[None, :, None]
        k_sel = jax.vmap(lambda kb, ib: kb[ib])(k, sel).reshape(B, Q_BLOCK, k_top, ATTN_HEADS, HEAD_DIM)
        v_sel = jax.vmap(lambda vb, ib: vb[ib])(v, sel).reshape(B, Q_BLOCK, k_top, ATTN_HEADS, HEAD_DIM)
        logits = jnp.einsum('bqhd,bqkhd->bqhk', qb, k_sel).astype(jnp.float32) * (HEAD_DIM ** -0.5)
        bias = rel_bias[rel_bucket(q_pos[None, :, None] - sel)]
        logits = logits + jnp.moveaxis(bias, -1, 2).astype(jnp.float32)
        logits = jnp.where(valid[:, :, None, :], logits, -jnp.inf)
        p = jax.nn.softmax(logits, axis=-1).astype(v.dtype)
        return jnp.einsum('bqhk,bqkhd->bqhd', p, v_sel)

    out = lax.map(block, jnp.arange(n_blocks))
    return jnp.moveaxis(out, 0, 1).reshape(B, S, ATTN_WIDTH)

def pool_mixer(u, w_pool, pool_scale):
    B, S = u.shape[0], u.shape[1]
    ug = u.reshape(B, S, POOL_GROUPS, POOL_GROUP_DIM)
    pos = jnp.arange(S)
    outs = []
    for g, w in enumerate(POOL_WINDOWS):
        ch = ug[:, :, g].astype(jnp.float32)
        c = lax.cumsum(ch, axis=1)
        c_shift = jnp.pad(c, ((0, 0), (w, 0), (0, 0)))[:, :S]
        count = jnp.minimum(pos + 1, w).astype(jnp.float32)[None, :, None]
        outs.append((c - c_shift) / count - ch)
    pooled = jnp.stack(outs, axis=2).astype(u.dtype)
    mixed = jnp.einsum('bsgc,gcd->bsgd', pooled, w_pool)
    return mixed.reshape(B, S, POOL_WIDTH) * pool_scale

def hier_moe(h, w_r1, b_r1, w_r2, b_r2, w_gate, w_up, w_down):
    B, S, D = h.shape
    t = h.reshape(-1, D)
    pg = jax.nn.softmax((t @ w_r1).astype(jnp.float32) + b_r1.astype(jnp.float32), axis=-1)
    pg_top, g = lax.top_k(pg, 1)
    lf = ((t @ w_r2).astype(jnp.float32) + b_r2.astype(jnp.float32)).reshape(-1, N_GROUPS, EXPERTS_PER_GROUP)
    lf_g = jnp.take_along_axis(lf, g[:, :, None], axis=1)[:, 0]
    pf = jax.nn.softmax(lf_g, axis=-1)
    pe, e_local = lax.top_k(pf, TOP_K_INNER)
    weights = pg_top * pe / jnp.sum(pe, axis=-1, keepdims=True)
    eid = g * EXPERTS_PER_GROUP + e_local
    combine = jnp.einsum('tk,tke->te', weights,
                         jax.nn.one_hot(eid, N_EXPERTS, dtype=jnp.float32)).astype(h.dtype)
    y = jnp.zeros_like(t)
    for e in range(N_EXPERTS):
        a = jax.nn.silu(t @ w_gate[e]) * (t @ w_up[e])
        y = y + combine[:, e:e + 1] * (a @ w_down[e])
    return y.reshape(B, S, D)

def setup_inputs(seed: int = 0) -> dict:
    key = jax.random.key(seed)
    ks = jax.random.split(key, 17)
    nrm = lambda k, shape, s: jax.random.normal(k, shape, jnp.float32) * s
    col_scale = jnp.ones((IN_WIDTH,), jnp.float32).at[V_OFF:IQ_OFF].set(DEEPNORM_BETA)
    return {
        'x': nrm(ks[0], (BATCH, SEQ, D_MODEL), 1.0),
        'w_in': nrm(ks[1], (DEPTH, D_MODEL, IN_WIDTH), D_MODEL ** -0.5) * col_scale,
        'w_pool': nrm(ks[2], (DEPTH, POOL_GROUPS, POOL_GROUP_DIM, POOL_GROUP_DIM), POOL_GROUP_DIM ** -0.5),
        'pool_scale': 1.0 + nrm(ks[3], (DEPTH, POOL_WIDTH), 0.05),
        'w_out': nrm(ks[4], (DEPTH, D_MODEL, D_MODEL), D_MODEL ** -0.5) * DEEPNORM_BETA,
        'rel_bias': nrm(ks[5], (REL_BUCKETS, ATTN_HEADS), 0.5),
        'ln1_g': 1.0 + nrm(ks[6], (DEPTH, D_MODEL), 0.05),
        'ln1_b': nrm(ks[7], (DEPTH, D_MODEL), 0.02),
        'w_r1': nrm(ks[8], (DEPTH, D_MODEL, N_GROUPS), D_MODEL ** -0.5),
        'b_r1': nrm(ks[9], (DEPTH, N_GROUPS), 0.01),
        'w_r2': nrm(ks[10], (DEPTH, D_MODEL, N_EXPERTS), D_MODEL ** -0.5),
        'b_r2': nrm(ks[11], (DEPTH, N_EXPERTS), 0.01),
        'w_gate': nrm(ks[12], (DEPTH, N_EXPERTS, D_MODEL, D_EXPERT), D_MODEL ** -0.5),
        'w_up': nrm(ks[13], (DEPTH, N_EXPERTS, D_MODEL, D_EXPERT), D_MODEL ** -0.5),
        'w_down': nrm(ks[14], (DEPTH, N_EXPERTS, D_EXPERT, D_MODEL), D_EXPERT ** -0.5) * DEEPNORM_BETA,
        'ln2_g': 1.0 + nrm(ks[15], (DEPTH, D_MODEL), 0.05),
        'ln2_b': nrm(ks[16], (DEPTH, D_MODEL), 0.02),
    }

def reference(x, w_in, w_pool, pool_scale, w_out, rel_bias, ln1_g, ln1_b, w_r1, b_r1, w_r2, b_r2,
              w_gate, w_up, w_down, ln2_g, ln2_b):
    B, S = x.shape[0], x.shape[1]
    h = x
    for l in range(DEPTH):
        proj = h @ w_in[l]
        q = proj[..., Q_OFF:K_OFF].reshape(B, S, ATTN_HEADS, HEAD_DIM)
        k = proj[..., K_OFF:V_OFF]
        v = proj[..., V_OFF:IQ_OFF]
        iq = proj[..., IQ_OFF:IK_OFF].reshape(B, S, IDX_HEADS, IDX_DIM)
        ik = proj[..., IK_OFF:IW_OFF]
        iw = proj[..., IW_OFF:P_OFF] * (IDX_HEADS ** -0.5)
        u = proj[..., P_OFF:IN_WIDTH]
        attn = dsa_attention(q, k, v, iq, ik, iw, rel_bias)
        pooled = pool_mixer(u, w_pool[l], pool_scale[l])
        mix = jnp.concatenate([attn, pooled], axis=-1) @ w_out[l]
        h = layer_norm(DEEPNORM_ALPHA * h + mix, ln1_g[l], ln1_b[l])
        ffn = hier_moe(h, w_r1[l], b_r1[l], w_r2[l], b_r2[l], w_gate[l], w_up[l], w_down[l])
        h = layer_norm(DEEPNORM_ALPHA * h + ffn, ln2_g[l], ln2_b[l])
    return h


_drawn_inputs = setup_inputs


def setup_inputs(seed=0):
    import zlib

    import numpy as np

    out = dict(_drawn_inputs(seed))
    spreads = {}
    factors = {'pool_scale': 3.225, 'rel_bias': 2.778, 'b_r1': 29.891, 'b_r2': 8.0, 'ln2_b': 2.861}
    for name, (base, spread) in spreads.items():
        noise = np.random.default_rng([zlib.crc32(name.encode()), seed]).standard_normal(out[name].shape)
        drawn = base * np.exp(spread * noise) if base else spread * noise
        out[name] = __import__('jax').numpy.asarray(drawn.astype(out[name].dtype))
    for name, factor in factors.items():
        out[name] = (out[name] * factor).astype(out[name].dtype)
    return out
```

```python
import math
from contextlib import ExitStack

import numpy as np

import concourse.bass as bass
from concourse import mybir

F32 = mybir.dt.float32
BF16 = mybir.dt.bfloat16
U32 = mybir.dt.uint32
I32 = mybir.dt.int32
ALU = mybir.AluOpType
ACT = mybir.ActivationFunctionType
AX = mybir.AxisListType

P = 128
SEQ = 512
D = 1024
NT = SEQ // P
KD = D // P
HEADS = 8
HD = 64
AW = HEADS * HD
NA = AW // P
TOPK = min(256, SEQ // 4)
WINDOWS = (2, 4, 8, 16)
PAD = WINDOWS[-1]
BUCKETS = 32
MAX_DIST = 128
Q_OFF, K_OFF, V_OFF, IQ_OFF = 0, AW, 2 * AW, 3 * AW
IK_OFF = IQ_OFF + AW
IW_OFF = IK_OFF + HD
U_OFF = IW_OFF + HEADS
GROUPS = 4
PER_GROUP = 8
NE = GROUPS * PER_GROUP
DE = 256
ME = DE // P
CAP = 64
SLOTS = 6
EPS = 1e-5
ALPHA = 2.0 ** 0.25
BIG = 1e30
NONCAUSAL = -1e38
TAKEN = -3e38
TW = SEQ + P
SCALE = HD ** -0.5


def bucket_onehot():
    n = np.maximum(SEQ - 1 - np.arange(TW), 0)
    half = BUCKETS // 2
    nf = np.maximum(n, 1).astype(np.float32)
    large = half + (np.log(nf / np.float32(half)) / np.float32(math.log(MAX_DIST / half)) * np.float32(BUCKETS - half)).astype(np.int32)
    b = np.where(n < half, n, np.minimum(large, BUCKETS - 1))
    return (b[None, :] == np.arange(BUCKETS)[:, None]).astype(np.float32)


def head_counts():
    t = np.arange(PAD) + 1
    return np.stack([w / np.minimum(t, w) for w in WINDOWS]).astype(np.float32)


def layer_kernel(nc, x, w_in, w_pool, pool_scale, w_out, rel_bias, ln1_g, ln1_b, w_r1, b_r1, w_r2, b_r2,
                 w_gate, w_up, w_down, ln2_g, ln2_b, onehot, headfix, out):
    ctx = ExitStack()
    with ctx:
        base = [(nc.sbuf_base + 63) // 64 * 64]
        KB = 1024

        def at(name, offset, shape, dt=F32):
            return nc.alloc_sbuf_tensor_at(name, [P, *shape], dt, offset=base[0] + offset)

        SLOT = 3 * KD * DE * 4
        wg, wu, wd = [], [], []
        for j in range(SLOTS):
            wg.append(at(f"wg{j}", j * SLOT, [KD, DE]))
            wu.append(at(f"wu{j}", j * SLOT + 8 * KB, [KD, DE]))
            wd.append(at(f"wd{j}", j * SLOT + 16 * KB, [ME, D]))
        o = SLOT
        qT = at("qT", o, [NA, SEQ]); o += 8 * KB
        kT = at("kT", o, [NA, SEQ]); o += 8 * KB
        iqT = at("iqT", o, [NA, SEQ]); o += 8 * KB
        v_sb = at("v_sb", o, [NT, AW]); o += 8 * KB
        bias8 = at("bias8", o, [HEADS, SEQ]); o += 16 * KB
        uT = at("uT", o, [NA, PAD + SEQ]); o += NA * (PAD + SEQ) * 4
        keep = [None] + [at(f"keep{b}", o + 256 * (b - 1) * (b + 2), [P * (b + 1)]) for b in range(1, NT)]; o += 4608
        wik = at("wik", o, [KD, P])
        lg = [at(f"lg{i}", o + 2 * KB * i, [SEQ]) for i in range(3)]; o += 6 * KB
        pT = [at(f"pT{i}", o + 2 * KB * i, [SEQ]) for i in range(2)]; o += 4 * KB
        assert o <= 4 * SLOT
        RB = KD * AW * 4
        ring = [at(f"ring{i}", 4 * SLOT + RB * i, [KD, AW]) for i in range(3)]
        wo = [at("wo0", 4 * SLOT + 2 * RB, [KD // 2, D]), at("wo1", 4 * SLOT, [KD // 2, D])]
        g1 = at("g1", 4 * SLOT + RB, [D])
        b1 = at("b1", 4 * SLOT + RB + 4 * KB, [D])
        yg = [[at(f"yg{t}_{c}", (2 * t + c) * 4 * KB, [D]) for c in range(2)] for t in range(NT)]
        o_rows = at("o_rows", 2 * SLOT, [NT, D])
        o_rowsT = at("o_rowsT", 3 * SLOT, [KD, SEQ])
        o_sil = at("o_sil", 5 * SLOT, [ME, SEQ])
        o_act = at("o_act", 5 * SLOT + 4 * KB, [ME, SEQ])
        OSLOT = 4
        o = 6 * SLOT
        h = at("h", o, [NT, D]); o += 16 * KB
        xT = at("xT", o, [KD, SEQ])
        mixT = at("mixT", o, [KD, SEQ])
        sel = at("sel", o, [NT, NE, CAP], BF16)
        xe = [at(f"xe{i}", o + 4 * KB * i, [D]) for i in range(2)]
        ye = [at(f"ye{i}", o + 8 * KB + 4 * KB * i, [D]) for i in range(2)]
        o += 16 * KB
        hT = [at(f"hT{i}", o + 4 * KB * i, [KD, P]) for i in range(2)]
        ptmp = [at(f"ptmp{i}", o + 2176 * i, [PAD + SEQ]) for i in range(2)]
        xeT = [at(f"xeT{i}", o + 2 * KB * i, [KD, CAP]) for i in range(2)]
        act_e = [at(f"act_e{i}", o + 4 * KB + 512 * i, [ME, CAP]) for i in range(2)]
        sil = [at(f"sil{i}", o + 5 * KB + 512 * i, [ME, CAP]) for i in range(2)]
        o += 8 * KB
        ikT = at("ikT", o, [SEQ])
        score = at("score", o + 2 * KB, [SEQ])
        relu = [at(f"relu{i}", o + 4 * KB + 2 * KB * i, [SEQ]) for i in range(4)]
        bm = [at(f"bm{i}", o + 4 * KB + 2 * KB * i, [SEQ]) for i in range(2)]
        g2 = at("g2", o, [D])
        b2 = at("b2", o + 4 * KB, [D])
        o += 12 * KB
        cursor = [o]

        def small(name, shape, dt=F32):
            n = int(np.prod(shape)) * (2 if dt == BF16 else 4)
            t = at(name, cursor[0], shape, dt)
            cursor[0] += (n + 31) // 32 * 32
            return t

        ident = small("ident", [P])
        tri = small("tri", [P])
        ones = small("ones", [P])
        flip = small("flip", [P])
        wiw = small("wiw", [KD, HEADS])
        iw = small("iw", [NT, HEADS])
        wpool = small("wpool", [NA, P])
        pscale = small("pscale", [NA])
        relb = small("relb", [HEADS])
        hfix = small("hfix", [NA, PAD])
        wr = small("wr", [KD, GROUPS + NE])
        br = small("br", [GROUPS + NE])
        m8 = small("m8", [8])
        nmx = small("nmx", [4])
        rsum = small("rsum", [4])
        rinv = small("rinv", [4])
        stats = small("stats", [2, 6])
        mv = small("mv", [2])
        var_e = small("var_e", [1])
        std = small("std", [1])
        rstd = small("rstd", [1])
        iota_e = small("iota_e", [NE])
        gid = small("gid", [GROUPS, PER_GROUP])
        iota_r = small("iota_r", [CAP])
        tokval_f = small("tokval_f", [NT, 2])
        tokval = small("tokval", [NT, 2], BF16)
        gl = small("gl", [NT, 8])
        lf = small("lf", [NE])
        gm8 = small("gm8", [8])
        gi8 = small("gi8", [8], U32)
        gidx = small("gidx", [1])
        em8 = small("em8", [NT, 8])
        ei8 = small("ei8", [8], U32)
        eidx = small("eidx", [NT, 2])
        rk = small("rk", [NT, 2])
        fits = small("fits", [NT, 2])
        wfit = small("wfit", [NT, 2])
        over = small("over", [NT, NE])
        over_e = small("over_e", [NT])
        pen = small("pen", [NE])
        hot = small("hot", [NT, 2, NE])
        hsum = small("hsum", [NT, NE])
        neg = small("neg", [NT, 2])
        zs = small("zs", [NT, 2])
        ex = small("ex", [NT, 4])
        wt = small("wt", [NT, 2])
        rank1 = small("rank1", [NT, NE])
        slotf = small("slotf", [NT, 2])
        sloti = small("sloti", [NT, 2], U32)
        scr = small("scr", [NE])
        lst = small("lst", [NE, 2])
        lsti = small("lsti", [NE], U32)
        cur = [small(f"cur{i}", [1], U32) for i in range(2)]
        most = small("most", [1])
        mosti = small("mosti", [1], I32)
        brow = at("brow", 0, [TW])
        hot_c = at("hot_c", 4 * KB, [TW])
        bias_up = at("bias_up", 8 * KB, [HEADS, SEQ])
        assert base[0] + cursor[0] <= nc.sbuf_usable_end, (base[0] + cursor[0], nc.sbuf_usable_end)

        bank = [ctx.enter_context(nc.psum_tensor(f"bank{i}", [P, 512], F32)) for i in range(8)]

        h_dram = nc.dram_tensor("h_rows", (SEQ, D), F32, kind="Internal").ap()
        y_dram = nc.dram_tensor("y_rows", (NE * CAP, D), F32, kind="Internal").ap()
        row_dram = nc.dram_tensor("bias_rows", (HEADS, TW), F32, kind="Internal")

        def sem(name):
            return ctx.enter_context(nc.semaphore(name))

        x_in = [sem(f"x_in{t}") for t in range(NT)]
        group_in = [sem(f"group_in{i}") for i in range(3)]
        wo_in = sem("wo_in")
        ln1_in = sem("ln1_in")
        ln2_in = sem("ln2_in")
        small_in = sem("small_in")
        onehot_in = sem("onehot_in")
        consts_ready = sem("consts_ready")
        pool_chain = sem("pool_chain")
        dve_chain = sem("dve_chain")
        act_chain = sem("act_chain")
        xT_ps = sem("xT_ps")
        xT_act = sem("xT_act")
        xT_dve = sem("xT_dve")
        row_ps = sem("row_ps")
        row_ready = sem("row_ready")
        row_out = sem("row_out")
        bias_in = sem("bias_in")
        bias_ready = sem("bias_ready")
        flip_ps = sem("flip_ps")
        flip_sb = sem("flip_sb")
        proj_ps = sem("proj_ps")
        proj_sb = sem("proj_sb")
        iw_ps = sem("iw_ps")
        iw_ready = sem("iw_ready")
        dots_ps = sem("dots_ps")
        relu_ready = sem("relu_ready")
        relu_used = sem("relu_used")
        score_sum = sem("score_sum")
        score_masked = sem("score_masked")
        keep_ready = sem("keep_ready")
        pooled_ready = sem("pooled_ready")
        mixed_ps = sem("mixed_ps")
        mixed_sb = sem("mixed_sb")
        qk_ps = sem("qk_ps")
        bm_ready = sem("bm_ready")
        logit_ready = sem("logit_ready")
        exp_ready = sem("exp_ready")
        rinv_ready = sem("rinv_ready")
        prob_ready = sem("prob_ready")
        pT_ps = sem("pT_ps")
        pT_ready = sem("pT_ready")
        pv_ps = sem("pv_ps")
        attn_sb = sem("attn_sb")
        out_ps = sem("out_ps")
        res_ready = sem("res_ready")
        var_ready = sem("var_ready")
        std_ready = sem("std_ready")
        norm_ready = sem("norm_ready")
        h_ready = sem("h_ready")
        h_stored = sem("h_stored")
        hT_ps = sem("hT_ps")
        hT_ready = sem("hT_ready")
        router_ps = sem("router_ps")
        router_sb = sem("router_sb")
        top_ready = sem("top_ready")
        gate_exp = sem("gate_exp")
        hot_ready = sem("hot_ready")
        rank_ps = sem("rank_ps")
        sel_ready = sem("sel_ready")
        list_ps = sem("list_ps")
        list_ready = sem("list_ready")
        slot_ready = sem("slot_ready")
        w_in_slot = [sem(f"w_in_slot{j}") for j in range(SLOTS)]
        cur_ready = sem("cur_ready")
        gather_begun = sem("gather_begun")
        rows_begun = sem("rows_begun")
        gathered = [sem(f"gathered{i}") for i in range(2)]
        xeT_ps = sem("xeT_ps")
        xeT_ready = sem("xeT_ready")
        gu_ps = sem("gu_ps")
        silu_ready = sem("silu_ready")
        act_ready = sem("act_ready")
        y_ps = sem("y_ps")
        y_lo = sem("y_lo")
        y_hi = sem("y_hi")
        y_stored = [sem(f"y_stored{i}") for i in range(2)]
        y_gathered = [sem(f"y_gathered{t}") for t in range(NT)]
        out_stored = sem("out_stored")
        count_ready = sem("count_ready")
        o_rows_in = sem("o_rows_in")
        o_rowsT_ps = sem("o_rowsT_ps")
        o_rowsT_ready = sem("o_rowsT_ready")
        o_w_in = sem("o_w_in")
        o_gu_ps = sem("o_gu_ps")
        o_silu_ready = sem("o_silu_ready")
        o_act_ready = sem("o_act_ready")
        o_weight_ready = sem("o_weight_ready")
        o_y_ps = sem("o_y_ps")
        o_added = sem("o_added")
        o_chain = sem("o_chain")

        group_cols = [IQ_OFF, Q_OFF, K_OFF, U_OFF, V_OFF]
        IQ, Q, K, U, V = range(5)
        ring_of = [0, 1, 2, 0, 1]
        tiles = [("ik", 0)] + [(IQ, m) for m in range(NA)]
        front = [("tile", i) for i in range(5)] + [("iw",)] + [("score", 1, j) for j in range(HEADS)]
        for more, b in ((2, 2), (3, 3)):
            for _ in range(more):
                front.append(("tile", len(tiles)))
                tiles.append([(g, m) for g in (Q, K) for m in range(NA)][len(tiles) - 5])
            front += [("score", b, j) for j in range(HEADS)]
            if b == 2:
                front += [("flip", hh) for hh in range(HEADS)]
        for g, m in [(g, m) for g in (Q, K, U, V) for m in range(NA)][len(tiles) - 5:]:
            front.append(("tile", len(tiles)))
            tiles.append((g, m))
        tile_no = {t: i for i, t in enumerate(tiles)}
        score_no = {(b, j): (b - 1) * HEADS + j for b in range(1, NT) for j in range(HEADS)}
        units = [(b, hh) for b in range(NT) for hh in range(HEADS)]
        NU = len(units)

        def keys(b):
            return P * (b + 1)

        def half(hh):
            return slice(HD * (hh % 2), HD * (hh % 2) + HD)

        SMALLS = 2 + 7 + NA

        block = ctx.enter_context(nc.Block())

        @block.sync
        def _(sp):
            win = w_in[0].rearrange("(k p) n -> p k n", p=P)
            xv = x[0].rearrange("(t p) d -> t p d", p=P)
            for t in range(NT):
                sp.dma_start(h[:, t, :], xv[t]).then_inc(x_in[t], 16)
                if t == 0:
                    for r in range(2):
                        sp.dma_start(wik[:, :, HD * r:HD * r + HD], win[:, :, IK_OFF:IK_OFF + HD]).then_inc(small_in, 16)
            for g in range(5):
                if g >= 3:
                    sp.wait_ge(proj_ps, tile_no[(g - 3, NA - 1)] + 1)
                sp.dma_start(ring[ring_of[g]][:, :, :], win[:, :, group_cols[g]:group_cols[g] + AW]).then_inc(group_in[ring_of[g]], 16)
            wov = w_out[0].rearrange("(k p) n -> p k n", p=P)
            sp.wait_ge(proj_ps, tile_no[(K, NA - 1)] + 1)
            sp.dma_start(wo[0][:, :, :], wov[:, 0:KD // 2, :]).then_inc(wo_in, 16)
            sp.wait_ge(proj_ps, tile_no[(U, NA - 1)] + 1)
            sp.dma_start(wo[1][:, :, :], wov[:, KD // 2:KD, :]).then_inc(wo_in, 16)
            sp.wait_ge(proj_ps, tile_no[(V, NA - 1)] + 1)
            sp.dma_start(g1[:, :], ln1_g[0].partition_broadcast(P)).then_inc(ln1_in, 16)
            sp.dma_start(b1[:, :], ln1_b[0].partition_broadcast(P)).then_inc(ln1_in, 16)

            def load_expert(e, j, loaded=None):
                loaded = loaded or w_in_slot[j]
                for dst, src in ((wg[j][:, :, :], w_gate), (wu[j][:, :, :], w_up)):
                    sp.dma_start(dst, src[0, bass.ds(e, 1), :, :].rearrange("o (p k) f -> p (o k) f", p=P)).then_inc(loaded, 16)
                sp.dma_start(wd[j][:, :, :], w_down[0, bass.ds(e, 1), :, :].rearrange("o (m p) n -> p (o m) n", p=P)).then_inc(loaded, 16)

            load_expert(0, 0)
            sp.wait_ge(attn_sb, NT)
            for j in range(1, 4):
                load_expert(j, j)
            sp.wait_ge(h_ready, NT)
            for j in range(4, SLOTS):
                load_expert(j, j)
            with sp.Fori(0, NE // SLOTS - 1) as g:
                for j in range(SLOTS):
                    sp.wait_ge(y_ps, g * SLOTS + j + 1)
                    load_expert(g * SLOTS + SLOTS + j, j)
            for j in range(NE % SLOTS):
                e = NE // SLOTS * SLOTS + j
                sp.wait_ge(y_ps, e - SLOTS + 1)
                load_expert(e, j)
            sp.wait_ge(y_ps, NE)
            sp.wait_ge(count_ready, 1)
            with sp.If(sp.value_load(mosti[0:1, 0:1], min_val=0, max_val=SEQ) > CAP):
                sp.dma_start(o_rows[:, :, :], h_dram.rearrange("(t p) d -> p t d", p=P)).then_inc(o_rows_in, 16)
                with sp.Fori(0, NE) as e:
                    sp.wait_ge(o_y_ps, e * NT + 1)
                    load_expert(e, OSLOT, o_w_in)
            ov = out[0].rearrange("(t p) d -> t p d", p=P)
            for t in range(NT):
                sp.wait_ge(h_ready, NT + t + 1)
                sp.dma_start(ov[t], h[:, t, :]).then_inc(out_stored, 16)
            sp.wait_ge(out_stored, 16 * NT)

        @block.gpsimd
        def _(pool):
            n = [0]

            def link(ins):
                n[0] += 1
                ins.then_inc(pool_chain, 1)
                pool.wait_ge(pool_chain, n[0])

            link(pool.memset(ident[:, :], 0.0))
            link(pool.affine_select(out=ident[:, :], in_=ident[:, :], compare_op=ALU.not_equal, fill=1.0, base=0,
                                    pattern=[[-1, P]], channel_multiplier=1))
            link(pool.memset(flip[:, :], 0.0))
            link(pool.affine_select(out=flip[:, :], in_=flip[:, :], compare_op=ALU.not_equal, fill=1.0, base=-(P - 1),
                                    pattern=[[1, P]], channel_multiplier=1))
            pool.memset(ones[:, :], 1.0).then_inc(consts_ready, 1)
            link(pool.memset(tri[:, :], 1.0))
            link(pool.affine_select(out=tri[:, :], in_=tri[:, :], compare_op=ALU.is_gt, fill=0.0, base=0,
                                    pattern=[[1, P]], channel_multiplier=-1))
            link(pool.memset(uT[:, :, 0:PAD], 0.0))
            link(pool.memset(ptmp[0][:, 0:PAD], 0.0))
            link(pool.memset(ptmp[1][:, 0:PAD], 0.0))
            link(pool.memset(gl[:, :, :], -BIG))
            for t, pat, b0, cm in ((iota_e, [[1, NE]], 0, 0), (iota_r, [[1, CAP]], 1, 0)):
                link(pool.iota(t[:, :], pattern=pat, base=b0, channel_multiplier=cm, allow_small_or_imprecise_dtypes=True))
            link(pool.iota(gid[:, :, :], pattern=[[1, GROUPS], [0, PER_GROUP]], base=0, channel_multiplier=0,
                           allow_small_or_imprecise_dtypes=True))
            link(pool.iota(tokval_f[:, :, 0], pattern=[[P, NT]], base=0, channel_multiplier=0, allow_small_or_imprecise_dtypes=True))
            link(pool.iota(tokval_f[:, :, 1], pattern=[[0, NT]], base=0, channel_multiplier=1, allow_small_or_imprecise_dtypes=True))
            pool.tensor_copy(tokval[:, :, :], tokval_f[:, :, :]).then_inc(consts_ready, 1)

            for b in range(1, NT):
                pool.wait_ge(score_sum, b)
                d = score[:, P * b:P * b + P]
                pool.affine_select(out=d, in_=d, compare_op=ALU.is_ge, fill=NONCAUSAL, base=0, pattern=[[-1, P]],
                                   channel_multiplier=1).then_inc(score_masked, 1)
                if b == 2:
                    for hh in range(HEADS):
                        pool.wait_ge(flip_sb, hh + 1)
                        pool.affine_select(out=bias8[:, hh, :], in_=bias8[:, hh, :], compare_op=ALU.is_ge, fill=-BIG, base=SEQ - P,
                                           pattern=[[-1, SEQ]], channel_multiplier=1).then_inc(bias_ready, 1)
            pool.wait_ge(small_in, 16 * SMALLS)
            for g, w in enumerate(WINDOWS):
                pool.wait_ge(proj_sb, tile_no[(U, g)] + 1)
                src, step, i = uT[:, g, :], 1, 0
                while step < w:
                    dst = ptmp[i]
                    link(pool.tensor_tensor(dst[:, PAD:], src[:, PAD:], src[:, PAD - step:PAD + SEQ - step], ALU.add))
                    src, step, i = dst, 2 * step, 1 - i
                link(pool.tensor_scalar(src[:, PAD:], src[:, PAD:], 1.0 / w, 1.0, ALU.mult, ALU.mult))
                link(pool.tensor_tensor(src[:, PAD:PAD + PAD], src[:, PAD:PAD + PAD], hfix[:, g, :], ALU.mult))
                n[0] += 1
                pool.tensor_tensor(uT[:, g, PAD:], src[:, PAD:], uT[:, g, PAD:], ALU.subtract).then_inc(pool_chain, 1)
                pool.wait_ge(pool_chain, n[0])
                pool.sem_inc(pooled_ready, 1)

            def bias_mask(u):
                b, hh = units[u]
                if b == 0:
                    return
                k = u - HEADS
                if k == 0:
                    pool.wait_ge(keep_ready, 3)
                if k >= 2:
                    pool.wait_ge(logit_ready, u - 1)
                pool.tensor_tensor(bm[u % 2][:, 0:keys(b)], bias8[:, hh, SEQ - keys(b):], keep[b][:, :], ALU.add).then_inc(bm_ready, 1)

            pool.wait_ge(bias_ready, HEADS)
            for u in range(NU):
                b, hh = units[u]
                if u + 1 < NU:
                    bias_mask(u + 1)
                pool.wait_ge(rinv_ready, u + 1)
                p = lg[u % 3][:, 0:keys(b)]
                pool.tensor_scalar(p, p, rinv[:, u % 4:u % 4 + 1], 1.0, ALU.mult, ALU.mult).then_inc(prob_ready, 1)

            pool.wait_ge(ln1_in, 32)
            for t in range(NT):
                pool.wait_ge(norm_ready, t + 1)
                link(pool.tensor_tensor(h[:, t, :], h[:, t, :], g1[:, :], ALU.mult))
                pool.tensor_tensor(h[:, t, :], h[:, t, :], b1[:, :], ALU.add).then_inc(h_ready, 1)

            pool.wait_ge(list_ready, 1)
            pool.wait_ge(h_stored, 16 * NT)

            def gather(e, j, first):
                i = j % 2
                if not first:
                    pool.wait_ge(xeT_ps, e - 1)
                k = pool.tensor_copy(cur[i][0:CAP, :], lsti[0:CAP, bass.ds(e, 1)])
                k.then_inc(cur_ready, 1)
                pool.wait_ge(cur_ready, e + 1)
                pool.sem_inc(gather_begun, 1)
                pool.indirect_dma_start(out=xe[i][0:CAP, :], out_offset=None, in_=h_dram,
                                        in_offset=bass.IndirectOffsetOnAxis(ap=cur[i][0:CAP, :], axis=0),
                                        ).then_inc(gathered[i], 16)

            for e in range(SLOTS):
                gather(e, e, e < 2)
            with pool.Fori(1, NE // SLOTS) as g:
                for j in range(SLOTS):
                    gather(g * SLOTS + j, j, False)
            for e in range(NE // SLOTS * SLOTS, NE):
                gather(e, e % SLOTS, False)

            pool.wait_ge(slot_ready, 1)
            for i in range(2):
                pool.wait_ge(y_stored[i], 16 * NE // 2)
            pool.wait_ge(y_ps, NE)
            for t in range(NT):
                for c in range(2):
                    pool.indirect_dma_start(out=yg[t][c][:, :], out_offset=None, in_=y_dram,
                                            in_offset=bass.IndirectOffsetOnAxis(ap=sloti[:, t, c:c + 1], axis=0),
                                            ).then_inc(y_gathered[t], 16)
            pool.wait_ge(ln2_in, 32)
            for t in range(NT):
                pool.wait_ge(norm_ready, NT + t + 1)
                link(pool.tensor_tensor(h[:, t, :], h[:, t, :], g2[:, :], ALU.mult))
                pool.tensor_tensor(h[:, t, :], h[:, t, :], b2[:, :], ALU.add).then_inc(h_ready, 1)

        @block.scalar
        def _(act):
            act.dma_start(relb[0:BUCKETS, :], rel_bias).then_inc(onehot_in, 16)
            act.dma_start(hot_c[0:BUCKETS, :], onehot).then_inc(onehot_in, 16)
            act.dma_start(wiw[:, :, :], w_in[0, :, IW_OFF:IW_OFF + HEADS].rearrange("(k p) n -> p k n", p=P)).then_inc(small_in, 16)
            act.dma_start(wpool[:, :, :], w_pool[0].rearrange("g c d -> c g d")).then_inc(small_in, 16)
            with nc.allow_non_contiguous_dma(reason="512 elements in all"):
                act.dma_start(pscale[:, :], pool_scale[0].rearrange("(g p) -> p g", p=P)).then_inc(small_in, 16)
            for g in range(NA):
                act.dma_start(hfix[:, g, :], headfix[g].partition_broadcast(P)).then_inc(small_in, 16)
            act.dma_start(wr[:, :, 0:GROUPS], w_r1[0].rearrange("(k p) n -> p k n", p=P)).then_inc(small_in, 16)
            act.dma_start(wr[:, :, GROUPS:], w_r2[0].rearrange("(k p) n -> p k n", p=P)).then_inc(small_in, 16)
            act.dma_start(br[:, 0:GROUPS], b_r1[0].partition_broadcast(P)).then_inc(small_in, 16)
            act.dma_start(br[:, GROUPS:], b_r2[0].partition_broadcast(P)).then_inc(small_in, 16)

            for g in range(1, 2 * NT, 2):
                act.wait_ge(xT_ps, g + 1)
                act.activation(xT[:, 4:8, P * (g // 2):P * (g // 2) + P], bank[1][:, :].rearrange("p (k t) -> p k t", k=4),
                               ACT.Copy).then_inc(xT_act, 1)
            act.wait_ge(row_ready, 2)
            act.dma_start(row_dram.ap(), brow[0:HEADS, :]).then_inc(row_out, 16)
            act.wait_ge(row_out, 16)
            act.dma_start(bias_up[:, :, :], bass.AP(row_dram, 0, [[1, P], [TW, HEADS], [1, SEQ]])).then_inc(bias_in, 16)

            for item in front:
                if item[0] == "tile":
                    i = item[1]
                    kind, m = tiles[i]
                    dst = {"ik": ikT[:, :], IQ: iqT[:, m, :], Q: qT[:, m, :], K: kT[:, m, :],
                           U: uT[:, m, PAD:], V: v_sb[:, m, :]}[kind]
                    act.wait_ge(proj_ps, i + 1)
                    act.activation(dst, bank[2 + i % 2][:, :], ACT.Copy).then_inc(proj_sb, 1)
                elif item[0] == "flip":
                    hh = item[1]
                    act.wait_ge(flip_ps, hh + 1)
                    act.activation(bias8[:, hh, :], bank[4 + 3 * (hh % 2)][:, :], ACT.Copy).then_inc(flip_sb, 1)
                elif item[0] == "score":
                    _, b, j = item
                    s = score_no[(b, j)]
                    act.wait_ge(dots_ps, s + 1)
                    if s >= 4:
                        act.wait_ge(relu_used, s - 3)
                    act.activation(relu[s % 4][:, 0:keys(b)], bank[5 + s % 2][:, 0:keys(b)], ACT.Relu, scale=SCALE).then_inc(relu_ready, 1)
            for g in range(NA):
                act.wait_ge(mixed_ps, g + 1)
                act.activation(mixT[:, NA + g, :], bank[2 + g % 2][:, :], ACT.Copy, scale=pscale[:, g:g + 1]).then_inc(mixed_sb, 1)

            for u in range(NU + 3):
                if u < NU:
                    b, hh = units[u]
                    act.wait_ge(logit_ready, u + 1)
                    p = lg[u % 3][:, 0:keys(b)]
                    if u >= 4:
                        act.wait_ge(rinv_ready, u - 3)
                    act.activation(p, p, ACT.Exp, bias=nmx[:, u % 4:u % 4 + 1], scale=-1.0,
                                   accum_out=rsum[:, u % 4:u % 4 + 1]).then_inc(exp_ready, 1)
                if 0 <= u - 2 < NU:
                    w = u - 2
                    b, hh = units[w]
                    act.wait_ge(pT_ps, w + 1)
                    if w >= 2:
                        act.wait_ge(pv_ps, w - 1)
                    act.activation(pT[w % 2][:, 0:keys(b)], bank[4 + w % 2][:, 0:keys(b)], ACT.Copy).then_inc(pT_ready, 1)
                if u >= 3 and units[u - 3][1] == HEADS - 1:
                    b = units[u - 3][0]
                    act.wait_ge(pv_ps, u - 2)
                    act.activation(mixT[:, 0:NA, P * b:P * b + P], bank[6 + b % 2][:, :].rearrange("p (m t) -> p m t", m=NA),
                                   ACT.Copy).then_inc(attn_sb, 1)

            for t in range(NT):
                act.wait_ge(var_ready, t + 1)
                act.activation(std[:, :], var_e[:, :], ACT.Sqrt).then_inc(std_ready, 1)
                act.wait_ge(h_ready, t + 1)
                act.dma_start(h_dram[P * t:P * t + P, :], h[:, t, :]).then_inc(h_stored, 16)
                act.wait_ge(hT_ps, t + 1)
                if t >= 2:
                    act.wait_ge(router_ps, t - 1)
                for k in range(2):
                    act.activation(hT[t % 2][:, 4 * k:4 * k + 4, :], bank[4 + k][:, :].rearrange("p (k t) -> p k t", k=4),
                                   ACT.Copy).then_inc(hT_ready, 1)
            act.wait_ge(h_ready, NT)
            act.dma_start(g2[:, :], ln2_g[0].partition_broadcast(P)).then_inc(ln2_in, 16)
            act.dma_start(b2[:, :], ln2_b[0].partition_broadcast(P)).then_inc(ln2_in, 16)
            for t in range(NT):
                act.wait_ge(top_ready, t + 1)
                act.activation(ex[:, t, :], gl[:, t, 0:GROUPS], ACT.Exp, bias=neg[:, t, 0:1], accum_out=zs[:, t, 0:1])
                act.activation(zs[:, t, 1:2], em8[:, t, 1:2], ACT.Exp, bias=neg[:, t, 1:2]).then_inc(gate_exp, 1)

            def rows_out(e, j, first):
                i = j % 2
                act.wait_ge(xeT_ps, e + 1)
                if not first:
                    act.wait_ge(gu_ps, e - 1)
                act.activation(xeT[i][:, :, :], bank[i][:, :].rearrange("p (k t) -> p k t", k=KD), ACT.Copy).then_inc(xeT_ready, 1)

            def silu(e, j, first):
                i = j % 2
                act.wait_ge(gu_ps, e + 1)
                if not first:
                    act.wait_ge(act_ready, e - 1)
                act.activation(sil[i][:, :, :], bank[2 + i][:, 0:ME * CAP].rearrange("p (m t) -> p m t", m=ME), ACT.Silu).then_inc(silu_ready, 1)

            def y_out(e, j, first, occurrence):
                i = j % 2
                act.wait_ge(y_ps, e + 1)
                if not first:
                    act.wait_ge(y_stored[i], occurrence * 16)
                act.activation(ye[i][0:CAP, 512:], bank[5 + 2 * i][0:CAP, :], ACT.Copy).then_inc(y_hi, 1)
                act.wait_ge(y_hi, e + 1)
                act.wait_ge(y_lo, e + 1)
                act.dma_start(y_dram[bass.ds(e * CAP, CAP), :], ye[i][0:CAP, :]).then_inc(y_stored[i], 16)

            rows_out(0, 0, True)
            rows_out(1, 1, True)
            silu(0, 0, True)
            for e in range(SLOTS):
                rows_out(e + 2, e, False)
                silu(e + 1, e + 1, e < 1)
                y_out(e, e, e < 2, e // 2)
            with act.Fori(1, NE // SLOTS) as g:
                for j in range(SLOTS):
                    rows_out(g * SLOTS + j + 2, j, False)
                    silu(g * SLOTS + j + 1, j + 1, False)
                    y_out(g * SLOTS + j, j, False, g * (SLOTS // 2) + j // 2)
            for e in range(NE // SLOTS * SLOTS, NE):
                if e + 1 < NE:
                    silu(e + 1, e + 1, False)
                y_out(e, e, False, e // 2)

            act.wait_ge(count_ready, 1)
            with act.If(act.value_load(mosti[0:1, 0:1], min_val=0, max_val=SEQ) > CAP):
                for t in range(NT):
                    for k in range(2):
                        act.wait_ge(o_rowsT_ps, 2 * t + k + 1)
                        act.activation(o_rowsT[:, 4 * k:4 * k + 4, P * t:P * t + P], bank[k][:, :].rearrange("p (k t) -> p k t", k=4),
                                       ACT.Copy).then_inc(o_rowsT_ready, 1)
                with act.Fori(0, NE) as e:
                    act.wait_ge(o_gu_ps, e + 1)
                    act.wait_ge(o_act_ready, e + 1)
                    for m in range(ME):
                        act.activation(o_sil[:, m, :], bank[m][:, :], ACT.Silu).then_inc(o_silu_ready, 1)

            for t in range(NT):
                act.wait_ge(var_ready, NT + t + 1)
                act.activation(std[:, :], var_e[:, :], ACT.Sqrt).then_inc(std_ready, 1)

        @block.vector
        def _(dve):
            n = [0]

            def link(ins):
                n[0] += 1
                ins.then_inc(dve_chain, 1)
                dve.wait_ge(dve_chain, n[0])

            for g in range(0, 2 * NT, 2):
                dve.wait_ge(xT_ps, g + 1)
                dve.tensor_copy(xT[:, 0:4, P * (g // 2):P * (g // 2) + P], bank[0][:, :].rearrange("p (k t) -> p k t", k=4)).then_inc(xT_dve, 1)
            dve.wait_ge(row_ps, 1)
            for i, bk in enumerate((4, 7)):
                dve.tensor_scalar(brow[0:HEADS, TW // 2 * i:TW // 2 * (i + 1)], bank[bk][0:HEADS, 0:TW // 2], 1.0 / SCALE, None,
                                  ALU.mult).then_inc(row_ready, 1)
            dve.wait_ge(iw_ps, 1)
            link(dve.tensor_scalar(iw[:, :, :], bank[0][:, 0:NT * HEADS].rearrange("p (t j) -> p t j", t=NT), HEADS ** -0.5, None, ALU.mult))
            for b in range(1, NT):
                s_b = score[:, 0:keys(b)]
                for j in range(HEADS):
                    s = score_no[(b, j)]
                    dve.wait_ge(relu_ready, s + 1)
                    r = relu[s % 4][:, 0:keys(b)]
                    if j == 0:
                        ins = dve.tensor_scalar(s_b, r, iw[:, b, 0:1], None, ALU.mult)
                    else:
                        ins = dve.scalar_tensor_tensor(out=s_b, in0=r, scalar=iw[:, b, j:j + 1], in1=s_b, op0=ALU.mult, op1=ALU.add)
                    ins.then_inc(relu_used, 1)
                    dve.wait_ge(relu_used, s + 1)
                dve.sem_inc(score_sum, 1)
                dve.wait_ge(score_masked, b)
                for _ in range(TOPK // 8):
                    link(dve.max(m8[:, :], s_b))
                    link(dve.match_replace(out=s_b, in_to_replace=m8[:, :], in_values=s_b, imm_value=TAKEN))
                n[0] += 1
                dve.tensor_scalar(keep[b][:, :], s_b, TAKEN / 2, -BIG, ALU.is_gt, ALU.mult).then_inc(dve_chain, 1)
                dve.wait_ge(dve_chain, n[0])
                dve.sem_inc(keep_ready, 1)

            dve.wait_ge(bias_ready, HEADS)
            for u in range(NU + 1):
                if u < NU:
                    b, hh = units[u]
                    dve.wait_ge(qk_ps, u + 1)
                    add = bias8[:, hh, SEQ - keys(b):]
                    if b:
                        dve.wait_ge(bm_ready, u - HEADS + 1)
                        add = bm[u % 2][:, 0:keys(b)]
                    if u >= 3:
                        dve.wait_ge(pT_ps, u - 2)
                    dve.tensor_tensor_reduce(out=lg[u % 3][:, 0:keys(b)], in0=bank[u % 2][:, 0:keys(b)], in1=add, scale=-SCALE,
                                             scalar=3e38, op0=ALU.add, op1=ALU.min, accum_out=nmx[:, u % 4:u % 4 + 1]).then_inc(logit_ready, 1)
                if u >= 1:
                    dve.wait_ge(exp_ready, u)
                    if u >= 5:
                        dve.wait_ge(prob_ready, u - 4)
                    dve.reciprocal(rinv[:, (u - 1) % 4:(u - 1) % 4 + 1], rsum[:, (u - 1) % 4:(u - 1) % 4 + 1]).then_inc(rinv_ready, 1)

            def normalise(t, k):
                for i in range(2):
                    link(dve.bn_stats(stats[:, i, :], h[:, t, 512 * i:512 * i + 512]))
                link(dve.bn_aggr(mv[:, :], stats[:, :, :]))
                dve.tensor_scalar(var_e[:, :], mv[:, 1:2], EPS, None, ALU.add).then_inc(var_ready, 1)
                dve.wait_ge(std_ready, k + 1)
                link(dve.reciprocal(rstd[:, :], std[:, :]))
                dve.tensor_scalar(h[:, t, :], h[:, t, :], mv[:, 0:1], rstd[:, 0:1], ALU.subtract, ALU.mult).then_inc(norm_ready, 1)

            def route(t):
                dve.wait_ge(router_ps, t + 1)
                ps = bank[6 + t % 2][:, 0:GROUPS + NE]
                link(dve.tensor_tensor(gl[:, t, 0:GROUPS], ps[:, 0:GROUPS], br[:, 0:GROUPS], ALU.add))
                dve.tensor_tensor(lf[:, :], ps[:, GROUPS:], br[:, GROUPS:], ALU.add).then_inc(router_sb, 1)
                dve.wait_ge(router_sb, t + 1)
                link(dve.max(gm8[:, :], gl[:, t, :]))
                link(dve.max_index(gi8[:, :], gm8[:, :], gl[:, t, :]))
                link(dve.tensor_copy(gidx[:, :], gi8[:, 0:1]))
                link(dve.tensor_scalar(pen[:, :], gid[:, :, :].rearrange("p g e -> p (g e)"), gidx[:, 0:1], -BIG, ALU.not_equal, ALU.mult))
                link(dve.tensor_tensor(lf[:, :], lf[:, :], pen[:, :], ALU.add))
                link(dve.max(em8[:, t, :], lf[:, :]))
                link(dve.max_index(ei8[:, :], em8[:, t, :], lf[:, :]))
                link(dve.tensor_copy(eidx[:, t, :], ei8[:, 0:2]))
                link(dve.tensor_scalar(neg[:, t, 0:1], gm8[:, 0:1], -1.0, None, ALU.mult))
                link(dve.tensor_scalar(neg[:, t, 1:2], em8[:, t, 0:1], -1.0, None, ALU.mult))
                dve.sem_inc(top_ready, 1)
                for c in range(2):
                    link(dve.tensor_scalar(hot[:, t, c, :], iota_e[:, :], eidx[:, t, c:c + 1], None, ALU.is_equal))
                dve.tensor_tensor(hsum[:, t, :], hot[:, t, 0, :], hot[:, t, 1, :], ALU.add).then_inc(hot_ready, 1)

            dve.wait_ge(small_in, 16 * SMALLS)
            dve.wait_ge(consts_ready, 2)
            for t in range(NT):
                dve.wait_ge(out_ps, t + 1)
                for i in range(2):
                    hv = h[:, t, 512 * i:512 * i + 512]
                    link(dve.scalar_tensor_tensor(out=hv, in0=hv, scalar=ALPHA, in1=bank[(2 if t % 2 == 0 else 0) + i][:, :],
                                                  op0=ALU.mult, op1=ALU.add))
                dve.sem_inc(res_ready, 1)
                normalise(t, t)
                if t >= 1:
                    route(t - 1)
            route(NT - 1)
            dve.wait_ge(rank_ps, 1)
            dve.wait_ge(hot_ready, NT)
            for t in range(NT):
                link(dve.scalar_tensor_tensor(out=rank1[:, t, :], in0=bank[7][:, NE * t:NE * t + NE], scalar=1.0, in1=hsum[:, t, :],
                                              op0=ALU.add, op1=ALU.mult))
            for t in range(NT):
                dve.tensor_tensor(sel[:, t, :, :], rank1[:, t, :].unsqueeze(2).to_broadcast([P, NE, CAP]),
                                  iota_r[:, :].unsqueeze(1).to_broadcast([P, NE, CAP]), ALU.is_equal).then_inc(sel_ready, 1)
            link(dve.max(m8[:, :], bank[7][:, NE * NT:NE * NT + NE]))
            dve.tensor_copy(mosti[:, :], m8[:, 0:1]).then_inc(count_ready, 1)
            for t in range(NT):
                for c in range(2):
                    link(dve.tensor_tensor_reduce(out=scr[:, :], in0=hot[:, t, c, :], in1=rank1[:, t, :], scale=1.0, scalar=0.0,
                                                  op0=ALU.mult, op1=ALU.add, accum_out=rk[:, t, c:c + 1]))
            link(dve.tensor_scalar(fits[:, :, :], rk[:, :, :], float(CAP), None, ALU.is_le))
            link(dve.tensor_scalar(rk[:, :, :], rk[:, :, :], float(CAP), -1.0, ALU.min, ALU.add))
            link(dve.scalar_tensor_tensor(out=slotf[:, :, :], in0=eidx[:, :, :], scalar=float(CAP), in1=rk[:, :, :], op0=ALU.mult, op1=ALU.add))
            dve.tensor_copy(sloti[:, :, :], slotf[:, :, :]).then_inc(slot_ready, 1)
            dve.wait_ge(list_ps, 1)
            link(dve.tensor_copy(lst[0:CAP, :, :], bank[2][0:CAP, 0:2 * NE].rearrange("p (e c) -> p e c", c=2)))
            dve.tensor_tensor(lsti[0:CAP, :], lst[0:CAP, :, 0], lst[0:CAP, :, 1], ALU.add).then_inc(list_ready, 1)
            dve.wait_ge(gate_exp, NT)
            link(dve.tensor_scalar(wt[:, :, 0], zs[:, :, 1], 1.0, None, ALU.add))
            link(dve.tensor_tensor(wt[:, :, 0], wt[:, :, 0], zs[:, :, 0], ALU.mult))
            link(dve.reciprocal(wt[:, :, 0], wt[:, :, 0]))
            link(dve.tensor_tensor(wt[:, :, 1], wt[:, :, 0], zs[:, :, 1], ALU.mult))
            link(dve.tensor_tensor(wfit[:, :, :], wt[:, :, :], fits[:, :, :], ALU.mult))
            dve.wait_ge(h_stored, 16 * NT)
            for t in range(NT):
                link(dve.tensor_scalar(h[:, t, :], h[:, t, :], ALPHA, None, ALU.mult))

            def gated(e, j, first):
                i = j % 2
                dve.wait_ge(silu_ready, e + 1)
                if not first:
                    dve.wait_ge(y_ps, e - 1)
                dve.tensor_tensor(act_e[i][:, :, :], bank[2 + i][:, ME * CAP:2 * ME * CAP].rearrange("p (m t) -> p m t", m=ME),
                                  sil[i][:, :, :], ALU.mult).then_inc(act_ready, 1)

            def y_out(e, j, first, occurrence):
                i = j % 2
                dve.wait_ge(y_ps, e + 1)
                if not first:
                    dve.wait_ge(y_stored[i], occurrence * 16)
                dve.tensor_copy(ye[i][0:CAP, 0:512], bank[4 + 2 * i][0:CAP, :]).then_inc(y_lo, 1)

            gated(0, 0, True)
            for e in range(SLOTS):
                gated(e + 1, e + 1, e < 1)
                y_out(e, e, e < 2, e // 2)
            with dve.Fori(1, NE // SLOTS) as g:
                for j in range(SLOTS):
                    gated(g * SLOTS + j + 1, j + 1, False)
                    y_out(g * SLOTS + j, j, False, g * (SLOTS // 2) + j // 2)
            for e in range(NE // SLOTS * SLOTS, NE):
                if e + 1 < NE:
                    gated(e + 1, e + 1, False)
                y_out(e, e % SLOTS, False, e // 2)

            with dve.If(dve.value_load(mosti[0:1, 0:1], min_val=0, max_val=SEQ) > CAP):
                for t in range(NT):
                    dve.tensor_scalar(scr[:, :], hot[:, t, 0, :], wt[:, t, 0:1], None, ALU.mult).then_inc(o_chain, 1)
                    dve.wait_ge(o_chain, 3 * t + 1)
                    dve.scalar_tensor_tensor(out=scr[:, :], in0=hot[:, t, 1, :], scalar=wt[:, t, 1:2], in1=scr[:, :],
                                             op0=ALU.mult, op1=ALU.add).then_inc(o_chain, 1)
                    dve.wait_ge(o_chain, 3 * t + 2)
                    dve.scalar_tensor_tensor(out=over[:, t, :], in0=rank1[:, t, :], scalar=float(CAP), in1=scr[:, :],
                                             op0=ALU.is_gt, op1=ALU.mult).then_inc(o_chain, 1)
                    dve.wait_ge(o_chain, 3 * t + 3)
                dve.sem_inc(o_added, 1)
                dve.sem_inc(o_act_ready, 1)
                with dve.Fori(0, NE) as e:
                    dve.wait_ge(o_added, e * NT + 1)
                    dve.tensor_copy(over_e[:, :], over[:, :, bass.ds(e, 1)].rearrange("p t o -> p (t o)")).then_inc(o_weight_ready, 1)
                    dve.wait_ge(o_silu_ready, e * ME + ME)
                    dve.wait_ge(o_y_ps, e * NT + 1)
                    for m in range(ME):
                        ins = dve.tensor_tensor(o_act[:, m, :], bank[2 + m][:, :], o_sil[:, m, :], ALU.mult)
                    ins.then_inc(o_act_ready, 1)
                    dve.wait_ge(o_weight_ready, e + 1)
                    for t in range(NT):
                        dve.wait_ge(o_y_ps, e * NT + t + 2)
                        for c in range(2):
                            hv = h[:, t, 512 * c:512 * c + 512]
                            ins = dve.scalar_tensor_tensor(out=hv, in0=bank[4 + 2 * (t % 2) + c][:, :], scalar=over_e[:, t:t + 1], in1=hv,
                                                           op0=ALU.mult, op1=ALU.add)
                        ins.then_inc(o_added, 1)
            for t in range(NT):
                dve.wait_ge(y_gathered[t], 32)
                for c in range(2):
                    link(dve.scalar_tensor_tensor(out=h[:, t, :], in0=yg[t][c][:, :], scalar=wfit[:, t, c:c + 1], in1=h[:, t, :],
                                                  op0=ALU.mult, op1=ALU.add))
                normalise(t, NT + t)

        @block.tensor
        def _(pe):
            pe.wait_ge(consts_ready, 1)
            for g in range(2 * NT):
                t, k0 = g // 2, 4 * (g % 2)
                if g % 2 == 0:
                    pe.wait_ge(x_in[t], 16)
                if g >= 2:
                    pe.wait_ge(xT_act if g % 2 else xT_dve, g // 2)
                for k in range(4):
                    ins = pe.transpose(bank[g % 2][:, P * k:P * k + P], h[:, t, P * (k0 + k):P * (k0 + k) + P], ident[:, :])
                ins.then_inc(xT_ps, 1)
            pe.wait_ge(onehot_in, 32)
            for i, bk in enumerate((4, 7)):
                ins = pe.matmul(bank[bk][0:HEADS, 0:TW // 2], relb[0:BUCKETS, :], hot_c[0:BUCKETS, TW // 2 * i:TW // 2 * (i + 1)], start=True, stop=True)
            ins.then_inc(row_ps, 1)
            pe.wait_ge(small_in, 16 * SMALLS)
            pe.wait_ge(xT_act, NT)
            pe.wait_ge(xT_dve, NT)
            seen = set()
            for item in front:
                if item[0] == "tile":
                    i = item[1]
                    kind, m = tiles[i]
                    if kind != "ik" and kind not in seen:
                        seen.add(kind)
                        pe.wait_ge(group_in[ring_of[kind]], 16 * (kind // 3 + 1))
                    if i >= 2:
                        pe.wait_ge(proj_sb, i - 1)
                    for k in range(KD):
                        if kind == "ik":
                            lhsT, rhs = wik[:, k, :], xT[:, k, :]
                        elif kind == V:
                            lhsT, rhs = xT[:, k, P * m:P * m + P], ring[ring_of[kind]][:, k, :]
                        else:
                            lhsT, rhs = ring[ring_of[kind]][:, k, P * m:P * m + P], xT[:, k, :]
                        ins = pe.matmul(bank[2 + i % 2][:, :], lhsT, rhs, start=k == 0, stop=k == KD - 1)
                    ins.then_inc(proj_ps, 1)
                elif item[0] == "iw":
                    for t in range(NT):
                        for k in range(KD):
                            ins = pe.matmul(bank[0][:, HEADS * t:HEADS * t + HEADS], xT[:, k, P * t:P * t + P], wiw[:, k, :],
                                            start=k == 0, stop=k == KD - 1)
                    ins.then_inc(iw_ps, 1)
                elif item[0] == "flip":
                    hh = item[1]
                    pe.wait_ge(bias_in, 16)
                    if hh >= 2:
                        pe.wait_ge(flip_sb, hh - 1)
                    pe.matmul(bank[4 + 3 * (hh % 2)][:, :], flip[:, :], bias_up[:, hh, :], start=True, stop=True).then_inc(flip_ps, 1)
                else:
                    _, b, j = item
                    s = score_no[(b, j)]
                    if s == 0:
                        pe.wait_ge(proj_sb, 5)
                    if s >= 2:
                        pe.wait_ge(relu_ready, s - 1)
                    pe.matmul(bank[5 + s % 2][:, 0:keys(b)], iqT[half(j), j // 2, P * b:P * b + P], ikT[half(j), 0:keys(b)],
                              start=True, stop=True).then_inc(dots_ps, 1)
            for g in range(NA):
                if g == 0:
                    pe.wait_ge(proj_sb, len(tiles))
                if g >= 2:
                    pe.wait_ge(mixed_sb, g - 1)
                pe.wait_ge(pooled_ready, g + 1)
                pe.matmul(bank[2 + g % 2][:, :], wpool[:, g, :], uT[:, g, PAD:], start=True, stop=True).then_inc(mixed_ps, 1)
            pe.wait_ge(relu_ready, len(score_no))
            for u in range(NU + 3):
                if u < NU:
                    b, hh = units[u]
                    if u >= 2:
                        pe.wait_ge(logit_ready, u - 1)
                    pe.matmul(bank[u % 2][:, 0:keys(b)], qT[half(hh), hh // 2, P * b:P * b + P], kT[half(hh), hh // 2, 0:keys(b)],
                              start=True, stop=True).then_inc(qk_ps, 1)
                if 0 <= u - 2 < NU:
                    w = u - 2
                    b, hh = units[w]
                    pe.wait_ge(prob_ready, w + 1)
                    if w >= 2:
                        pe.wait_ge(pT_ready, w - 1)
                    for k in range(b + 1):
                        ins = pe.transpose(bank[4 + w % 2][:, P * k:P * k + P], lg[w % 3][:, P * k:P * k + P], ident[:, :])
                    ins.then_inc(pT_ps, 1)
                if u >= 3:
                    w = u - 3
                    b, hh = units[w]
                    pe.wait_ge(pT_ready, w + 1)
                    if hh == 0 and b >= 2:
                        pe.wait_ge(attn_sb, b - 1)
                    for k in range(b + 1):
                        ins = pe.matmul(bank[6 + b % 2][half(hh), P * (hh // 2):P * (hh // 2) + P], v_sb[:, k, HD * hh:HD * hh + HD],
                                        pT[w % 2][:, P * k:P * k + P], start=k == 0, stop=k == b)
                    ins.then_inc(pv_ps, 1)
            pe.wait_ge(mixed_sb, NA)
            pe.wait_ge(attn_sb, NT)
            pe.wait_ge(wo_in, 32)

            def router(t):
                pe.wait_ge(h_ready, t + 1)
                if t >= 1:
                    pe.wait_ge(hT_ready, 2 * t)
                for k in range(KD):
                    ins = pe.transpose(bank[4 + k // 4][:, P * (k % 4):P * (k % 4) + P], h[:, t, P * k:P * k + P], ident[:, :])
                ins.then_inc(hT_ps, 1)
                pe.wait_ge(hT_ready, 2 * t + 2)
                if t >= 2:
                    pe.wait_ge(router_sb, t - 1)
                for k in range(KD):
                    ins = pe.matmul(bank[6 + t % 2][:, 0:GROUPS + NE], hT[t % 2][:, k, :], wr[:, k, :], start=k == 0, stop=k == KD - 1)
                ins.then_inc(router_ps, 1)

            for t in range(NT):
                if t >= 2:
                    pe.wait_ge(res_ready, t - 1)
                for i in range(2):
                    for k in range(KD):
                        ins = pe.matmul(bank[(2 if t % 2 == 0 else 0) + i][:, :], mixT[:, k, P * t:P * t + P],
                                        wo[k // 4][:, k % 4, 512 * i:512 * i + 512], start=k == 0, stop=k == KD - 1)
                ins.then_inc(out_ps, 1)
                if t >= 2:
                    router(t - 2)
            router(NT - 2)
            router(NT - 1)
            pe.wait_ge(hot_ready, NT)
            for t in range(NT):
                for s in range(t + 1):
                    ins = pe.matmul(bank[7][:, NE * t:NE * t + NE], (tri if s == t else ones)[:, :], hsum[:, s, :], start=s == 0, stop=s == t)
            for s in range(NT):
                ins = pe.matmul(bank[7][:, NE * NT:NE * NT + NE], ones[:, :], hsum[:, s, :], start=s == 0, stop=s == NT - 1)
            ins.then_inc(rank_ps, 1)
            pe.wait_ge(sel_ready, NT)
            for e in range(NE):
                for t in range(NT):
                    ins = pe.matmul(bank[2][0:CAP, 2 * e:2 * e + 2], sel[:, t, e, :], tokval[:, t, :], start=t == 0, stop=t == NT - 1)
            ins.then_inc(list_ps, 1)

            def rows(e, j, first, occurrence):
                i = j % 2
                pe.wait_ge(gathered[i], occurrence * 16 + 16)
                if not first:
                    pe.wait_ge(xeT_ready, e - 1)
                pe.sem_inc(rows_begun, 1)
                xv = xe[i][0:CAP, :].rearrange("t (p k) -> t k p", k=KD)
                for k in range(KD):
                    ins = pe.transpose(bank[i][:, CAP * k:CAP * k + CAP], xv[:, k, :], ident[0:CAP, 0:CAP])
                ins.then_inc(xeT_ps, 1)

            def gate_up(e, j, first, turn):
                i = j % 2
                pe.wait_ge(xeT_ready, e + 1)
                pe.wait_ge(w_in_slot[j], turn * 48 + 48)
                if not first:
                    pe.wait_ge(act_ready, e - 1)
                for s, w in enumerate((wg, wu)):
                    for m in range(ME):
                        c = (s * ME + m) * CAP
                        for k in range(KD):
                            ins = pe.matmul(bank[2 + i][:, c:c + CAP], w[j][:, k, P * m:P * m + P], xeT[i][:, k, :], start=k == 0, stop=k == KD - 1)
                ins.then_inc(gu_ps, 1)

            def down(e, j, first):
                i = j % 2
                pe.wait_ge(act_ready, e + 1)
                if not first:
                    pe.wait_ge(y_lo, e - 1)
                    pe.wait_ge(y_hi, e - 1)
                for c in range(2):
                    for m in range(ME):
                        ins = pe.matmul(bank[4 + 2 * i + c][0:CAP, :], act_e[i][:, m, :], wd[j][:, m, 512 * c:512 * c + 512], start=m == 0, stop=m == ME - 1)
                ins.then_inc(y_ps, 1)

            rows(0, 0, True, 0)
            rows(1, 1, True, 0)
            gate_up(0, 0, True, 0)
            for e in range(SLOTS):
                rows(e + 2, e + 2, False, (e + 2) // 2)
                gate_up(e + 1, (e + 1) % SLOTS, e < 1, (e + 1) // SLOTS)
                down(e, e, e < 2)
            with pe.Fori(1, NE // SLOTS) as g:
                for j in range(SLOTS):
                    rows(g * SLOTS + j + 2, j, False, g * (SLOTS // 2) + j // 2 + 1)
                    gate_up(g * SLOTS + j + 1, (j + 1) % SLOTS, False, g + (j + 1) // SLOTS)
                    down(g * SLOTS + j, j, False)
            for e in range(NE // SLOTS * SLOTS, NE):
                if e + 1 < NE:
                    gate_up(e + 1, (e + 1) % SLOTS, False, (e + 1) // SLOTS)
                down(e, e % SLOTS, False)

            pe.wait_ge(count_ready, 1)
            with pe.If(pe.value_load(mosti[0:1, 0:1], min_val=0, max_val=SEQ) > CAP):
                pe.wait_ge(o_rows_in, 16)
                pe.wait_ge(y_lo, NE)
                pe.wait_ge(y_hi, NE)
                for t in range(NT):
                    for k in range(2):
                        if t:
                            pe.wait_ge(o_rowsT_ready, 2 * t + k - 1)
                        for q in range(4):
                            ins = pe.transpose(bank[k][:, P * q:P * q + P], o_rows[:, t, :].rearrange("p (c k) -> p k c", k=KD)[:, 4 * k + q, :], ident[:, :])
                        ins.then_inc(o_rowsT_ps, 1)
                pe.wait_ge(o_rowsT_ready, 2 * NT)
                pe.sem_inc(o_y_ps, 1)
                with pe.Fori(0, NE) as e:
                    pe.wait_ge(o_w_in, e * 48 + 48)
                    pe.wait_ge(o_act_ready, e + 1)
                    pe.wait_ge(o_added, e * NT + 1)
                    for s, w in enumerate((wg, wu)):
                        for m in range(ME):
                            for k in range(KD):
                                ins = pe.matmul(bank[2 * s + m][:, :], w[OSLOT][:, k, P * m:P * m + P], o_rowsT[:, k, :], start=k == 0, stop=k == KD - 1)
                    ins.then_inc(o_gu_ps, 1)
                    pe.wait_ge(o_act_ready, e + 2)
                    for t in range(NT):
                        if t >= 2:
                            pe.wait_ge(o_added, e * NT + t)
                        for c in range(2):
                            for m in range(ME):
                                ins = pe.matmul(bank[4 + 2 * (t % 2) + c][:, :], o_act[:, m, P * t:P * t + P], wd[OSLOT][:, m, 512 * c:512 * c + 512],
                                                start=m == 0, stop=m == ME - 1)
                        ins.then_inc(o_y_ps, 1)


_INS = ['x', 'w_in', 'w_pool', 'pool_scale', 'w_out', 'rel_bias', 'ln1_g', 'ln1_b', 'w_r1', 'b_r1', 'w_r2', 'b_r2',
        'w_gate', 'w_up', 'w_down', 'ln2_g', 'ln2_b']


def kernel(**inputs):
    import numpy as _np
    import concourse.bacc as _bacc
    from concourse import mybir as _mybir
    from concourse.bass_utils import run_bass_kernel_spmd as _run

    nc = _bacc.Bacc("TRN2", target_bir_lowering=False, num_devices=1)
    arrays, args = {}, []
    given = {name: inputs[name] for name in _INS}
    given["onehot"] = bucket_onehot()
    given["headfix"] = head_counts()
    for name, a in given.items():
        a = _np.ascontiguousarray(a)
        arrays[f"in_{name}_dram"] = a
        args.append(nc.dram_tensor(f"in_{name}_dram", a.shape, _mybir.dt.from_np(a.dtype), kind="ExternalInput").ap())
    args.append(nc.dram_tensor("out_0_dram", (1, SEQ, D), _mybir.dt.float32, kind="ExternalOutput").ap())
    layer_kernel(nc, *args)
    r = _run(nc, [arrays], core_ids=[0])
    return r.results[0]["out_0_dram"]
```

```python
import math
from contextlib import ExitStack

import numpy as np

import concourse.bass as bass
from concourse import mybir

F32 = mybir.dt.float32
F32R = mybir.dt.float32r
BF16 = mybir.dt.bfloat16
U32 = mybir.dt.uint32
I32 = mybir.dt.int32
ALU = mybir.AluOpType
ACT = mybir.ActivationFunctionType
AX = mybir.AxisListType

P = 128
SEQ = 512
D = 1024
NT = SEQ // P
KD = D // P
HEADS = 8
HD = 64
AW = HEADS * HD
NA = AW // P
TOPK = min(256, SEQ // 4)
WINDOWS = (2, 4, 8, 16)
PAD = WINDOWS[-1]
BUCKETS = 32
MAX_DIST = 128
Q_OFF, K_OFF, V_OFF, IQ_OFF = 0, AW, 2 * AW, 3 * AW
IK_OFF = IQ_OFF + AW
IW_OFF = IK_OFF + HD
U_OFF = IW_OFF + HEADS
GROUPS = 4
PER_GROUP = 8
NE = GROUPS * PER_GROUP
DE = 256
ME = DE // P
CAP = 64
SLOTS = 6
CHUNKS = 4
KC = 2 * KD // CHUNKS
EPS = 1e-5
ALPHA = 2.0 ** 0.25
BIG = 1e30
NONCAUSAL = -1e38
TAKEN = -3e38
TW = SEQ + P
SCALE = HD ** -0.5


def bucket_onehot():
    n = np.maximum(SEQ - 1 - np.arange(TW), 0)
    half = BUCKETS // 2
    nf = np.maximum(n, 1).astype(np.float32)
    large = half + (np.log(nf / np.float32(half)) / np.float32(math.log(MAX_DIST / half)) * np.float32(BUCKETS - half)).astype(np.int32)
    b = np.where(n < half, n, np.minimum(large, BUCKETS - 1))
    return (b[None, :] == np.arange(BUCKETS)[:, None]).astype(np.float32)


def head_counts():
    t = np.arange(PAD) + 1
    return np.stack([w / np.minimum(t, w) for w in WINDOWS]).astype(np.float32)


def layer_kernel(nc, x, w_in, w_pool, pool_scale, w_out, rel_bias, ln1_g, ln1_b, w_r1, b_r1, w_r2, b_r2,
                 w_gate, w_up, w_down, ln2_g, ln2_b, onehot, headfix, out):
    ctx = ExitStack()
    with ctx:
        base = [(nc.sbuf_base + 63) // 64 * 64]
        KB = 1024

        def at(name, offset, shape, dt=F32):
            return nc.alloc_sbuf_tensor_at(name, [P, *shape], dt, offset=base[0] + offset)

        SLOT = 3 * KD * DE * 4
        wg, wu, wd = [], [], []
        for j in range(SLOTS):
            wg.append(at(f"wg{j}", j * SLOT, [KD, DE]))
            wu.append(at(f"wu{j}", j * SLOT + 8 * KB, [KD, DE]))
            wd.append(at(f"wd{j}", j * SLOT + 16 * KB, [ME, D]))
        w_low = [at(f"w_low{j}", j * SLOT, [CHUNKS, KC, DE], F32R) for j in range(SLOTS)]
        o = SLOT
        qT = at("qT", o, [NA, SEQ]); o += 8 * KB
        kT = at("kT", o, [NA, SEQ]); o += 8 * KB
        iqT = at("iqT", o, [NA, SEQ]); o += 8 * KB
        v_sb = at("v_sb", o, [NT, AW]); o += 8 * KB
        bias8 = at("bias8", o, [HEADS, SEQ]); o += 16 * KB
        uT = at("uT", o, [NA, PAD + SEQ]); o += NA * (PAD + SEQ) * 4
        keep = [None] + [at(f"keep{b}", o + 256 * (b - 1) * (b + 2), [P * (b + 1)]) for b in range(1, NT)]; o += 4608
        wik = at("wik", o, [KD, HD + HEADS])
        lg = [at(f"lg{i}", o + 2 * KB * i, [SEQ]) for i in range(3)]; o += 6 * KB
        pT = [at(f"pT{i}", o + 2 * KB * i, [SEQ]) for i in range(2)]; o += 4 * KB
        assert o <= 4 * SLOT
        RB = KD * AW * 4
        ring = [at(f"ring{i}", 4 * SLOT + RB * i, [KD, AW]) for i in range(3)]
        wo = [at("wo0", 4 * SLOT + 2 * RB, [KD // 2, D]), at("wo1", 4 * SLOT, [KD // 2, D])]
        g1 = at("g1", 4 * SLOT + RB, [D])
        b1 = at("b1", 4 * SLOT + RB + 4 * KB, [D])
        yg = [[at(f"yg{t}_{c}", (2 * t + c) * 4 * KB, [D]) for c in range(2)] for t in range(NT)]
        res = at("res", 2 * SLOT, [NT, D])
        g2 = at("g2", 3 * SLOT + 16 * KB, [D])
        b2 = at("b2", 3 * SLOT + 20 * KB, [D])
        o_rows = at("o_rows", 6 * SLOT, [NT, D])
        o_rowsT = at("o_rowsT", 3 * SLOT, [KD, SEQ])
        o_sil = at("o_sil", 5 * SLOT, [ME, SEQ])
        o_act = at("o_act", 5 * SLOT + 4 * KB, [ME, SEQ])
        OSLOT = 4
        o = 6 * SLOT
        h = at("h", o, [NT, D])
        w_high = at("w_high", o, [CHUNKS, KC, DE], F32R)
        o += 16 * KB
        xT = at("xT", o, [KD, SEQ])
        mixT = at("mixT", o, [KD, SEQ])
        xe = [at(f"xe{i}", o + 4 * KB * i, [D]) for i in range(2)]
        xeT = [at(f"xeT{i}", o + 8 * KB + 4 * KB * i, [KD, 2, CAP], F32R) for i in range(2)]
        o += 16 * KB
        ptmp = [at(f"ptmp{i}", o + 2176 * i, [PAD + SEQ]) for i in range(2)]
        lg += [at(f"lg{3 + i}", o + 2 * KB * i, [SEQ]) for i in range(2)]
        hT = [at(f"hT{i}", o + 4 * KB * i, [KD, P]) for i in range(2)]
        ye = [at(f"ye{i}", o + 4 * KB * i, [D]) for i in range(2)]
        o += 8 * KB
        ikT = at("ikT", o, [SEQ])
        score = at("score", o + 2 * KB, [SEQ])
        relu = [at(f"relu{i}", o + 4 * KB + 2 * KB * i, [SEQ]) for i in range(4)]
        bm = [at(f"bm{i}", o + 4 * KB + 2 * KB * i, [SEQ]) for i in range(4)]
        gu_sb = at("gu_sb", o, [2 * DE])
        act_e = [at(f"act_e{i}", o + 4 * KB + 512 * i, [ME, CAP]) for i in range(2)]
        sil = [at(f"sil{i}", o + 5 * KB + 512 * i, [ME, CAP]) for i in range(2)]
        hot_tok = at("hot_tok", o + 6 * KB, [NT, 2, NE])
        hot_rank = at("hot_rank", o + 7 * KB, [NT, 2, NE])
        at_rank = at("at_rank", o + 8 * KB, [NT, 2, CAP])
        iwT = at("iwT", o + 10 * KB, [SEQ])
        o += 12 * KB
        cursor = [o]

        def small(name, shape, dt=F32):
            n = int(np.prod(shape)) * (2 if dt == BF16 else 4)
            t = at(name, cursor[0], shape, dt)
            cursor[0] += (n + 31) // 32 * 32
            return t

        ident = small("ident", [P])
        tri = small("tri", [P])
        ones = small("ones", [P])
        flip = small("flip", [P])
        iw = small("iw", [NT, HEADS])
        wpool = small("wpool", [NA, P])
        pscale = small("pscale", [NA])
        relb = small("relb", [HEADS])
        hfix = small("hfix", [NA, PAD])
        wr = small("wr", [KD, GROUPS + NE])
        br = small("br", [GROUPS + NE])
        m8 = small("m8", [8])
        nmx = small("nmx", [8])
        rsum = small("rsum", [8])
        rinv = small("rinv", [8])
        stats = small("stats", [2, 6])
        mv = small("mv", [2])
        var_e = small("var_e", [1])
        std = small("std", [1])
        rstd = small("rstd", [1])
        nmr = small("nmr", [1])
        iota_e = small("iota_e", [NE])
        fold = small("fold", [CAP])
        gid = small("gid", [GROUPS, PER_GROUP])
        iota_r = small("iota_r", [CAP])
        gl = small("gl", [NT, 8])
        lf = small("lf", [NE])
        gm8 = small("gm8", [8])
        gi8 = small("gi8", [8], U32)
        gidx = small("gidx", [1])
        em8 = small("em8", [NT, 8])
        ei8 = small("ei8", [8], U32)
        eidx = small("eidx", [NT, 2])
        tok = small("tok", [NT])
        lsti = small("lsti", [NE], U32)
        cur = [small(f"cur{i}", [1], U32) for i in range(2)]
        rk = small("rk", [NT, 2])
        fits = small("fits", [NT, 2])
        wfit = small("wfit", [NT, 2])
        over = small("over", [NT, NE])
        over_e = small("over_e", [NT])
        pen = small("pen", [NE])
        hot = small("hot", [NT, 2, NE])
        hsum = small("hsum", [NT, NE])
        neg = small("neg", [NT, 2])
        zs = small("zs", [NT, 2])
        ex = small("ex", [NT, 4])
        wt = small("wt", [NT, 2])
        rank1 = small("rank1", [NT, NE])
        slotf = small("slotf", [NT, 2])
        sloti = small("sloti", [NT, 2], U32)
        scr = small("scr", [NE])
        mosti = small("mosti", [1], I32)
        brow = at("brow", 0, [TW])
        hot_c = at("hot_c", 4 * KB, [TW])
        bias_up = at("bias_up", 8 * KB, [HEADS, SEQ])
        assert base[0] + cursor[0] <= nc.sbuf_usable_end, (base[0] + cursor[0], nc.sbuf_usable_end)

        bank = [ctx.enter_context(nc.psum_tensor(f"bank{i}", [P, 512], F32)) for i in range(8)]

        y_dram = nc.dram_tensor("y_rows", (NE * CAP, D), F32, kind="Internal").ap()
        h_dram = nc.dram_tensor("h_rows", (SEQ, D), F32, kind="Internal").ap()
        row_dram = nc.dram_tensor("bias_rows", (HEADS, TW), F32, kind="Internal")

        def sem(name):
            return ctx.enter_context(nc.semaphore(name))

        x_in = [sem(f"x_in{t}") for t in range(NT)]
        group_in = [sem(f"group_in{i}") for i in range(3)]
        wo_in = sem("wo_in")
        ln1_in = sem("ln1_in")
        ln2_in = sem("ln2_in")
        wik_in = sem("wik_in")
        small_in = sem("small_in")
        onehot_in = sem("onehot_in")
        consts_ready = sem("consts_ready")
        pool_chain = sem("pool_chain")
        dve_chain = sem("dve_chain")
        act_chain = sem("act_chain")
        xT_ps = sem("xT_ps")
        xT_act = sem("xT_act")
        xT_dve = sem("xT_dve")
        row_ps = sem("row_ps")
        row_ready = sem("row_ready")
        row_out = sem("row_out")
        bias_in = sem("bias_in")
        bias_ready = sem("bias_ready")
        flip_ps = sem("flip_ps")
        flip_sb = sem("flip_sb")
        proj_ps = sem("proj_ps")
        proj_sb = sem("proj_sb")
        iwT_ready = sem("iwT_ready")
        iw_ps = sem("iw_ps")
        iw_ready = sem("iw_ready")
        dots_ps = sem("dots_ps")
        relu_ready = sem("relu_ready")
        relu_used = sem("relu_used")
        score_sum = sem("score_sum")
        score_masked = sem("score_masked")
        keep_ready = sem("keep_ready")
        pooled_ready = sem("pooled_ready")
        mixed_ps = sem("mixed_ps")
        mixed_sb = sem("mixed_sb")
        qk_ps = sem("qk_ps")
        bm_ready = sem("bm_ready")
        logit_ready = sem("logit_ready")
        exp_ready = sem("exp_ready")
        rinv_ready = sem("rinv_ready")
        prob_ready = sem("prob_ready")
        pT_ps = sem("pT_ps")
        pT_ready = sem("pT_ready")
        pv_ps = sem("pv_ps")
        attn_sb = sem("attn_sb")
        out_ps = sem("out_ps")
        res_ready = sem("res_ready")
        var_ready = sem("var_ready")
        std_ready = sem("std_ready")
        scale_ready = sem("scale_ready")
        norm_ready = sem("norm_ready")
        gain_ready = sem("gain_ready")
        h_stored = sem("h_stored")
        res_in = sem("res_in")
        res_sum = sem("res_sum")
        h_ready = sem("h_ready")
        hT_ps = sem("hT_ps")
        hT_ready = sem("hT_ready")
        router_ps = sem("router_ps")
        router_sb = sem("router_sb")
        top_ready = sem("top_ready")
        gate_exp = sem("gate_exp")
        hot_ready = sem("hot_ready")
        rank_ps = sem("rank_ps")
        hot_tok_ready = sem("hot_tok_ready")
        at_rank_ready = sem("at_rank_ready")
        list_ps = sem("list_ps")
        list_ready = sem("list_ready")
        cur_ready = sem("cur_ready")
        gather_begun = sem("gather_begun")
        rows_begun = sem("rows_begun")
        gathered = [sem(f"gathered{i}") for i in range(2)]
        slot_ready = sem("slot_ready")
        w_in_slot = [sem(f"w_in_slot{j}") for j in range(SLOTS)]
        xeT_ps = sem("xeT_ps")
        xe_high = sem("xe_high")
        xe_low = sem("xe_low")
        w_high_ready = sem("w_high_ready")
        w_low_ready = sem("w_low_ready")
        piece_done = sem("piece_done")
        gu_out = sem("gu_out")
        gu_ps = sem("gu_ps")
        silu_ready = sem("silu_ready")
        act_ready = sem("act_ready")
        y_ps = sem("y_ps")
        y_lo = sem("y_lo")
        y_hi = sem("y_hi")
        y_stored = [sem(f"y_stored{i}") for i in range(2)]
        y_gathered = [sem(f"y_gathered{t}") for t in range(NT)]
        out_stored = sem("out_stored")
        count_ready = sem("count_ready")
        o_rows_in = sem("o_rows_in")
        o_rowsT_ps = sem("o_rowsT_ps")
        o_rowsT_ready = sem("o_rowsT_ready")
        o_w_in = sem("o_w_in")
        o_gu_ps = sem("o_gu_ps")
        o_silu_ready = sem("o_silu_ready")
        o_act_ready = sem("o_act_ready")
        o_weight_ready = sem("o_weight_ready")
        o_y_ps = sem("o_y_ps")
        o_added = sem("o_added")
        o_chain = sem("o_chain")

        group_cols = [IQ_OFF, Q_OFF, K_OFF, U_OFF, V_OFF]
        IQ, Q, K, U, V = range(5)
        ring_of = [0, 1, 2, 0, 1]
        tiles = [("ik", 0)] + [(IQ, m) for m in range(NA)]
        front = [("tile", i) for i in range(5)] + [("iw",)] + [("score", 1, j) for j in range(HEADS)]
        for more, b in ((2, 2), (3, 3)):
            for _ in range(more):
                front.append(("tile", len(tiles)))
                tiles.append([(g, m) for g in (Q, K) for m in range(NA)][len(tiles) - 5])
            front += [("score", b, j) for j in range(HEADS)]
            if b == 2:
                front += [("flip", hh) for hh in range(HEADS)]
        for g, m in [(g, m) for g in (Q, K, U, V) for m in range(NA)][len(tiles) - 5:]:
            front.append(("tile", len(tiles)))
            tiles.append((g, m))
        tile_no = {t: i for i, t in enumerate(tiles)}
        score_no = {(b, j): (b - 1) * HEADS + j for b in range(1, NT) for j in range(HEADS)}
        units = [(b, hh) for b in range(NT) for hh in range(HEADS)]
        NU = len(units)

        def keys(b):
            return P * (b + 1)

        def piece(j, c):
            return (wg, wu)[c * KC // KD][j][:, c * KC % KD:c * KC % KD + KC, :]

        def half(hh):
            return slice(HD * (hh % 2), HD * (hh % 2) + HD)

        SMALLS = 6 + NA

        block = ctx.enter_context(nc.Block())

        @block.sync
        def _(sp):
            win = w_in[0].rearrange("(k p) n -> p k n", p=P)
            xv = x[0].rearrange("(t p) d -> t p d", p=P)
            for t in range(NT):
                sp.dma_start(h[:, t, :], xv[t]).then_inc(x_in[t], 16)
                if t == 0:
                    sp.dma_start(wik[:, :, :], win[:, :, IK_OFF:U_OFF]).then_inc(wik_in, 16)
            for g in range(5):
                if g >= 3:
                    sp.wait_ge(proj_ps, tile_no[(g - 3, NA - 1)] + 1)
                sp.dma_start(ring[ring_of[g]][:, :, :], win[:, :, group_cols[g]:group_cols[g] + AW]).then_inc(group_in[ring_of[g]], 16)
            wov = w_out[0].rearrange("(k p) n -> p k n", p=P)
            sp.wait_ge(proj_ps, tile_no[(K, NA - 1)] + 1)
            sp.dma_start(wo[0][:, :, :], wov[:, 0:KD // 2, :]).then_inc(wo_in, 16)
            sp.wait_ge(proj_ps, tile_no[(U, NA - 1)] + 1)
            sp.dma_start(wo[1][:, :, :], wov[:, KD // 2:KD, :]).then_inc(wo_in, 16)
            sp.wait_ge(proj_ps, tile_no[(V, NA - 1)] + 1)
            sp.dma_start(g1[:, :], ln1_g[0].partition_broadcast(P)).then_inc(ln1_in, 16)
            sp.dma_start(b1[:, :], ln1_b[0].partition_broadcast(P)).then_inc(ln1_in, 16)

            def load_expert(e, j, loaded=None):
                loaded = loaded or w_in_slot[j]
                for dst, src in ((wg[j][:, :, :], w_gate), (wu[j][:, :, :], w_up)):
                    sp.dma_start(dst, src[0, bass.ds(e, 1), :, :].rearrange("o (p k) f -> p (o k) f", p=P)).then_inc(loaded, 16)
                sp.dma_start(wd[j][:, :, :], w_down[0, bass.ds(e, 1), :, :].rearrange("o (m p) n -> p (o m) n", p=P)).then_inc(loaded, 16)

            load_expert(0, 0)
            sp.wait_ge(attn_sb, NT)
            for j in range(1, 4):
                load_expert(j, j)
            for t in range(NT):
                sp.wait_ge(h_ready, t + 1)
                sp.dma_start(h_dram[P * t:P * t + P, :], h[:, t, :]).then_inc(h_stored, 16)
            for j in range(4, SLOTS):
                load_expert(j, j)
            with sp.Fori(0, NE // SLOTS - 1) as g:
                for j in range(SLOTS):
                    sp.wait_ge(y_ps, g * SLOTS + j + 1)
                    load_expert(g * SLOTS + SLOTS + j, j)
            for j in range(NE % SLOTS):
                e = NE // SLOTS * SLOTS + j
                sp.wait_ge(y_ps, e - SLOTS + 1)
                load_expert(e, j)
            sp.wait_ge(y_ps, NE - NE % SLOTS - SLOTS + 4)
            sp.dma_start(res[:, :, :], h_dram.rearrange("(t p) d -> p t d", p=P)).then_inc(res_in, 16)
            sp.dma_start(g2[:, :], ln2_g[0].partition_broadcast(P)).then_inc(ln2_in, 16)
            sp.dma_start(b2[:, :], ln2_b[0].partition_broadcast(P)).then_inc(ln2_in, 16)
            sp.wait_ge(y_ps, NE)
            sp.wait_ge(count_ready, 1)
            with sp.If(sp.value_load(mosti[0:1, 0:1], min_val=0, max_val=SEQ) > CAP):
                sp.dma_start(o_rows[:, :, :], h_dram.rearrange("(t p) d -> p t d", p=P)).then_inc(o_rows_in, 16)
                with sp.Fori(0, NE) as e:
                    sp.wait_ge(o_y_ps, e * NT + 1)
                    load_expert(e, OSLOT, o_w_in)
            ov = out[0].rearrange("(t p) d -> t p d", p=P)
            for t in range(NT):
                sp.wait_ge(h_ready, NT + t + 1)
                sp.dma_start(ov[t], res[:, t, :]).then_inc(out_stored, 16)
            sp.wait_ge(out_stored, 16 * NT)

        @block.gpsimd
        def _(pool):
            n = [0]

            def link(ins):
                n[0] += 1
                ins.then_inc(pool_chain, 1)
                pool.wait_ge(pool_chain, n[0])

            link(pool.memset(ident[:, :], 0.0))
            link(pool.affine_select(out=ident[:, :], in_=ident[:, :], compare_op=ALU.not_equal, fill=1.0, base=0,
                                    pattern=[[-1, P]], channel_multiplier=1))
            link(pool.memset(flip[:, :], 0.0))
            link(pool.affine_select(out=flip[:, :], in_=flip[:, :], compare_op=ALU.not_equal, fill=1.0, base=-(P - 1),
                                    pattern=[[1, P]], channel_multiplier=1))
            pool.memset(ones[:, :], 1.0).then_inc(consts_ready, 1)
            link(pool.memset(tri[:, :], 1.0))
            link(pool.affine_select(out=tri[:, :], in_=tri[:, :], compare_op=ALU.is_gt, fill=0.0, base=0,
                                    pattern=[[1, P]], channel_multiplier=-1))
            link(pool.memset(uT[:, :, 0:PAD], 0.0))
            link(pool.memset(ptmp[0][:, 0:PAD], 0.0))
            link(pool.memset(ptmp[1][:, 0:PAD], 0.0))
            link(pool.memset(gl[:, :, :], -BIG))
            for t, pat, b0, cm in ((iota_e, [[1, NE]], 0, 0), (iota_r, [[1, CAP]], 1, 0)):
                link(pool.iota(t[:, :], pattern=pat, base=b0, channel_multiplier=cm, allow_small_or_imprecise_dtypes=True))
            link(pool.iota(gid[:, :, :], pattern=[[1, GROUPS], [0, PER_GROUP]], base=0, channel_multiplier=0,
                           allow_small_or_imprecise_dtypes=True))
            link(pool.memset(fold[:, :], 0.0))
            for first_row in (0, CAP):
                link(pool.affine_select(out=fold[:, :], in_=fold[:, :], compare_op=ALU.not_equal, fill=1.0, base=-first_row,
                                        pattern=[[-1, CAP]], channel_multiplier=1))
            pool.iota(tok[:, :], pattern=[[P, NT]], base=0, channel_multiplier=1,
                      allow_small_or_imprecise_dtypes=True).then_inc(consts_ready, 1)

            for b in range(1, NT):
                pool.wait_ge(score_sum, b)
                d = score[:, P * b:P * b + P]
                pool.affine_select(out=d, in_=d, compare_op=ALU.is_ge, fill=NONCAUSAL, base=0, pattern=[[-1, P]],
                                   channel_multiplier=1).then_inc(score_masked, 1)
                if b == 2:
                    for hh in range(HEADS):
                        pool.wait_ge(flip_sb, hh + 1)
                        pool.affine_select(out=bias8[:, hh, :], in_=bias8[:, hh, :], compare_op=ALU.is_ge, fill=-BIG, base=SEQ - P,
                                           pattern=[[-1, SEQ]], channel_multiplier=1).then_inc(bias_ready, 1)
            pool.wait_ge(small_in, 16 * SMALLS)
            for g, w in enumerate(WINDOWS):
                pool.wait_ge(proj_sb, tile_no[(U, g)] + 1)
                src, step, i = uT[:, g, :], 1, 0
                while step < w:
                    dst = ptmp[i]
                    link(pool.tensor_tensor(dst[:, PAD:], src[:, PAD:], src[:, PAD - step:PAD + SEQ - step], ALU.add))
                    src, step, i = dst, 2 * step, 1 - i
                link(pool.tensor_scalar(src[:, PAD:], src[:, PAD:], 1.0 / w, 1.0, ALU.mult, ALU.mult))
                link(pool.tensor_tensor(src[:, PAD:PAD + PAD], src[:, PAD:PAD + PAD], hfix[:, g, :], ALU.mult))
                n[0] += 1
                pool.tensor_tensor(uT[:, g, PAD:], src[:, PAD:], uT[:, g, PAD:], ALU.subtract).then_inc(pool_chain, 1)
                pool.wait_ge(pool_chain, n[0])
                pool.sem_inc(pooled_ready, 1)

            def bias_mask(u):
                b, hh = units[u]
                if b == 0 or hh % 2:
                    return
                pool.wait_ge(keep_ready, b)
                if u < HEADS + 4:
                    pool.wait_ge(relu_used, len(score_no))
                else:
                    pool.wait_ge(logit_ready, u - 3)
                pool.tensor_tensor(bm[u % 4][:, 0:keys(b)], bias8[:, hh, SEQ - keys(b):], keep[b][:, :], ALU.add).then_inc(bm_ready, 1)

            pool.wait_ge(bias_ready, HEADS)
            for u in range(NU):
                b, hh = units[u]
                if u + 3 < NU:
                    bias_mask(u + 3)
                pool.wait_ge(rinv_ready, u + 1)
                p = lg[u % 5][:, 0:keys(b)]
                pool.tensor_scalar(p, p, rinv[:, u % 8:u % 8 + 1], 1.0, ALU.mult, ALU.mult).then_inc(prob_ready, 1)

            pool.wait_ge(ln1_in, 32)
            for t in range(NT):
                pool.wait_ge(gain_ready, t + 1)
                pool.tensor_tensor(h[:, t, :], h[:, t, :], b1[:, :], ALU.add).then_inc(h_ready, 1)

            pool.wait_ge(list_ready, 1)
            pool.wait_ge(h_stored, 16 * NT)
            pool.wait_ge(out_ps, NT)

            def gather(e, j, first):
                i = j % 2
                if not first:
                    pool.wait_ge(xeT_ps, e - 1)
                k = pool.tensor_copy(cur[i][0:CAP, :], lsti[0:CAP, bass.ds(e, 1)])
                k.then_inc(cur_ready, 1)
                pool.wait_ge(cur_ready, e + 1)
                pool.sem_inc(gather_begun, 1)
                pool.indirect_dma_start(out=xe[i][0:CAP, :], out_offset=None, in_=h_dram,
                                        in_offset=bass.IndirectOffsetOnAxis(ap=cur[i][0:CAP, :], axis=0),
                                        ).then_inc(gathered[i], 16)

            for e in range(SLOTS):
                gather(e, e, e < 2)
            with pool.Fori(1, NE // SLOTS) as g:
                for j in range(SLOTS):
                    gather(g * SLOTS + j, j, False)
            for e in range(NE // SLOTS * SLOTS, NE):
                gather(e, e % SLOTS, False)
            pool.wait_ge(res_in, 16)
            for t in range(NT):
                pool.tensor_scalar(res[:, t, :], res[:, t, :], ALPHA, 1.0, ALU.mult, ALU.mult).then_inc(res_sum, 1)

            pool.wait_ge(slot_ready, 1)
            for i in range(2):
                pool.wait_ge(y_stored[i], 16 * NE // 2)
            pool.wait_ge(y_ps, NE)
            for t in range(NT):
                for c in range(2):
                    pool.indirect_dma_start(out=yg[t][c][:, :], out_offset=None, in_=y_dram,
                                            in_offset=bass.IndirectOffsetOnAxis(ap=sloti[:, t, c:c + 1], axis=0),
                                            ).then_inc(y_gathered[t], 16)
            pool.wait_ge(ln2_in, 32)
            for t in range(NT):
                pool.wait_ge(gain_ready, NT + t + 1)
                pool.tensor_tensor(res[:, t, :], res[:, t, :], b2[:, :], ALU.add).then_inc(h_ready, 1)

        @block.scalar
        def _(act):
            act.dma_start(relb[0:BUCKETS, :], rel_bias).then_inc(onehot_in, 16)
            act.dma_start(hot_c[0:BUCKETS, :], onehot).then_inc(onehot_in, 16)
            for g in range(1, 2 * NT, 2):
                act.wait_ge(xT_ps, g + 1)
                act.activation(xT[:, 4:8, P * (g // 2):P * (g // 2) + P], bank[1][:, :].rearrange("p (k t) -> p k t", k=4),
                               ACT.Copy).then_inc(xT_act, 1)
            act.wait_ge(row_ready, 2)
            act.dma_start(row_dram.ap(), brow[0:HEADS, :]).then_inc(row_out, 16)
            act.wait_ge(row_out, 16)
            act.dma_start(bias_up[:, :, :], bass.AP(row_dram, 0, [[1, P], [TW, HEADS], [1, SEQ]])).then_inc(bias_in, 16)

            for item in front:
                if item == ("score", 1, 0):
                    act.wait_ge(group_in[2], 16)
                    act.dma_start(wpool[:, :, :], w_pool[0].rearrange("g c d -> c g d")).then_inc(small_in, 16)
                    with nc.allow_non_contiguous_dma(reason="512 elements in all"):
                        act.dma_start(pscale[:, :], pool_scale[0].rearrange("(g p) -> p g", p=P)).then_inc(small_in, 16)
                    for g in range(NA):
                        act.dma_start(hfix[:, g, :], headfix[g].partition_broadcast(P)).then_inc(small_in, 16)
                    act.dma_start(wr[:, :, 0:GROUPS], w_r1[0].rearrange("(k p) n -> p k n", p=P)).then_inc(small_in, 16)
                    act.dma_start(wr[:, :, GROUPS:], w_r2[0].rearrange("(k p) n -> p k n", p=P)).then_inc(small_in, 16)
                    act.dma_start(br[:, 0:GROUPS], b_r1[0].partition_broadcast(P)).then_inc(small_in, 16)
                    act.dma_start(br[:, GROUPS:], b_r2[0].partition_broadcast(P)).then_inc(small_in, 16)
                if item[0] == "tile":
                    i = item[1]
                    kind, m = tiles[i]
                    act.wait_ge(proj_ps, i + 1)
                    if kind == "ik":
                        act.activation(ikT[0:HD, :], bank[2][0:HD, :], ACT.Copy)
                        act.activation(ikT[HD:P, :], bank[2][0:HD, :], ACT.Copy)
                        act.activation(iwT[0:HEADS, :], bank[2][HD:HD + HEADS, :], ACT.Copy).then_inc(proj_sb, 1)
                        continue
                    dst = {IQ: iqT[:, m, :], Q: qT[:, m, :], K: kT[:, m, :],
                           U: uT[:, m, PAD:], V: v_sb[:, m, :]}[kind]
                    act.activation(dst, bank[2 + i % 2][:, :], ACT.Copy).then_inc(proj_sb, 1)
                elif item[0] == "flip":
                    hh = item[1]
                    act.wait_ge(flip_ps, hh + 1)
                    act.activation(bias8[:, hh, :], bank[4 + 3 * (hh % 2)][:, :], ACT.Copy).then_inc(flip_sb, 1)
                elif item[0] == "score":
                    _, b, j = item
                    s = score_no[(b, j)]
                    act.wait_ge(dots_ps, s + 1)
                    if s >= 4:
                        act.wait_ge(relu_used, s - 3)
                    act.activation(relu[s % 4][:, 0:keys(b)], bank[5 + s % 2][:, 0:keys(b)], ACT.Relu, scale=SCALE).then_inc(relu_ready, 1)
            for g in range(NA):
                act.wait_ge(mixed_ps, g + 1)
                act.activation(mixT[:, NA + g, :], bank[2 + g % 2][:, :], ACT.Copy, scale=pscale[:, g:g + 1]).then_inc(mixed_sb, 1)

            for u in range(NU + 4):
                if u < NU:
                    b, hh = units[u]
                    act.wait_ge(logit_ready, u + 1)
                    p = lg[u % 5][:, 0:keys(b)]
                    if u >= 8:
                        act.wait_ge(rinv_ready, u - 7)
                    act.activation(p, p, ACT.Exp, bias=nmx[:, u % 8:u % 8 + 1], scale=-1.0,
                                   accum_out=rsum[:, u % 8:u % 8 + 1]).then_inc(exp_ready, 1)
                if 0 <= u - 3 < NU:
                    w = u - 3
                    b, hh = units[w]
                    act.wait_ge(pT_ps, w + 1)
                    if w >= 2:
                        act.wait_ge(pv_ps, w - 1)
                    act.activation(pT[w % 2][:, 0:keys(b)], bank[4 + w % 2][:, 0:keys(b)], ACT.Copy).then_inc(pT_ready, 1)
                if u >= 4 and units[u - 4][1] == HEADS - 1:
                    b = units[u - 4][0]
                    act.wait_ge(pv_ps, u - 3)
                    act.activation(mixT[:, 0:NA, P * b:P * b + P], bank[6 + b % 2][:, :].rearrange("p (m t) -> p m t", m=NA),
                                   ACT.Copy).then_inc(attn_sb, 1)

            def normalise(t, k, rows):
                act.wait_ge(var_ready, k + 1)
                act.activation(std[:, :], var_e[:, :], ACT.Sqrt).then_inc(std_ready, 1)
                act.wait_ge(scale_ready, k + 1)
                act.activation(rows, rows, ACT.Identity, bias=nmr[:, 0:1], scale=rstd[:, 0:1]).then_inc(norm_ready, 1)

            def transposed_h(t):
                act.wait_ge(hT_ps, t + 1)
                if t >= 2:
                    act.wait_ge(router_ps, t - 1)
                for k in range(2):
                    act.activation(hT[t % 2][:, 4 * k:4 * k + 4, :], bank[4 + k][:, :].rearrange("p (k t) -> p k t", k=4),
                                   ACT.Copy).then_inc(hT_ready, 1)

            for t in range(NT):
                normalise(t, t, h[:, t, :])
                if t >= 1:
                    transposed_h(t - 1)
            transposed_h(NT - 1)
            for t in range(NT):
                act.wait_ge(top_ready, t + 1)
                act.activation(ex[:, t, :], gl[:, t, 0:GROUPS], ACT.Exp, bias=neg[:, t, 0:1], accum_out=zs[:, t, 0:1])
                act.activation(zs[:, t, 1:2], em8[:, t, 1:2], ACT.Exp, bias=neg[:, t, 1:2]).then_inc(gate_exp, 1)

            def rows_high(e, j, first):
                i = j % 2
                act.wait_ge(xeT_ps, e + 1)
                if not first:
                    act.wait_ge(piece_done, CHUNKS * e - CHUNKS)
                act.activation(xeT[i][:, :, 0, :], bank[0][:, 0:KD * CAP].rearrange("p (k t) -> p k t", k=KD), ACT.Copy).then_inc(xe_high, 1)

            def weights_high(e, j, first, turn, pieces):
                act.wait_ge(w_in_slot[j], turn * 48 + 48)
                for c in pieces:
                    if not first:
                        act.wait_ge(piece_done, CHUNKS * e - CHUNKS + c + 1)
                    act.activation(w_high[:, c, :, :], piece(j, c), ACT.Copy).then_inc(w_high_ready, 1)

            def gate_up_out(e, first):
                act.wait_ge(piece_done, CHUNKS * e + CHUNKS)
                if not first:
                    act.wait_ge(gu_ps, e)
                act.activation(gu_sb[0:2 * CAP, :], bank[1][0:2 * CAP, :], ACT.Copy).then_inc(gu_out, 1)

            def silu(e, j, first):
                i = j % 2
                act.wait_ge(gu_ps, e + 1)
                if not first:
                    act.wait_ge(act_ready, e - 1)
                act.activation(sil[i][:, :, :], bank[2][:, 0:ME * CAP].rearrange("p (m t) -> p m t", m=ME), ACT.Silu).then_inc(silu_ready, 1)

            def y_out(e, j, first, occurrence):
                i = j % 2
                act.wait_ge(y_ps, e + 1)
                if not first:
                    act.wait_ge(y_stored[i], occurrence * 16)
                act.activation(ye[i][0:CAP, 512:], bank[5 + 2 * i][0:CAP, :], ACT.Copy).then_inc(y_hi, 1)
                act.wait_ge(y_hi, e + 1)
                act.wait_ge(y_lo, e + 1)
                act.dma_start(y_dram[bass.ds(e * CAP, CAP), :], ye[i][0:CAP, :]).then_inc(y_stored[i], 16)

            act.wait_ge(h_stored, 16 * NT)
            act.wait_ge(hT_ps, NT)
            weights_high(0, 0, True, 0, range(CHUNKS))
            rows_high(0, 0, True)
            rows_high(1, 1, True)
            weights_high(1, 1, False, 0, range(CHUNKS - 1))
            gate_up_out(0, True)
            weights_high(1, 1, False, 0, (CHUNKS - 1,))
            silu(0, 0, True)

            def step(e, j, turn, first, second, occurrence):
                turn2, slot2 = turn + (j + 2) // SLOTS, (j + 2) % SLOTS
                rows_high(e + 2, j, False)
                weights_high(e + 2, slot2, False, turn2, range(CHUNKS - 1))
                gate_up_out(e + 1, False)
                weights_high(e + 2, slot2, False, turn2, (CHUNKS - 1,))
                y_out(e, j, second, occurrence)
                silu(e + 1, j + 1, first)

            for e in range(SLOTS):
                step(e, e, 0, e < 1, e < 2, e // 2)
            with act.Fori(1, NE // SLOTS) as g:
                for j in range(SLOTS):
                    step(g * SLOTS + j, j, g, False, False, g * (SLOTS // 2) + j // 2)
            for e in range(NE // SLOTS * SLOTS, NE):
                if e + 1 < NE:
                    gate_up_out(e + 1, False)
                y_out(e, e, False, e // 2)
                if e + 1 < NE:
                    silu(e + 1, e + 1, False)

            act.wait_ge(count_ready, 1)
            with act.If(act.value_load(mosti[0:1, 0:1], min_val=0, max_val=SEQ) > CAP):
                for t in range(NT):
                    for k in range(2):
                        act.wait_ge(o_rowsT_ps, 2 * t + k + 1)
                        act.activation(o_rowsT[:, 4 * k:4 * k + 4, P * t:P * t + P], bank[k][:, :].rearrange("p (k t) -> p k t", k=4),
                                       ACT.Copy).then_inc(o_rowsT_ready, 1)
                with act.Fori(0, NE) as e:
                    act.wait_ge(o_gu_ps, e + 1)
                    act.wait_ge(o_act_ready, e + 1)
                    for m in range(ME):
                        act.activation(o_sil[:, m, :], bank[m][:, :], ACT.Silu).then_inc(o_silu_ready, 1)

            for t in range(NT):
                normalise(t, NT + t, res[:, t, :])

        @block.vector
        def _(dve):
            n = [0]

            def link(ins):
                n[0] += 1
                ins.then_inc(dve_chain, 1)
                dve.wait_ge(dve_chain, n[0])

            for g in range(0, 2 * NT, 2):
                dve.wait_ge(xT_ps, g + 1)
                dve.tensor_copy(xT[:, 0:4, P * (g // 2):P * (g // 2) + P], bank[0][:, :].rearrange("p (k t) -> p k t", k=4)).then_inc(xT_dve, 1)
            dve.wait_ge(row_ps, 1)
            for i, bk in enumerate((4, 7)):
                dve.tensor_scalar(brow[0:HEADS, TW // 2 * i:TW // 2 * (i + 1)], bank[bk][0:HEADS, 0:TW // 2], 1.0 / SCALE, None,
                                  ALU.mult).then_inc(row_ready, 1)
            dve.wait_ge(iw_ps, 1)
            link(dve.tensor_scalar(iw[:, :, :], bank[0][:, 0:NT * HEADS].rearrange("p (t j) -> p t j", t=NT), HEADS ** -0.5, None, ALU.mult))
            for b in range(1, NT):
                s_b = score[:, 0:keys(b)]
                for j in range(HEADS):
                    s = score_no[(b, j)]
                    dve.wait_ge(relu_ready, s + 1)
                    r = relu[s % 4][:, 0:keys(b)]
                    if j == 0:
                        ins = dve.tensor_scalar(s_b, r, iw[:, b, 0:1], None, ALU.mult)
                    else:
                        ins = dve.scalar_tensor_tensor(out=s_b, in0=r, scalar=iw[:, b, j:j + 1], in1=s_b, op0=ALU.mult, op1=ALU.add)
                    ins.then_inc(relu_used, 1)
                    dve.wait_ge(relu_used, s + 1)
                dve.sem_inc(score_sum, 1)
                dve.wait_ge(score_masked, b)
                for _ in range(TOPK // 8):
                    link(dve.max(m8[:, :], s_b))
                    link(dve.match_replace(out=s_b, in_to_replace=m8[:, :], in_values=s_b, imm_value=TAKEN))
                n[0] += 1
                dve.tensor_scalar(keep[b][:, :], s_b, TAKEN / 2, -BIG, ALU.is_gt, ALU.mult).then_inc(dve_chain, 1)
                dve.wait_ge(dve_chain, n[0])
                dve.sem_inc(keep_ready, 1)

            dve.wait_ge(bias_ready, HEADS)
            for u in range(NU + 1):
                if u < NU:
                    b, hh = units[u]
                    dve.wait_ge(qk_ps, u + 1)
                    add = bias8[:, hh, SEQ - keys(b):]
                    if b:
                        add = bm[u % 4][:, 0:keys(b)]
                        if hh % 2:
                            link(dve.tensor_tensor(add, bias8[:, hh, SEQ - keys(b):], keep[b][:, :], ALU.add))
                        else:
                            dve.wait_ge(bm_ready, (u - HEADS) // 2 + 1)
                    if u >= 5:
                        dve.wait_ge(pT_ps, u - 4)
                    dve.tensor_tensor_reduce(out=lg[u % 5][:, 0:keys(b)], in0=bank[u % 2][:, 0:keys(b)], in1=add, scale=-SCALE,
                                             scalar=3e38, op0=ALU.add, op1=ALU.min, accum_out=nmx[:, u % 8:u % 8 + 1]).then_inc(logit_ready, 1)
                if u >= 1:
                    dve.wait_ge(exp_ready, u)
                    if u >= 9:
                        dve.wait_ge(prob_ready, u - 8)
                    dve.reciprocal(rinv[:, (u - 1) % 8:(u - 1) % 8 + 1], rsum[:, (u - 1) % 8:(u - 1) % 8 + 1]).then_inc(rinv_ready, 1)

            def normalise(t, k, rows, gain):
                for i in range(2):
                    link(dve.bn_stats(stats[:, i, :], rows[:, 512 * i:512 * i + 512]))
                link(dve.bn_aggr(mv[:, :], stats[:, :, :]))
                dve.tensor_scalar(var_e[:, :], mv[:, 1:2], EPS, None, ALU.add).then_inc(var_ready, 1)
                dve.wait_ge(std_ready, k + 1)
                link(dve.reciprocal(rstd[:, :], std[:, :]))
                dve.tensor_scalar(nmr[:, :], mv[:, 0:1], rstd[:, 0:1], -1.0, ALU.mult, ALU.mult).then_inc(scale_ready, 1)
                dve.wait_ge(norm_ready, k + 1)
                dve.tensor_tensor(rows, rows, gain, ALU.mult).then_inc(gain_ready, 1)

            def route(t):
                dve.wait_ge(router_ps, t + 1)
                ps = bank[6 + t % 2][:, 0:GROUPS + NE]
                link(dve.tensor_tensor(gl[:, t, 0:GROUPS], ps[:, 0:GROUPS], br[:, 0:GROUPS], ALU.add))
                dve.tensor_tensor(lf[:, :], ps[:, GROUPS:], br[:, GROUPS:], ALU.add).then_inc(router_sb, 1)
                dve.wait_ge(router_sb, t + 1)
                link(dve.max(gm8[:, :], gl[:, t, :]))
                link(dve.max_index(gi8[:, :], gm8[:, :], gl[:, t, :]))
                link(dve.tensor_copy(gidx[:, :], gi8[:, 0:1]))
                link(dve.tensor_scalar(pen[:, :], gid[:, :, :].rearrange("p g e -> p (g e)"), gidx[:, 0:1], -BIG, ALU.not_equal, ALU.mult))
                link(dve.tensor_tensor(lf[:, :], lf[:, :], pen[:, :], ALU.add))
                link(dve.max(em8[:, t, :], lf[:, :]))
                link(dve.max_index(ei8[:, :], em8[:, t, :], lf[:, :]))
                link(dve.tensor_copy(eidx[:, t, :], ei8[:, 0:2]))
                link(dve.tensor_scalar(neg[:, t, 0:1], gm8[:, 0:1], -1.0, None, ALU.mult))
                link(dve.tensor_scalar(neg[:, t, 1:2], em8[:, t, 0:1], -1.0, None, ALU.mult))
                dve.sem_inc(top_ready, 1)
                for c in range(2):
                    link(dve.tensor_scalar(hot[:, t, c, :], iota_e[:, :], eidx[:, t, c:c + 1], None, ALU.is_equal))
                dve.tensor_tensor(hsum[:, t, :], hot[:, t, 0, :], hot[:, t, 1, :], ALU.add).then_inc(hot_ready, 1)
                dve.tensor_scalar(hot_tok[:, t, :, :], hot[:, t, :, :], tok[:, t:t + 1], None, ALU.mult).then_inc(hot_tok_ready, 1)

            dve.wait_ge(small_in, 16 * SMALLS)
            dve.wait_ge(consts_ready, 2)
            for t in range(NT):
                dve.wait_ge(out_ps, t + 1)
                for i in range(2):
                    hv = h[:, t, 512 * i:512 * i + 512]
                    link(dve.scalar_tensor_tensor(out=hv, in0=hv, scalar=ALPHA, in1=bank[(2 if t % 2 == 0 else 0) + i][:, :],
                                                  op0=ALU.mult, op1=ALU.add))
                dve.sem_inc(res_ready, 1)
                if t == 0:
                    dve.wait_ge(ln1_in, 32)
                normalise(t, t, h[:, t, :], g1[:, :])
                if t >= 1:
                    route(t - 1)
            route(NT - 1)
            dve.wait_ge(rank_ps, 1)
            dve.wait_ge(hot_ready, NT)
            link(dve.scalar_tensor_tensor(out=rank1[:, :, :], in0=bank[7][:, 0:NE * NT].rearrange("p (t e) -> p t e", t=NT), scalar=1.0,
                                          in1=hsum[:, :, :], op0=ALU.add, op1=ALU.mult))
            for c in range(2):
                link(dve.tensor_tensor(hot_rank[:, :, c, :], hot[:, :, c, :], rank1[:, :, :], ALU.mult))
            link(dve.tensor_reduce(out=rk[:, :, :], in_=hot_rank[:, :, :, :], axis=AX.X, op=ALU.add))
            for t in range(NT):
                ins = dve.tensor_tensor(at_rank[:, t, :, :], iota_r[:, :].unsqueeze(1).to_broadcast([P, 2, CAP]),
                                        rk[:, t, :].unsqueeze(2).to_broadcast([P, 2, CAP]), ALU.is_equal)
            link(ins)
            dve.sem_inc(at_rank_ready, 1)
            dve.wait_ge(list_ps, 1)
            dve.tensor_copy(lsti[0:CAP, :], bank[2][0:CAP, 0:NE]).then_inc(list_ready, 1)
            link(dve.max(m8[:, :], bank[7][:, NE * NT:NE * NT + NE]))
            dve.tensor_copy(mosti[:, :], m8[:, 0:1]).then_inc(count_ready, 1)
            link(dve.tensor_scalar(fits[:, :, :], rk[:, :, :], float(CAP), None, ALU.is_le))
            link(dve.tensor_scalar(rk[:, :, :], rk[:, :, :], float(CAP), -1.0, ALU.min, ALU.add))
            link(dve.scalar_tensor_tensor(out=slotf[:, :, :], in0=eidx[:, :, :], scalar=float(CAP), in1=rk[:, :, :], op0=ALU.mult, op1=ALU.add))
            dve.tensor_copy(sloti[:, :, :], slotf[:, :, :]).then_inc(slot_ready, 1)
            dve.wait_ge(gate_exp, NT)
            link(dve.tensor_scalar(wt[:, :, 0], zs[:, :, 1], 1.0, None, ALU.add))
            link(dve.tensor_tensor(wt[:, :, 0], wt[:, :, 0], zs[:, :, 0], ALU.mult))
            link(dve.reciprocal(wt[:, :, 0], wt[:, :, 0]))
            link(dve.tensor_tensor(wt[:, :, 1], wt[:, :, 0], zs[:, :, 1], ALU.mult))
            link(dve.tensor_tensor(wfit[:, :, :], wt[:, :, :], fits[:, :, :], ALU.mult))
            def gated(e, j, first):
                i = j % 2
                dve.wait_ge(silu_ready, e + 1)
                if not first:
                    dve.wait_ge(y_ps, e - 1)
                dve.tensor_tensor(act_e[i][:, :, :], bank[2][:, ME * CAP:2 * ME * CAP].rearrange("p (m t) -> p m t", m=ME),
                                  sil[i][:, :, :], ALU.mult).then_inc(act_ready, 1)

            def y_out(e, j, first, occurrence):
                i = j % 2
                dve.wait_ge(y_ps, e + 1)
                if not first:
                    dve.wait_ge(y_stored[i], occurrence * 16)
                dve.tensor_copy(ye[i][0:CAP, 0:512], bank[4 + 2 * i][0:CAP, :]).then_inc(y_lo, 1)

            def rows_low(e, j, first):
                i = j % 2
                dve.wait_ge(xe_high, e + 1)
                dve.tensor_tensor(xeT[i][:, :, 1, :], bank[0][:, 0:KD * CAP].rearrange("p (k t) -> p k t", k=KD),
                                  xeT[i][:, :, 0, :].bitcast(F32), ALU.subtract).then_inc(xe_low, 1)

            def weights_low(e, j):
                for c in range(CHUNKS):
                    dve.wait_ge(w_high_ready, CHUNKS * e + c + 1)
                    dve.tensor_tensor(w_low[j][:, c, :, :], piece(j, c), w_high[:, c, :, :].bitcast(F32),
                                      ALU.subtract).then_inc(w_low_ready, 1)

            weights_low(0, 0)
            rows_low(0, 0, True)
            rows_low(1, 1, True)
            weights_low(1, 1)
            gated(0, 0, True)
            for e in range(SLOTS):
                rows_low(e + 2, e, False)
                weights_low(e + 2, (e + 2) % SLOTS)
                y_out(e, e, e < 2, e // 2)
                gated(e + 1, e + 1, e < 1)
            with dve.Fori(1, NE // SLOTS) as g:
                for j in range(SLOTS):
                    rows_low(g * SLOTS + j + 2, j, False)
                    weights_low(g * SLOTS + j + 2, (j + 2) % SLOTS)
                    y_out(g * SLOTS + j, j, False, g * (SLOTS // 2) + j // 2)
                    gated(g * SLOTS + j + 1, j + 1, False)
            for e in range(NE // SLOTS * SLOTS, NE):
                y_out(e, e % SLOTS, False, e // 2)
                if e + 1 < NE:
                    gated(e + 1, e + 1, False)

            with dve.If(dve.value_load(mosti[0:1, 0:1], min_val=0, max_val=SEQ) > CAP):
                for t in range(NT):
                    dve.tensor_scalar(scr[:, :], hot[:, t, 0, :], wt[:, t, 0:1], None, ALU.mult).then_inc(o_chain, 1)
                    dve.wait_ge(o_chain, 3 * t + 1)
                    dve.scalar_tensor_tensor(out=scr[:, :], in0=hot[:, t, 1, :], scalar=wt[:, t, 1:2], in1=scr[:, :],
                                             op0=ALU.mult, op1=ALU.add).then_inc(o_chain, 1)
                    dve.wait_ge(o_chain, 3 * t + 2)
                    dve.scalar_tensor_tensor(out=over[:, t, :], in0=rank1[:, t, :], scalar=float(CAP), in1=scr[:, :],
                                             op0=ALU.is_gt, op1=ALU.mult).then_inc(o_chain, 1)
                    dve.wait_ge(o_chain, 3 * t + 3)
                dve.wait_ge(res_sum, NT)
                dve.sem_inc(o_added, 1)
                dve.sem_inc(o_act_ready, 1)
                with dve.Fori(0, NE) as e:
                    dve.wait_ge(o_added, e * NT + 1)
                    dve.tensor_copy(over_e[:, :], over[:, :, bass.ds(e, 1)].rearrange("p t o -> p (t o)")).then_inc(o_weight_ready, 1)
                    dve.wait_ge(o_silu_ready, e * ME + ME)
                    dve.wait_ge(o_y_ps, e * NT + 1)
                    for m in range(ME):
                        ins = dve.tensor_tensor(o_act[:, m, :], bank[2 + m][:, :], o_sil[:, m, :], ALU.mult)
                    ins.then_inc(o_act_ready, 1)
                    dve.wait_ge(o_weight_ready, e + 1)
                    for t in range(NT):
                        dve.wait_ge(o_y_ps, e * NT + t + 2)
                        for c in range(2):
                            hv = res[:, t, 512 * c:512 * c + 512]
                            ins = dve.scalar_tensor_tensor(out=hv, in0=bank[4 + 2 * (t % 2) + c][:, :], scalar=over_e[:, t:t + 1], in1=hv,
                                                           op0=ALU.mult, op1=ALU.add)
                        ins.then_inc(o_added, 1)
            for t in range(NT):
                dve.wait_ge(y_gathered[t], 32)
                dve.wait_ge(res_sum, NT)
                for c in range(2):
                    link(dve.scalar_tensor_tensor(out=res[:, t, :], in0=yg[t][c][:, :], scalar=wfit[:, t, c:c + 1],
                                                  in1=res[:, t, :], op0=ALU.mult, op1=ALU.add))
                if t == 0:
                    dve.wait_ge(ln2_in, 32)
                normalise(t, NT + t, res[:, t, :], g2[:, :])

        @block.tensor
        def _(pe):
            pe.wait_ge(consts_ready, 1)
            for g in range(2 * NT):
                t, k0 = g // 2, 4 * (g % 2)
                if g % 2 == 0:
                    pe.wait_ge(x_in[t], 16)
                if g >= 2:
                    pe.wait_ge(xT_act if g % 2 else xT_dve, g // 2)
                for k in range(4):
                    ins = pe.transpose(bank[g % 2][:, P * k:P * k + P], h[:, t, P * (k0 + k):P * (k0 + k) + P], ident[:, :])
                ins.then_inc(xT_ps, 1)
            pe.wait_ge(onehot_in, 32)
            for i, bk in enumerate((4, 7)):
                ins = pe.matmul(bank[bk][0:HEADS, 0:TW // 2], relb[0:BUCKETS, :], hot_c[0:BUCKETS, TW // 2 * i:TW // 2 * (i + 1)], start=True, stop=True)
            ins.then_inc(row_ps, 1)
            pe.wait_ge(wik_in, 16)
            pe.wait_ge(xT_act, NT)
            pe.wait_ge(xT_dve, NT)
            seen = set()
            for item in front:
                if item[0] == "tile":
                    i = item[1]
                    kind, m = tiles[i]
                    if kind != "ik" and kind not in seen:
                        seen.add(kind)
                        pe.wait_ge(group_in[ring_of[kind]], 16 * (kind // 3 + 1))
                    if i >= 2:
                        pe.wait_ge(proj_sb, i - 1)
                    for k in range(KD):
                        if kind == "ik":
                            lhsT, rhs = wik[:, k, :], xT[:, k, :]
                        elif kind == V:
                            lhsT, rhs = xT[:, k, P * m:P * m + P], ring[ring_of[kind]][:, k, :]
                        else:
                            lhsT, rhs = ring[ring_of[kind]][:, k, P * m:P * m + P], xT[:, k, :]
                        rows_out = HD + HEADS if kind == "ik" else P
                        ins = pe.matmul(bank[2 + i % 2][0:rows_out, :], lhsT, rhs, start=k == 0, stop=k == KD - 1)
                    ins.then_inc(proj_ps, 1)
                elif item[0] == "iw":
                    pe.wait_ge(proj_sb, 1)
                    for t in range(NT):
                        ins = pe.transpose(bank[0][:, HEADS * t:HEADS * t + HEADS], iwT[0:HEADS, P * t:P * t + P], ident[0:HEADS, 0:HEADS])
                    ins.then_inc(iw_ps, 1)
                elif item[0] == "flip":
                    hh = item[1]
                    pe.wait_ge(bias_in, 16)
                    if hh >= 2:
                        pe.wait_ge(flip_sb, hh - 1)
                    pe.matmul(bank[4 + 3 * (hh % 2)][:, :], flip[:, :], bias_up[:, hh, :], start=True, stop=True).then_inc(flip_ps, 1)
                else:
                    _, b, j = item
                    s = score_no[(b, j)]
                    if s == 0:
                        pe.wait_ge(proj_sb, 5)
                    if s >= 2:
                        pe.wait_ge(relu_ready, s - 1)
                    pe.matmul(bank[5 + s % 2][:, 0:keys(b)], iqT[half(j), j // 2, P * b:P * b + P], ikT[half(j), 0:keys(b)],
                              start=True, stop=True).then_inc(dots_ps, 1)
            pe.wait_ge(small_in, 16 * SMALLS)
            for g in range(NA):
                if g == 0:
                    pe.wait_ge(proj_sb, len(tiles))
                if g >= 2:
                    pe.wait_ge(mixed_sb, g - 1)
                pe.wait_ge(pooled_ready, g + 1)
                pe.matmul(bank[2 + g % 2][:, :], wpool[:, g, :], uT[:, g, PAD:], start=True, stop=True).then_inc(mixed_ps, 1)
            pe.wait_ge(relu_ready, len(score_no))
            for u in range(NU + 4):
                if u < NU:
                    b, hh = units[u]
                    if u >= 2:
                        pe.wait_ge(logit_ready, u - 1)
                    pe.matmul(bank[u % 2][:, 0:keys(b)], qT[half(hh), hh // 2, P * b:P * b + P], kT[half(hh), hh // 2, 0:keys(b)],
                              start=True, stop=True).then_inc(qk_ps, 1)
                if 0 <= u - 3 < NU:
                    w = u - 3
                    b, hh = units[w]
                    pe.wait_ge(prob_ready, w + 1)
                    if w >= 2:
                        pe.wait_ge(pT_ready, w - 1)
                    for k in range(b + 1):
                        ins = pe.transpose(bank[4 + w % 2][:, P * k:P * k + P], lg[w % 5][:, P * k:P * k + P], ident[:, :])
                    ins.then_inc(pT_ps, 1)
                if u >= 4:
                    w = u - 4
                    b, hh = units[w]
                    pe.wait_ge(pT_ready, w + 1)
                    if hh == 0 and b >= 2:
                        pe.wait_ge(attn_sb, b - 1)
                    for k in range(b + 1):
                        ins = pe.matmul(bank[6 + b % 2][half(hh), P * (hh // 2):P * (hh // 2) + P], v_sb[:, k, HD * hh:HD * hh + HD],
                                        pT[w % 2][:, P * k:P * k + P], start=k == 0, stop=k == b)
                    ins.then_inc(pv_ps, 1)
            pe.wait_ge(mixed_sb, NA)
            pe.wait_ge(attn_sb, NT)
            pe.wait_ge(wo_in, 32)

            def router(t):
                pe.wait_ge(h_ready, t + 1)
                if t >= 1:
                    pe.wait_ge(hT_ready, 2 * t)
                for k in range(KD):
                    ins = pe.transpose(bank[4 + k // 4][:, P * (k % 4):P * (k % 4) + P], h[:, t, P * k:P * k + P], ident[:, :])
                ins.then_inc(hT_ps, 1)
                pe.wait_ge(hT_ready, 2 * t + 2)
                if t >= 2:
                    pe.wait_ge(router_sb, t - 1)
                for k in range(KD):
                    ins = pe.matmul(bank[6 + t % 2][:, 0:GROUPS + NE], hT[t % 2][:, k, :], wr[:, k, :], start=k == 0, stop=k == KD - 1)
                ins.then_inc(router_ps, 1)

            for t in range(NT):
                if t >= 2:
                    pe.wait_ge(res_ready, t - 1)
                for i in range(2):
                    for k in range(KD):
                        ins = pe.matmul(bank[(2 if t % 2 == 0 else 0) + i][:, :], mixT[:, k, P * t:P * t + P],
                                        wo[k // 4][:, k % 4, 512 * i:512 * i + 512], start=k == 0, stop=k == KD - 1)
                ins.then_inc(out_ps, 1)
                if t >= 2:
                    router(t - 2)
            router(NT - 2)
            router(NT - 1)
            pe.wait_ge(hot_ready, NT)
            for t in range(NT):
                for s in range(t + 1):
                    ins = pe.matmul(bank[7][:, NE * t:NE * t + NE], (tri if s == t else ones)[:, :], hsum[:, s, :], start=s == 0, stop=s == t)
            for s in range(NT):
                ins = pe.matmul(bank[7][:, NE * NT:NE * NT + NE], ones[:, :], hsum[:, s, :], start=s == 0, stop=s == NT - 1)
            ins.then_inc(rank_ps, 1)
            pe.wait_ge(hot_tok_ready, NT)
            pe.wait_ge(at_rank_ready, 1)
            for t in range(NT):
                for c in range(2):
                    ins = pe.matmul(bank[2][0:CAP, 0:NE], at_rank[:, t, c, :], hot_tok[:, t, c, :], start=t + c == 0, stop=(t, c) == (NT - 1, 1))
            ins.then_inc(list_ps, 1)

            def rows(e, j, first, occurrence):
                i = j % 2
                pe.wait_ge(gathered[i], occurrence * 16 + 16)
                if not first:
                    pe.wait_ge(xe_low, e)
                pe.sem_inc(rows_begun, 1)
                xv = xe[i][0:CAP, :].rearrange("t (p k) -> t k p", k=KD)
                for k in range(KD):
                    ins = pe.transpose(bank[0][:, CAP * k:CAP * k + CAP], xv[:, k, :], ident[0:CAP, 0:CAP])
                ins.then_inc(xeT_ps, 1)

            def gate_up(e, j, first):
                i = j % 2
                pe.wait_ge(xe_low, e + 1)
                if not first:
                    pe.wait_ge(gu_out, e)
                for c in range(CHUNKS):
                    pe.wait_ge(w_low_ready, CHUNKS * e + c + 1)
                    s, k0 = c * KC // KD, c * KC % KD
                    for part in (w_low[j], w_high):
                        for k in range(KC):
                            ins = pe.matmul(bank[1][0:2 * CAP, DE * s:DE * s + DE], xeT[i][:, k0 + k, :, :], part[:, c, k, :],
                                            start=k0 + k == 0 and part is not w_high, stop=k0 + k == KD - 1 and part is w_high)
                    ins.then_inc(piece_done, 1)

            def fold_gate_up(e, first):
                pe.wait_ge(gu_out, e + 1)
                if not first:
                    pe.wait_ge(act_ready, e)
                for m in range(2 * ME):
                    ins = pe.matmul(bank[2][:, CAP * m:CAP * m + CAP], gu_sb[0:2 * CAP, P * m:P * m + P], fold[0:2 * CAP, :], start=True, stop=True)
                ins.then_inc(gu_ps, 1)

            def down(e, j, first):
                i = j % 2
                pe.wait_ge(act_ready, e + 1)
                if not first:
                    pe.wait_ge(y_lo, e - 1)
                    pe.wait_ge(y_hi, e - 1)
                for c in range(2):
                    for m in range(ME):
                        ins = pe.matmul(bank[4 + 2 * i + c][0:CAP, :], act_e[i][:, m, :], wd[j][:, m, 512 * c:512 * c + 512], start=m == 0, stop=m == ME - 1)
                ins.then_inc(y_ps, 1)

            rows(0, 0, True, 0)
            rows(1, 1, False, 0)
            gate_up(0, 0, True)
            fold_gate_up(0, True)
            for e in range(SLOTS):
                rows(e + 2, e + 2, False, (e + 2) // 2)
                gate_up(e + 1, (e + 1) % SLOTS, False)
                down(e, e, e < 2)
                fold_gate_up(e + 1, False)
            with pe.Fori(1, NE // SLOTS) as g:
                for j in range(SLOTS):
                    rows(g * SLOTS + j + 2, j, False, g * (SLOTS // 2) + j // 2 + 1)
                    gate_up(g * SLOTS + j + 1, (j + 1) % SLOTS, False)
                    down(g * SLOTS + j, j, False)
                    fold_gate_up(g * SLOTS + j + 1, False)
            for e in range(NE // SLOTS * SLOTS, NE):
                if e + 1 < NE:
                    gate_up(e + 1, (e + 1) % SLOTS, False)
                down(e, e % SLOTS, False)
                if e + 1 < NE:
                    fold_gate_up(e + 1, False)

            pe.wait_ge(count_ready, 1)
            with pe.If(pe.value_load(mosti[0:1, 0:1], min_val=0, max_val=SEQ) > CAP):
                pe.wait_ge(o_rows_in, 16)
                pe.wait_ge(y_lo, NE)
                pe.wait_ge(y_hi, NE)
                for t in range(NT):
                    for k in range(2):
                        if t:
                            pe.wait_ge(o_rowsT_ready, 2 * t + k - 1)
                        for q in range(4):
                            ins = pe.transpose(bank[k][:, P * q:P * q + P], o_rows[:, t, :].rearrange("p (c k) -> p k c", k=KD)[:, 4 * k + q, :], ident[:, :])
                        ins.then_inc(o_rowsT_ps, 1)
                pe.wait_ge(o_rowsT_ready, 2 * NT)
                pe.sem_inc(o_y_ps, 1)
                with pe.Fori(0, NE) as e:
                    pe.wait_ge(o_w_in, e * 48 + 48)
                    pe.wait_ge(o_act_ready, e + 1)
                    pe.wait_ge(o_added, e * NT + 1)
                    for s, w in enumerate((wg, wu)):
                        for m in range(ME):
                            for k in range(KD):
                                ins = pe.matmul(bank[2 * s + m][:, :], w[OSLOT][:, k, P * m:P * m + P], o_rowsT[:, k, :], start=k == 0, stop=k == KD - 1)
                    ins.then_inc(o_gu_ps, 1)
                    pe.wait_ge(o_act_ready, e + 2)
                    for t in range(NT):
                        if t >= 2:
                            pe.wait_ge(o_added, e * NT + t)
                        for c in range(2):
                            for m in range(ME):
                                ins = pe.matmul(bank[4 + 2 * (t % 2) + c][:, :], o_act[:, m, P * t:P * t + P], wd[OSLOT][:, m, 512 * c:512 * c + 512],
                                                start=m == 0, stop=m == ME - 1)
                        ins.then_inc(o_y_ps, 1)


_INS = ['x', 'w_in', 'w_pool', 'pool_scale', 'w_out', 'rel_bias', 'ln1_g', 'ln1_b', 'w_r1', 'b_r1', 'w_r2', 'b_r2',
        'w_gate', 'w_up', 'w_down', 'ln2_g', 'ln2_b']


def kernel(**inputs):
    import numpy as _np
    import concourse.bacc as _bacc
    from concourse import mybir as _mybir
    from concourse.bass_utils import run_bass_kernel_spmd as _run

    nc = _bacc.Bacc("TRN2", target_bir_lowering=False, num_devices=1)
    arrays, args = {}, []
    given = {name: inputs[name] for name in _INS}
    given["onehot"] = bucket_onehot()
    given["headfix"] = head_counts()
    for name, a in given.items():
        a = _np.ascontiguousarray(a)
        arrays[f"in_{name}_dram"] = a
        args.append(nc.dram_tensor(f"in_{name}_dram", a.shape, _mybir.dt.from_np(a.dtype), kind="ExternalInput").ap())
    args.append(nc.dram_tensor("out_0_dram", (1, SEQ, D), _mybir.dt.float32, kind="ExternalOutput").ap())
    layer_kernel(nc, *args)
    r = _run(nc, [arrays], core_ids=[0])
    return r.results[0]["out_0_dram"]
```

```python
import math
from contextlib import ExitStack

import numpy as np

import concourse.bass as bass
from concourse import mybir

F32 = mybir.dt.float32
F32R = mybir.dt.float32r
BF16 = mybir.dt.bfloat16
U32 = mybir.dt.uint32
I32 = mybir.dt.int32
ALU = mybir.AluOpType
ACT = mybir.ActivationFunctionType
AX = mybir.AxisListType

P = 128
SEQ = 512
D = 1024
NT = SEQ // P
KD = D // P
HEADS = 8
HD = 64
AW = HEADS * HD
NA = AW // P
TOPK = min(256, SEQ // 4)
WINDOWS = (2, 4, 8, 16)
PAD = WINDOWS[-1]
BUCKETS = 32
MAX_DIST = 128
Q_OFF, K_OFF, V_OFF, IQ_OFF = 0, AW, 2 * AW, 3 * AW
IK_OFF = IQ_OFF + AW
IW_OFF = IK_OFF + HD
U_OFF = IW_OFF + HEADS
GROUPS = 4
PER_GROUP = 8
NE = GROUPS * PER_GROUP
DE = 256
ME = DE // P
CAP = 64
SLOTS = 6
CHUNKS = 4
KC = 2 * KD // CHUNKS
EPS = 1e-5
ALPHA = 2.0 ** 0.25
BIG = 1e30
NONCAUSAL = -1e38
TAKEN = -3e38
TW = SEQ + P
SCALE = HD ** -0.5


def bucket_onehot():
    n = np.maximum(SEQ - 1 - np.arange(TW), 0)
    half = BUCKETS // 2
    nf = np.maximum(n, 1).astype(np.float32)
    large = half + (np.log(nf / np.float32(half)) / np.float32(math.log(MAX_DIST / half)) * np.float32(BUCKETS - half)).astype(np.int32)
    b = np.where(n < half, n, np.minimum(large, BUCKETS - 1))
    return (b[None, :] == np.arange(BUCKETS)[:, None]).astype(np.float32)


def head_counts():
    t = np.arange(PAD) + 1
    return np.stack([w / np.minimum(t, w) for w in WINDOWS]).astype(np.float32)


def layer_kernel(nc, x, w_in, w_pool, pool_scale, w_out, rel_bias, ln1_g, ln1_b, w_r1, b_r1, w_r2, b_r2,
                 w_gate, w_up, w_down, ln2_g, ln2_b, onehot, headfix, out):
    ctx = ExitStack()
    with ctx:
        base = [(nc.sbuf_base + 63) // 64 * 64]
        KB = 1024
        T_LAG, PV_LAG = 4, 5
        LG = 7
        QKB = 4

        def at(name, offset, shape, dt=F32):
            return nc.alloc_sbuf_tensor_at(name, [P, *shape], dt, offset=base[0] + offset)

        SLOT = 3 * KD * DE * 4
        wg, wu, wd = [], [], []
        for j in range(SLOTS):
            wg.append(at(f"wg{j}", j * SLOT, [KD, DE]))
            wu.append(at(f"wu{j}", j * SLOT + 8 * KB, [KD, DE]))
            wd.append(at(f"wd{j}", j * SLOT + 16 * KB, [ME, D]))
        w_low = [at(f"w_low{j}", j * SLOT, [CHUNKS, KC, DE], F32R) for j in range(SLOTS)]
        o = SLOT
        qT = at("qT", o, [NA, SEQ]); o += 8 * KB
        kT = at("kT", o, [NA, SEQ]); o += 8 * KB
        v_sb = at("v_sb", o, [NT, AW])
        wu_high = [at(f"wu_high{i}", o + 4 * KB * i, [KD, P], F32R) for i in range(2)]
        o += 8 * KB
        bias8 = at("bias8", o, [HEADS, SEQ]); o += 16 * KB
        keep = [None] + [at(f"keep{b}", o + 256 * (b - 1) * (b + 2), [P * (b + 1)]) for b in range(1, NT)]; o += 4608
        wik = at("wik", o, [KD, HD + HEADS])
        wik_low = at("wik_low", o, [KD, HD + HEADS], F32R)
        lg = [at(f"lg{i}", o + 2 * KB * i, [SEQ]) for i in range(3)]; o += 6 * KB
        pT = [at(f"pT{i}", o + 2 * KB * i, [SEQ]) for i in range(2)]; o += 4 * KB
        assert o <= 3 * SLOT + 7 * KB
        iqT = at("iqT", o, [NA, SEQ])
        o += 8 * KB
        uT = at("uT", o, [NA, PAD + SEQ])
        o += NA * (PAD + SEQ) * 4
        assert o <= 4 * SLOT
        RB = KD * AW * 4
        ring = [at(f"ring{i}", 4 * SLOT + RB * i, [KD, AW]) for i in range(3)]
        ring_low = [at(f"ring_low{i}", 4 * SLOT + RB * i, [KD, AW], F32R) for i in range(3)]
        v_high = at("v_high", 4 * SLOT + 2 * RB, [KD, AW], F32R)
        wo = [at("wo0", 4 * SLOT + 2 * RB, [KD // 2, D]), at("wo1", 4 * SLOT, [KD // 2, D])]
        wo_low = [at("wo_low0", 4 * SLOT + 2 * RB, [KD // 2, D], F32R), at("wo_low1", 4 * SLOT, [KD // 2, D], F32R)]
        wo_high_at = [8 * KB, 12 * KB, 16 * KB, 20 * KB, 0, 4 * KB, 4 * SLOT + RB + 8 * KB, 4 * SLOT + RB + 12 * KB]
        wo_high = [at(f"wo_high{k}", wo_high_at[k], [D], F32R) for k in range(KD)]
        g1 = at("g1", 4 * SLOT + RB, [D])
        b1 = at("b1", 4 * SLOT + RB + 4 * KB, [D])
        yg = [[at(f"yg{t}_{c}", (2 * t + c) * 4 * KB, [D]) for c in range(2)] for t in range(NT)]
        res = at("res", 2 * SLOT, [NT, D])
        g2 = at("g2", 3 * SLOT + 16 * KB, [D])
        b2 = at("b2", 3 * SLOT + 20 * KB, [D])
        o_rows = at("o_rows", 6 * SLOT, [NT, D])
        o_rowsT = at("o_rowsT", 3 * SLOT, [KD, SEQ])
        o_sil = at("o_sil", 5 * SLOT, [ME, SEQ])
        o_act = at("o_act", 5 * SLOT + 4 * KB, [ME, SEQ])
        OSLOT = 4
        o = 6 * SLOT
        h = at("h", o, [NT, D])
        mix_low = at("mix_low", o, [NT, KD, P], F32R)
        w_high = at("w_high", o, [CHUNKS, KC, DE], F32R)
        o += 16 * KB
        xT_high = at("xT_high", o, [KD, SEQ], F32R)
        xT_low = at("xT_low", 8 * KB, [KD, SEQ], F32R)
        mix_high = at("mix_high", o, [KD, SEQ], F32R)
        xe = [at(f"xe{i}", o + 4 * KB * i, [D]) for i in range(2)]
        xeT = [at(f"xeT{i}", o + 8 * KB + 4 * KB * i, [KD, 2, CAP], F32R) for i in range(2)]
        o += 16 * KB
        wt_high = [at(f"wt_high{i}", o + 4 * KB * i, [KD, P], F32R) for i in range(2)]
        ptmp = [at(f"ptmp{i}", o + 2176 * i, [PAD + SEQ]) for i in range(2)]
        lg += [at(f"lg{3 + i}", o + 2 * KB * i, [SEQ]) for i in range(4)]
        hT = [at(f"hT{i}", o + 4 * KB * i, [KD, P]) for i in range(2)]
        ye = [at(f"ye{i}", o + 4 * KB * i, [D]) for i in range(2)]
        o += 8 * KB
        ikT = at("ikT", o, [SEQ])
        score = at("score", o + 2 * KB, [SEQ])
        relu = [at(f"relu{i}", o + 4 * KB + 2 * KB * i, [SEQ]) for i in range(4)]
        bm = [at(f"bm{i}", o + 4 * KB + 2 * KB * i, [SEQ]) for i in range(4)]
        x_again = [[at("x_again0_0", o, [D // 2]), at("x_again0_1", o + 2 * KB, [D // 2])],
                   [at("x_again1_0", o + 4 * KB, [D // 2]), at("x_again1_1", o + 10 * KB, [D // 2])]]
        gu_sb = at("gu_sb", o, [2 * DE])
        act_e = [at(f"act_e{i}", o + 4 * KB + 512 * i, [ME, CAP]) for i in range(2)]
        sil = [at(f"sil{i}", o + 5 * KB + 512 * i, [ME, CAP]) for i in range(2)]
        hot_tok = at("hot_tok", o + 6 * KB, [NT, 2, NE])
        hot_rank = at("hot_rank", o + 7 * KB, [NT, 2, NE])
        at_rank = at("at_rank", o + 8 * KB, [NT, 2, CAP])
        iwT = at("iwT", o + 10 * KB, [SEQ])
        o += 12 * KB
        cursor = [o]

        def small(name, shape, dt=F32):
            n = int(np.prod(shape)) * (2 if dt == BF16 else 4)
            t = at(name, cursor[0], shape, dt)
            cursor[0] += (n + 31) // 32 * 32
            return t

        ident = small("ident", [P])
        tri = small("tri", [P])
        ones = small("ones", [P])
        iw = small("iw", [NT, HEADS])
        wpool = small("wpool", [NA, P])
        pscale = small("pscale", [NA])
        relb = small("relb", [HEADS])
        hfix = small("hfix", [NA, PAD])
        gT = small("gT", [KD])
        bT = small("bT", [KD])
        wr = small("wr", [KD, GROUPS + NE])
        br = small("br", [GROUPS + NE])
        m8 = small("m8", [8])
        nmx = small("nmx", [8])
        rsum = small("rsum", [8])
        rinv = small("rinv", [8])
        probe = small("probe", [1])
        stats = small("stats", [2, 6])
        mv = small("mv", [2])
        var_e = small("var_e", [1])
        std = small("std", [1])
        rstd = small("rstd", [1])
        nmr = small("nmr", [1])
        iota_e = small("iota_e", [NE])
        fold = small("fold", [CAP])
        gid = small("gid", [GROUPS, PER_GROUP])
        iota_r = small("iota_r", [CAP])
        gl = small("gl", [NT, 8])
        lf = small("lf", [NE])
        gm8 = small("gm8", [8])
        gi8 = small("gi8", [8], U32)
        gidx = small("gidx", [1])
        em8 = small("em8", [NT, 8])
        ei8 = small("ei8", [8], U32)
        eidx = small("eidx", [NT, 2])
        tok = small("tok", [NT])
        lsti = small("lsti", [NE], U32)
        cur = [small(f"cur{i}", [1], U32) for i in range(2)]
        rk = small("rk", [NT, 2])
        fits = small("fits", [NT, 2])
        wfit = small("wfit", [NT, 2])
        over = small("over", [NT, NE])
        over_e = small("over_e", [NT])
        pen = small("pen", [NE])
        hot = small("hot", [NT, 2, NE])
        hsum = small("hsum", [NT, NE])
        earlier = small("earlier", [NT + 1, NE])
        neg = small("neg", [NT, 2])
        zs = small("zs", [NT, 2])
        ex = small("ex", [NT, 4])
        wt = small("wt", [NT, 2])
        rank1 = small("rank1", [NT, NE])
        slotf = small("slotf", [NT, 2])
        sloti = small("sloti", [NT, 2], U32)
        scr = small("scr", [NE])
        mosti = small("mosti", [1], I32)
        brow = at("brow", 0, [TW])
        hot_c = at("hot_c", 4 * KB, [TW])
        assert base[0] + cursor[0] <= nc.sbuf_usable_end, (base[0] + cursor[0], nc.sbuf_usable_end)

        bank = [ctx.enter_context(nc.psum_tensor(f"bank{i}", [P, 512], F32)) for i in range(8)]

        y_dram = nc.dram_tensor("y_rows", (NE * CAP, D), F32, kind="Internal").ap()
        h_dram = nc.dram_tensor("h_rows", (SEQ, D), F32, kind="Internal").ap()
        row_dram = nc.dram_tensor("bias_rows", (P, HEADS, TW), F32, kind="Internal")

        def sem(name):
            return ctx.enter_context(nc.semaphore(name))

        x_in = [sem(f"x_in{t}") for t in range(NT)]
        x_again_in = [sem(f"x_again_in{i}") for i in range(2)]
        group_in = [sem(f"group_in{i}") for i in range(3)]
        wo_in = [sem(f"wo_in{i}") for i in range(2)]
        wo_high_ready = sem("wo_high_ready")
        wo_low_dve = sem("wo_low_dve")
        wo_low_pool = sem("wo_low_pool")
        ln1_in = sem("ln1_in")
        ln2_in = sem("ln2_in")
        wik_in = sem("wik_in")
        small_in = sem("small_in")
        onehot_in = sem("onehot_in")
        consts_ready = sem("consts_ready")
        pool_chain = sem("pool_chain")
        dve_chain = sem("dve_chain")
        act_chain = sem("act_chain")
        xT_ps = sem("xT_ps")
        xT_high_ready = sem("xT_high_ready")
        xT_low_ready = sem("xT_low_ready")
        wt_high_ready = sem("wt_high_ready")
        wt_low_ready = sem("wt_low_ready")
        v_high_ready = sem("v_high_ready")
        v_low_ready = sem("v_low_ready")
        row_ps = sem("row_ps")
        row_ready = sem("row_ready")
        row_out = sem("row_out")
        bias_in = sem("bias_in")
        bias_ready = sem("bias_ready")
        proj_ps = sem("proj_ps")
        proj_sb = sem("proj_sb")
        iwT_ready = sem("iwT_ready")
        iw_ps = sem("iw_ps")
        iw_ready = sem("iw_ready")
        dots_ps = sem("dots_ps")
        relu_ready = sem("relu_ready")
        relu_used = sem("relu_used")
        score_sum = sem("score_sum")
        score_masked = sem("score_masked")
        keep_ready = sem("keep_ready")
        pooled_ready = sem("pooled_ready")
        mixed_ps = sem("mixed_ps")
        mixed_high = sem("mixed_high")
        mixed_sb = sem("mixed_sb")
        qk_ps = sem("qk_ps")
        bm_ready = sem("bm_ready")
        logit_ready = sem("logit_ready")
        exp_ready = sem("exp_ready")
        rinv_ready = sem("rinv_ready")
        prob_ready = sem("prob_ready")
        pT_ps = sem("pT_ps")
        pT_ready = sem("pT_ready")
        pv_ps = sem("pv_ps")
        attn_high = sem("attn_high")
        attn_sb = sem("attn_sb")
        out_ps = sem("out_ps")
        res_ready = sem("res_ready")
        var_ready = sem("var_ready")
        std_ready = sem("std_ready")
        scale_ready = sem("scale_ready")
        norm_ready = sem("norm_ready")
        gain_ready = sem("gain_ready")
        h_stored = sem("h_stored")
        res_in = sem("res_in")
        res_sum = sem("res_sum")
        h_ready = sem("h_ready")
        out_ready = sem("out_ready")
        hT_ps = sem("hT_ps")
        hT_ready = sem("hT_ready")
        hT_ready_dve = sem("hT_ready_dve")
        router_ps = sem("router_ps")
        router_sb = sem("router_sb")
        top_ready = sem("top_ready")
        gate_exp = sem("gate_exp")
        hot_ready = sem("hot_ready")
        earlier_ready = sem("earlier_ready")
        rank_ps = sem("rank_ps")
        hot_tok_ready = sem("hot_tok_ready")
        rank1_ready = sem("rank1_ready")
        at_rank_ready = sem("at_rank_ready")
        list_ps = sem("list_ps")
        list_ready = sem("list_ready")
        cur_ready = sem("cur_ready")
        gather_begun = sem("gather_begun")
        rows_begun = sem("rows_begun")
        gathered = [sem(f"gathered{i}") for i in range(2)]
        slot_ready = sem("slot_ready")
        gu_in_slot = [sem(f"gu_in_slot{j}") for j in range(SLOTS)]
        down_in_slot = [sem(f"down_in_slot{j}") for j in range(SLOTS)]
        xeT_ps = sem("xeT_ps")
        xe_high = sem("xe_high")
        xe_low = sem("xe_low")
        w_high_ready = sem("w_high_ready")
        w_low_ready = sem("w_low_ready")
        piece_done = sem("piece_done")
        gu_out = sem("gu_out")
        gu_ps = sem("gu_ps")
        silu_ready = sem("silu_ready")
        act_ready = sem("act_ready")
        y_ps = sem("y_ps")
        y_lo = sem("y_lo")
        y_hi = sem("y_hi")
        y_stored = [sem(f"y_stored{i}") for i in range(2)]
        y_gathered = [sem(f"y_gathered{t}") for t in range(NT)]
        out_stored = sem("out_stored")
        count_ps = sem("count_ps")
        count_ready = sem("count_ready")
        o_rows_in = sem("o_rows_in")
        o_rowsT_ps = sem("o_rowsT_ps")
        o_rowsT_ready = sem("o_rowsT_ready")
        o_w_in = sem("o_w_in")
        o_gu_ps = sem("o_gu_ps")
        o_silu_ready = sem("o_silu_ready")
        o_act_ready = sem("o_act_ready")
        o_weight_ready = sem("o_weight_ready")
        o_y_ps = sem("o_y_ps")
        o_added = sem("o_added")
        o_chain = sem("o_chain")

        group_cols = [IQ_OFF, Q_OFF, K_OFF, U_OFF, V_OFF]
        IQ, Q, K, U, V = range(5)
        ring_of = [0, 1, 2, 0, 1]
        tiles = [("ik", 0)] + [(g, m) for g in (IQ, Q, K, U, V) for m in range(NA)]
        units_in = {5: (1, 0, 3), 6: (1, 3, 6), 7: (1, 6, 8), 10: (2, 0, 3), 11: (2, 3, 6), 12: (2, 6, 8), 15: (3, 0, 3), 16: (3, 3, 6), 17: (3, 6, 8)}
        front = []
        LATE = len(tiles) - 2
        for i in range(LATE):
            if i == 5:
                front.append(("iw",))
            if i in units_in:
                b, j0, j1 = units_in[i]
                front += [("score", b, j) for j in range(j0, j1)]
            front.append(("tile", i))
        tile_no = {t: i for i, t in enumerate(tiles)}
        score_no = {(b, j): (b - 1) * HEADS + j for b in range(1, NT) for j in range(HEADS)}
        units = [(b, hh) for b in range(NT) for hh in range(HEADS)]
        NU = len(units)

        def keys(b):
            return P * (b + 1)

        def piece(j, c):
            return (wg, wu)[c * KC // KD][j][:, c * KC % KD:c * KC % KD + KC, :]

        def tile_parts(i):
            kind, m = tiles[i]
            if kind == "ik":
                return wik[:, :, :], wt_high[0][:, :, 0:HD + HEADS], wik_low[:, :, :]
            cols = slice(P * m, P * m + P)
            return (ring[ring_of[kind]][:, :, cols], (wu_high if kind == U else wt_high)[i % 2][:, :, :],
                    ring_low[ring_of[kind]][:, :, cols])

        FIRST_SPLIT = 16
        mixes = [8, 10, 12, 14]

        def split_of_wo(u):
            c = u // 2 - FIRST_SPLIT // 2
            return None if u % 2 or not 0 <= c < KD else (c // 2, slice(D // 2 * (c % 2), D // 2 * (c % 2) + D // 2))

        def qk_bank(u):
            return u % 2 if u < 20 else u % QKB

        EARLY_ROUNDS = 4
        FIRST_V = tile_no[(V, 0)]

        def half(hh):
            return slice(HD * (hh % 2), HD * (hh % 2) + HD)

        SMALLS = 8 + NA

        block = ctx.enter_context(nc.Block())

        @block.sync
        def _(sp):
            win = w_in[0].rearrange("(k p) n -> p k n", p=P)
            xv = x[0].rearrange("(t p) d -> t p d", p=P)
            for t in range(NT):
                sp.dma_start(h[:, t, :], xv[t]).then_inc(x_in[t], 16)
                if t == 0:
                    sp.dma_start(wik[:, :, :], win[:, :, IK_OFF:U_OFF]).then_inc(wik_in, 16)
            for g in range(3):
                sp.dma_start(ring[ring_of[g]][:, :, :], win[:, :, group_cols[g]:group_cols[g] + AW]).then_inc(group_in[ring_of[g]], 16)
            sp.wait_ge(row_ready, 2)
            sp.dma_start(row_dram.ap().rearrange("c h j -> h c j"), brow[0:HEADS, :].unsqueeze(1).to_broadcast([HEADS, P, TW])).then_inc(row_out, 16)
            sp.wait_ge(row_out, 16)
            sp.dma_start(bias8[:, :, :], bass.AP(row_dram, P - 1, [[HEADS * TW - 1, P], [TW, HEADS], [1, SEQ]])).then_inc(bias_in, 16)
            sp.dma_start(wpool[:, :, :], w_pool[0].rearrange("g c d -> c g d")).then_inc(small_in, 16)
            with nc.allow_non_contiguous_dma(reason="2560 elements in all"):
                sp.dma_start(gT[:, :], ln1_g[0].rearrange("(k p) -> p k", p=P)).then_inc(small_in, 16)
                sp.dma_start(bT[:, :], ln1_b[0].rearrange("(k p) -> p k", p=P)).then_inc(small_in, 16)
                sp.dma_start(pscale[:, :], pool_scale[0].rearrange("(g p) -> p g", p=P)).then_inc(small_in, 16)
            for g in range(NA):
                sp.dma_start(hfix[:, g, :], headfix[g].partition_broadcast(P)).then_inc(small_in, 16)
            sp.dma_start(wr[:, :, 0:GROUPS], w_r1[0].rearrange("(k p) n -> p k n", p=P)).then_inc(small_in, 16)
            sp.dma_start(wr[:, :, GROUPS:], w_r2[0].rearrange("(k p) n -> p k n", p=P)).then_inc(small_in, 16)
            sp.dma_start(br[:, 0:GROUPS], b_r1[0].partition_broadcast(P)).then_inc(small_in, 16)
            sp.dma_start(br[:, GROUPS:], b_r2[0].partition_broadcast(P)).then_inc(small_in, 16)
            for g in range(3, 5):
                sp.wait_ge(proj_ps, tile_no[(g - 3, NA - 1)] + 1)
                sp.dma_start(ring[ring_of[g]][:, :, :], win[:, :, group_cols[g]:group_cols[g] + AW]).then_inc(group_in[ring_of[g]], 16)
            wov = w_out[0].rearrange("(k p) n -> p k n", p=P)
            sp.wait_ge(proj_ps, tile_no[(U, NA - 1)] + 1)
            sp.dma_start(wo[1][:, :, :], wov[:, KD // 2:KD, :]).then_inc(wo_in[1], 16)
            sp.wait_ge(proj_ps, tile_no[(V, NA - 1)] + 1)
            sp.dma_start(wo[0][:, :, :], wov[:, 0:KD // 2, :]).then_inc(wo_in[0], 16)
            sp.dma_start(g1[:, :], ln1_g[0].partition_broadcast(P)).then_inc(ln1_in, 16)
            sp.dma_start(b1[:, :], ln1_b[0].partition_broadcast(P)).then_inc(ln1_in, 16)

            def load_gate_up(e, j, loaded):
                for dst, src in ((wg[j][:, :, :], w_gate), (wu[j][:, :, :], w_up)):
                    sp.dma_start(dst, src[0, bass.ds(e, 1), :, :].rearrange("o (p k) f -> p (o k) f", p=P)).then_inc(loaded, 16)

            def load_down(e, j, loaded):
                sp.dma_start(wd[j][:, :, :], w_down[0, bass.ds(e, 1), :, :].rearrange("o (m p) n -> p (o m) n", p=P)).then_inc(loaded, 16)

            def load_expert(e, j):
                load_gate_up(e, j, gu_in_slot[j])
                load_down(e, j, down_in_slot[j])

            sp.wait_ge(attn_sb, NT)

            def load_x_again(t):
                for i in range(2):
                    sp.dma_start(x_again[t % 2][i][:, :], xv[t][:, D // 2 * i:D // 2 * (i + 1)]).then_inc(x_again_in[t % 2], 16)

            load_x_again(0)
            load_x_again(1)
            for j in (1, 2, 3):
                load_expert(j, j)

            def store_h(t):
                sp.wait_ge(h_ready, t + 1)
                sp.dma_start(h_dram[P * t:P * t + P, :], h[:, t, :]).then_inc(h_stored, 16)

            for t in range(2):
                sp.wait_ge(res_ready, t + 1)
                load_x_again(t + 2)
                store_h(t)
            sp.wait_ge(out_ps, NT)
            load_expert(0, 0)
            store_h(2)
            load_gate_up(4, 4, gu_in_slot[4])
            store_h(3)
            load_down(4, 4, down_in_slot[4])
            sp.wait_ge(gathered[1], 16)
            load_expert(5, 5)

            def next_gate_up(e, j):
                sp.wait_ge(piece_done, CHUNKS * e + CHUNKS)
                load_gate_up(e + SLOTS, j, gu_in_slot[j])

            def next_down(e, j):
                sp.wait_ge(y_ps, e + 1)
                load_down(e + SLOTS, j, down_in_slot[j])

            next_gate_up(0, 0)
            with sp.Fori(0, NE // SLOTS - 1) as g:
                for j in range(SLOTS):
                    next_gate_up(g * SLOTS + j + 1, (j + 1) % SLOTS)
                    next_down(g * SLOTS + j, j)
            for e in range(NE // SLOTS * SLOTS - SLOTS, NE - SLOTS):
                if e + 1 < NE - SLOTS:
                    next_gate_up(e + 1, (e + 1) % SLOTS)
                next_down(e, e % SLOTS)
            sp.wait_ge(y_ps, NE - NE % SLOTS - SLOTS + 4)
            sp.dma_start(res[:, :, :], h_dram.rearrange("(t p) d -> p t d", p=P)).then_inc(res_in, 16)
            sp.dma_start(g2[:, :], ln2_g[0].partition_broadcast(P)).then_inc(ln2_in, 16)
            sp.dma_start(b2[:, :], ln2_b[0].partition_broadcast(P)).then_inc(ln2_in, 16)
            sp.wait_ge(y_ps, NE)
            sp.wait_ge(count_ready, 1)
            with sp.If(sp.value_load(mosti[0:1, 0:1], min_val=0, max_val=SEQ) > CAP):
                sp.dma_start(o_rows[:, :, :], h_dram.rearrange("(t p) d -> p t d", p=P)).then_inc(o_rows_in, 16)
                with sp.Fori(0, NE) as e:
                    sp.wait_ge(o_y_ps, e * NT + 1)
                    load_gate_up(e, OSLOT, o_w_in)
                    load_down(e, OSLOT, o_w_in)
            ov = out[0].rearrange("(t p) d -> t p d", p=P)
            for t in range(NT):
                sp.wait_ge(out_ready, 2 * t + 2)
                sp.dma_start(ov[t], res[:, t, :]).then_inc(out_stored, 16)
            sp.wait_ge(out_stored, 16 * NT)

        @block.gpsimd
        def _(pool):
            n = [0]

            def link(ins):
                n[0] += 1
                ins.then_inc(pool_chain, 1)
                pool.wait_ge(pool_chain, n[0])

            link(pool.memset(ident[:, :], 0.0))
            link(pool.affine_select(out=ident[:, :], in_=ident[:, :], compare_op=ALU.not_equal, fill=1.0, base=0,
                                    pattern=[[-1, P]], channel_multiplier=1))
            pool.memset(ones[:, :], 1.0).then_inc(consts_ready, 1)
            link(pool.memset(tri[:, :], 1.0))
            link(pool.affine_select(out=tri[:, :], in_=tri[:, :], compare_op=ALU.is_gt, fill=0.0, base=0,
                                    pattern=[[1, P]], channel_multiplier=-1))
            link(pool.memset(uT[:, :, 0:PAD], 0.0))
            link(pool.memset(gl[:, :, :], -BIG))
            link(pool.memset(earlier[:, 0, :], 0.0))
            for t, pat, b0, cm in ((iota_e, [[1, NE]], 0, 0), (iota_r, [[1, CAP]], 1, 0)):
                link(pool.iota(t[:, :], pattern=pat, base=b0, channel_multiplier=cm, allow_small_or_imprecise_dtypes=True))
            link(pool.iota(gid[:, :, :], pattern=[[1, GROUPS], [0, PER_GROUP]], base=0, channel_multiplier=0,
                           allow_small_or_imprecise_dtypes=True))
            link(pool.memset(fold[:, :], 0.0))
            for first_row in (0, CAP):
                link(pool.affine_select(out=fold[:, :], in_=fold[:, :], compare_op=ALU.not_equal, fill=1.0, base=-first_row,
                                        pattern=[[-1, CAP]], channel_multiplier=1))
            pool.iota(tok[:, :], pattern=[[P, NT]], base=0, channel_multiplier=1,
                      allow_small_or_imprecise_dtypes=True).then_inc(consts_ready, 1)

            def tile_low(i):
                if i < FIRST_V:
                    raw, high, low = tile_parts(i)
                    pool.wait_ge(wt_high_ready, i + 1)
                    pool.tensor_tensor(low, raw, high.bitcast(F32), ALU.subtract).then_inc(wt_low_ready, 1)

            def mix_group(g):
                w = WINDOWS[g]
                if g == 0:
                    pool.wait_ge(small_in, 16 * SMALLS)
                    pool.wait_ge(proj_ps, tile_no[(U, 0)])
                    link(pool.memset(ptmp[0][:, 0:PAD], 0.0))
                    link(pool.memset(ptmp[1][:, 0:PAD], 0.0))
                pool.wait_ge(proj_sb, tile_no[(U, g)] + 1)
                src, step, i = uT[:, g, :], 1, 0
                while step < w:
                    dst = ptmp[i]
                    link(pool.tensor_tensor(dst[:, PAD:], src[:, PAD:], src[:, PAD - step:PAD + SEQ - step], ALU.add))
                    src, step, i = dst, 2 * step, 1 - i
                link(pool.tensor_scalar(src[:, PAD:], src[:, PAD:], 1.0 / w, 1.0, ALU.mult, ALU.mult))
                link(pool.tensor_tensor(src[:, PAD:PAD + PAD], src[:, PAD:PAD + PAD], hfix[:, g, :], ALU.mult))
                link(pool.tensor_tensor(uT[:, g, PAD:], src[:, PAD:], uT[:, g, PAD:], ALU.subtract))
                pool.sem_inc(pooled_ready, 1)

            tile_low(0)
            tile_low(1)
            for item in front:
                if item[0] == "tile":
                    tile_low(item[1] + 2)
                    g = item[1] - tile_no[(U, 1)]
                    if 0 <= g < NA - 1:
                        mix_group(g)
                elif item[0] == "score" and item[2] == HEADS - 1:
                    b = item[1]
                    pool.wait_ge(score_sum, b)
                    d = score[:, P * b:P * b + P]
                    pool.affine_select(out=d, in_=d, compare_op=ALU.is_ge, fill=NONCAUSAL, base=0, pattern=[[-1, P]],
                                       channel_multiplier=1).then_inc(score_masked, 1)
                    if b == 1:
                        pool.wait_ge(bias_in, 16)
                        for hh in range(HEADS):
                            pool.affine_select(out=bias8[:, hh, :], in_=bias8[:, hh, :], compare_op=ALU.is_ge, fill=-BIG, base=SEQ - P,
                                               pattern=[[-1, SEQ]], channel_multiplier=1).then_inc(bias_ready, 1)
            mix_group(NA - 1)

            def bias_mask(u):
                b, hh = units[u]
                if b == 0 or hh % 2:
                    return
                pool.wait_ge(keep_ready, b)
                if u < HEADS + 4:
                    pool.wait_ge(relu_used, len(score_no))
                else:
                    pool.wait_ge(logit_ready, u - 3)
                pool.tensor_tensor(bm[u % 4][:, 0:keys(b)], bias8[:, hh, SEQ - keys(b):], keep[b][:, :], ALU.add).then_inc(bm_ready, 1)

            pool.wait_ge(bias_ready, HEADS)
            for u in range(NU):
                b, hh = units[u]
                if u + 3 < NU:
                    bias_mask(u + 3)
                pool.wait_ge(rinv_ready, u + 1)
                p = lg[u % LG][:, 0:keys(b)]
                pool.tensor_scalar(p, p, rinv[:, u % 8:u % 8 + 1], 1.0, ALU.mult, ALU.mult).then_inc(prob_ready, 1)
                if split_of_wo(u) and u % 4:
                    k, cols = split_of_wo(u)
                    pool.wait_ge(wo_high_ready, KD // 2 + u // 2 - FIRST_SPLIT // 2 + 1)
                    pool.tensor_tensor(wo_low[0][:, k, cols], wo[0][:, k, cols], wo_high[k][:, cols].bitcast(F32),
                                       ALU.subtract).then_inc(wo_low_pool, 1)

            pool.wait_ge(ln1_in, 32)
            for t in range(NT):
                pool.wait_ge(norm_ready, t + 1)
                pool.wait_ge(hT_ps, t + 1)
                link(pool.tensor_tensor(h[:, t, :], h[:, t, :], g1[:, :], ALU.mult))
                pool.tensor_tensor(h[:, t, :], h[:, t, :], b1[:, :], ALU.add).then_inc(h_ready, 1)

            pool.wait_ge(list_ready, 1)
            pool.wait_ge(h_stored, 16 * NT)
            pool.wait_ge(out_ps, NT)

            def gather(e, j, first):
                i = j % 2
                if not first:
                    pool.wait_ge(xeT_ps, e - 1)
                k = pool.tensor_copy(cur[i][0:CAP, :], lsti[0:CAP, bass.ds(e, 1)])
                k.then_inc(cur_ready, 1)
                pool.wait_ge(cur_ready, e - 1)
                pool.sem_inc(gather_begun, 1)
                pool.indirect_dma_start(out=xe[i][0:CAP, :], out_offset=None, in_=h_dram,
                                        in_offset=bass.IndirectOffsetOnAxis(ap=cur[i][0:CAP, :], axis=0),
                                        ).then_inc(gathered[i], 16)

            for e in range(2):
                pool.indirect_dma_start(out=xe[e][0:CAP, :], out_offset=None, in_=h_dram,
                                        in_offset=bass.IndirectOffsetOnAxis(ap=lsti[0:CAP, e:e + 1], axis=0),
                                        ).then_inc(gathered[e], 16)
            for e in range(2, SLOTS):
                gather(e, e, False)
            with pool.Fori(1, NE // SLOTS) as g:
                for j in range(SLOTS):
                    gather(g * SLOTS + j, j, False)
            for e in range(NE // SLOTS * SLOTS, NE):
                gather(e, e % SLOTS, False)
            pool.wait_ge(res_in, 16)
            for t in range(NT):
                pool.tensor_scalar(res[:, t, :], res[:, t, :], ALPHA, 1.0, ALU.mult, ALU.mult).then_inc(res_sum, 1)

            pool.wait_ge(slot_ready, 1)
            for i in range(2):
                pool.wait_ge(y_stored[i], 16 * NE // 2)
            pool.wait_ge(y_ps, NE)
            for t in range(NT):
                for c in range(2):
                    pool.indirect_dma_start(out=yg[t][c][:, :], out_offset=None, in_=y_dram,
                                            in_offset=bass.IndirectOffsetOnAxis(ap=sloti[:, t, c:c + 1], axis=0),
                                            ).then_inc(y_gathered[t], 16)
            pool.wait_ge(ln2_in, 32)
            for t in range(NT):
                if t < NT - 1:
                    pool.wait_ge(norm_ready, NT + t + 1)
                    link(pool.tensor_tensor(res[:, t, :], res[:, t, :], g2[:, :], ALU.mult))
                    pool.tensor_tensor(res[:, t, :], res[:, t, :], b2[:, :], ALU.add).then_inc(out_ready, 2)
                else:
                    pool.wait_ge(gain_ready, 1)
                    pool.tensor_tensor(res[:, t, D // 2:], res[:, t, D // 2:], b2[:, D // 2:], ALU.add).then_inc(out_ready, 1)

        @block.scalar
        def _(act):
            act.dma_start(relb[0:BUCKETS, :], rel_bias).then_inc(onehot_in, 16)
            act.dma_start(hot_c[0:BUCKETS, :], onehot).then_inc(onehot_in, 16)
            def tile_high(i):
                if i < FIRST_V:
                    kind, m = tiles[i]
                    raw, high, low = tile_parts(i)
                    if kind == "ik":
                        act.wait_ge(wik_in, 16)
                    elif m == 0:
                        act.wait_ge(group_in[ring_of[kind]], 16 * (kind // 3 + 1))
                    act.activation(high, raw, ACT.Copy).then_inc(wt_high_ready, 1)

            tile_high(0)
            for g in range(2 * NT):
                act.wait_ge(xT_ps, g + 1)
                k0 = 4 * (g % 2)
                act.activation(xT_high[:, k0:k0 + 4, P * (g // 2):P * (g // 2) + P], bank[g % 2][:, :].rearrange("p (k t) -> p k t", k=4),
                               ACT.Copy).then_inc(xT_high_ready, 1)
            tile_high(1)
            for item in front:
                if item[0] == "tile":
                    i = item[1]
                    kind, m = tiles[i]
                    act.wait_ge(proj_ps, i + 1)
                    if kind == "ik":
                        act.activation(ikT[0:HD, :], bank[2][0:HD, :], ACT.Copy)
                        act.activation(ikT[HD:P, :], bank[2][0:HD, :], ACT.Copy)
                        act.activation(iwT[0:HEADS, :], bank[2][HD:HD + HEADS, :], ACT.Copy).then_inc(proj_sb, 1)
                        tile_high(2)
                        continue
                    dst = {IQ: iqT[:, m, :], Q: qT[:, m, :], K: kT[:, m, :],
                           U: uT[:, m, PAD:], V: v_sb[:, m, :]}[kind]
                    act.activation(dst, bank[2 + i % 2][:, :], ACT.Copy).then_inc(proj_sb, 1)
                    tile_high(i + 2)
                    if (kind, m) == (V, 1):
                        act.wait_ge(wo_in[1], 16)
                        act.wait_ge(row_out, 16)
                        for k in range(KD // 2, KD - 2):
                            act.activation(wo_high[k][:, :], wo[1][:, k - KD // 2, :], ACT.Copy).then_inc(wo_high_ready, 1)
                    if (kind, m) == (K, NA - 1):
                        act.wait_ge(group_in[ring_of[V]], 32)
                        for c in range(4):
                            act.activation(v_high[:, 2 * c:2 * c + 2, :], ring[ring_of[V]][:, 2 * c:2 * c + 2, :], ACT.Copy).then_inc(v_high_ready, 1)
                elif item[0] == "score":
                    _, b, j = item
                    s = score_no[(b, j)]
                    act.wait_ge(dots_ps, s + 1)
                    if s >= 4:
                        act.wait_ge(relu_used, s - 3)
                    act.activation(relu[s % 4][:, 0:keys(b)], bank[5 + s % 2][:, 0:keys(b)], ACT.Relu, scale=SCALE).then_inc(relu_ready, 1)
            for u in range(NU + PV_LAG):
                if 0 <= u - T_LAG < NU:
                    w = u - T_LAG
                    b, hh = units[w]
                    act.wait_ge(pT_ps, w + 1)
                    if w >= 2:
                        act.wait_ge(pv_ps, w - 1)
                    act.activation(pT[w % 2][:, 0:keys(b)], bank[4 + w % 2][:, 0:keys(b)], ACT.Copy).then_inc(pT_ready, 1)
                if u < NU:
                    b, hh = units[u]
                    act.wait_ge(logit_ready, u + 1)
                    p = lg[u % LG][:, 0:keys(b)]
                    if u >= 8:
                        act.wait_ge(rinv_ready, u - 7)
                    act.activation(p, p, ACT.Exp, bias=nmx[:, u % 8:u % 8 + 1], scale=-1.0,
                                   accum_out=rsum[:, u % 8:u % 8 + 1]).then_inc(exp_ready, 1)
                if u >= PV_LAG and units[u - PV_LAG][1] == HEADS - 1:
                    b = units[u - PV_LAG][0]
                    act.wait_ge(pv_ps, u - PV_LAG + 1)
                    act.activation(mix_high[:, 0:NA, P * b:P * b + P], bank[6 + b % 2][:, :].rearrange("p (m t) -> p m t", m=NA),
                                   ACT.Copy).then_inc(attn_high, 1)
                if u in (4, 8):
                    i = LATE + u // 4 - 1
                    act.wait_ge(proj_ps, i + 1)
                    act.activation(v_sb[:, tiles[i][1], :], bank[2 + i % 2][:, :], ACT.Copy).then_inc(proj_sb, 1)
                if u - 1 in mixes:
                    g = mixes.index(u - 1)
                    act.wait_ge(mixed_ps, g + 1)
                    act.activation(mix_high[:, NA + g, :], bank[3 - g % 2][:, :], ACT.Copy, scale=pscale[:, g:g + 1]).then_inc(mixed_high, 1)
                if u in (9, 11):
                    k = KD - 2 + (u - 9) // 2
                    act.activation(wo_high[k][:, :], wo[1][:, k - KD // 2, :], ACT.Copy).then_inc(wo_high_ready, 1)
                if split_of_wo(u):
                    k, cols = split_of_wo(u)
                    act.wait_ge(wo_in[0], 16)
                    act.activation(wo_high[k][:, cols], wo[0][:, k, cols], ACT.Copy).then_inc(wo_high_ready, 1)

            def normalise(t, k, rows):
                act.wait_ge(var_ready, k + 1)
                act.activation(std[:, :], var_e[:, :], ACT.Sqrt).then_inc(std_ready, 1)
                act.wait_ge(scale_ready, k + 1)
                act.activation(rows, rows, ACT.Identity, bias=nmr[:, 0:1], scale=rstd[:, 0:1]).then_inc(norm_ready, 1)

            def transposed_h(t):
                act.wait_ge(hT_ps, t + 1)
                if t >= 2:
                    act.wait_ge(router_ps, t - 1)
                for k in range(KD // 2):
                    ins = act.activation(hT[t % 2][:, k, :], bank[4][:, P * k:P * k + P], ACT.Identity,
                                         bias=bT[:, k:k + 1], scale=gT[:, k:k + 1])
                ins.then_inc(hT_ready, 1)

            for t in range(NT):
                if t >= 1:
                    transposed_h(t - 1)
                normalise(t, t, h[:, t, :])
            transposed_h(NT - 1)
            def rows_high(e, j, first):
                i = j % 2
                act.wait_ge(xeT_ps, e + 1)
                if not first:
                    act.wait_ge(piece_done, CHUNKS * e - CHUNKS)
                act.activation(xeT[i][:, :, 0, :], bank[0][:, 0:KD * CAP].rearrange("p (k t) -> p k t", k=KD), ACT.Copy).then_inc(xe_high, 1)

            def weights_high(e, j, first, turn, pieces):
                act.wait_ge(gu_in_slot[j], turn * 32 + 32)
                for c in pieces:
                    if not first:
                        act.wait_ge(piece_done, CHUNKS * e - CHUNKS + c + 1)
                    act.activation(w_high[:, c, :, :], piece(j, c), ACT.Copy).then_inc(w_high_ready, 1)

            def gate_up_out(e, first):
                act.wait_ge(piece_done, CHUNKS * e + CHUNKS)
                if not first:
                    act.wait_ge(gu_ps, e)
                act.activation(gu_sb[0:2 * CAP, :], bank[1][0:2 * CAP, :], ACT.Copy).then_inc(gu_out, 1)

            def silu(e, j, first):
                i = j % 2
                act.wait_ge(gu_ps, e + 1)
                if not first:
                    act.wait_ge(act_ready, e - 1)
                act.activation(sil[i][:, :, :], bank[2][:, 0:ME * CAP].rearrange("p (m t) -> p m t", m=ME), ACT.Silu).then_inc(silu_ready, 1)

            def y_out(e, j, first, occurrence):
                i = j % 2
                act.wait_ge(y_ps, e + 1)
                if not first:
                    act.wait_ge(y_stored[i], occurrence * 16)
                act.activation(ye[i][0:CAP, 512:], bank[5 + 2 * i][0:CAP, :], ACT.Copy).then_inc(y_hi, 1)
                act.wait_ge(y_hi, e + 1)
                act.wait_ge(y_lo, e + 1)
                act.dma_start(y_dram[bass.ds(e * CAP, CAP), :], ye[i][0:CAP, :]).then_inc(y_stored[i], 16)

            for t in range(NT):
                act.wait_ge(top_ready, t + 1)
                act.activation(ex[:, t, :], gl[:, t, 0:GROUPS], ACT.Exp, bias=neg[:, t, 0:1], accum_out=zs[:, t, 0:1])
                act.activation(zs[:, t, 1:2], em8[:, t, 1:2], ACT.Exp, bias=neg[:, t, 1:2]).then_inc(gate_exp, 1)

            act.activation(probe[:, :], ones[:, 0:1], ACT.Silu)

            act.wait_ge(h_stored, 16 * NT)
            act.wait_ge(hT_ps, NT)
            weights_high(0, 0, True, 0, range(CHUNKS))
            rows_high(0, 0, True)
            rows_high(1, 1, True)
            weights_high(1, 1, False, 0, range(CHUNKS - 1))
            gate_up_out(0, True)
            weights_high(1, 1, False, 0, (CHUNKS - 1,))
            silu(0, 0, True)

            def step(e, j, turn, first, second, occurrence):
                turn2, slot2 = turn + (j + 2) // SLOTS, (j + 2) % SLOTS
                rows_high(e + 2, j, False)
                weights_high(e + 2, slot2, False, turn2, range(CHUNKS - 1))
                gate_up_out(e + 1, False)
                weights_high(e + 2, slot2, False, turn2, (CHUNKS - 1,))
                y_out(e, j, second, occurrence)
                silu(e + 1, j + 1, first)

            for e in range(SLOTS):
                step(e, e, 0, e < 1, e < 2, e // 2)
            with act.Fori(1, NE // SLOTS) as g:
                for j in range(SLOTS):
                    step(g * SLOTS + j, j, g, False, False, g * (SLOTS // 2) + j // 2)
            for e in range(NE // SLOTS * SLOTS, NE):
                if e + 1 < NE:
                    gate_up_out(e + 1, False)
                y_out(e, e, False, e // 2)
                if e + 1 < NE:
                    silu(e + 1, e + 1, False)

            act.wait_ge(count_ready, 1)
            with act.If(act.value_load(mosti[0:1, 0:1], min_val=0, max_val=SEQ) > CAP):
                for t in range(NT):
                    for k in range(2):
                        act.wait_ge(o_rowsT_ps, 2 * t + k + 1)
                        act.activation(o_rowsT[:, 4 * k:4 * k + 4, P * t:P * t + P], bank[k][:, :].rearrange("p (k t) -> p k t", k=4),
                                       ACT.Copy).then_inc(o_rowsT_ready, 1)
                with act.Fori(0, NE) as e:
                    act.wait_ge(o_gu_ps, e + 1)
                    act.wait_ge(o_act_ready, e + 1)
                    for m in range(ME):
                        act.activation(o_sil[:, m, :], bank[m][:, :], ACT.Silu).then_inc(o_silu_ready, 1)

            for t in range(NT):
                normalise(t, NT + t, res[:, t, :])

        @block.vector
        def _(dve):
            n = [0]

            def link(ins):
                n[0] += 1
                ins.then_inc(dve_chain, 1)
                dve.wait_ge(dve_chain, n[0])

            for g in range(2 * NT):
                dve.wait_ge(xT_high_ready, g + 1)
                k0, cols = 4 * (g % 2), slice(P * (g // 2), P * (g // 2) + P)
                dve.tensor_tensor(xT_low[:, k0:k0 + 4, cols], bank[g % 2][:, :].rearrange("p (k t) -> p k t", k=4),
                                  xT_high[:, k0:k0 + 4, cols].bitcast(F32), ALU.subtract).then_inc(xT_low_ready, 1)
            dve.wait_ge(row_ps, 1)
            for i, bk in enumerate((4, 7)):
                dve.tensor_scalar(brow[0:HEADS, TW // 2 * i:TW // 2 * (i + 1)], bank[bk][0:HEADS, 0:TW // 2], 1.0 / SCALE, None,
                                  ALU.mult).then_inc(row_ready, 1)
            dve.wait_ge(iw_ps, 1)
            link(dve.tensor_scalar(iw[:, :, :], bank[0][:, 0:NT * HEADS].rearrange("p (t j) -> p t j", t=NT), HEADS ** -0.5, None, ALU.mult))
            def topk_round(b):
                s_b = score[:, 0:keys(b)]
                link(dve.max(m8[:, :], s_b))
                link(dve.match_replace(out=s_b, in_to_replace=m8[:, :], in_values=s_b, imm_value=TAKEN))

            def mark_kept(b):
                link(dve.tensor_scalar(keep[b][:, :], score[:, 0:keys(b)], TAKEN / 2, -BIG, ALU.is_gt, ALU.mult))
                dve.sem_inc(keep_ready, 1)

            for b in range(1, NT):
                s_b = score[:, 0:keys(b)]
                for j in range(HEADS):
                    s = score_no[(b, j)]
                    dve.wait_ge(relu_ready, s + 1)
                    r = relu[s % 4][:, 0:keys(b)]
                    if j == 0:
                        ins = dve.tensor_scalar(s_b, r, iw[:, b, 0:1], None, ALU.mult)
                    else:
                        ins = dve.scalar_tensor_tensor(out=s_b, in0=r, scalar=iw[:, b, j:j + 1], in1=s_b, op0=ALU.mult, op1=ALU.add)
                    ins.then_inc(relu_used, 1)
                    dve.wait_ge(relu_used, s + 1)
                dve.sem_inc(score_sum, 1)
                dve.wait_ge(score_masked, b)
                for r in range(TOPK // 8 if b < NT - 1 else EARLY_ROUNDS):
                    topk_round(b)
                if b < NT - 1:
                    mark_kept(b)
                if b == 2:
                    for c in range(4):
                        dve.wait_ge(v_high_ready, c + 1)
                        dve.tensor_tensor(ring_low[ring_of[V]][:, 2 * c:2 * c + 2, :], ring[ring_of[V]][:, 2 * c:2 * c + 2, :],
                                          v_high[:, 2 * c:2 * c + 2, :].bitcast(F32), ALU.subtract).then_inc(v_low_ready, 1)

            def wo_second_half_low(k):
                dve.wait_ge(wo_high_ready, k - KD // 2 + 1)
                dve.tensor_tensor(wo_low[1][:, k - KD // 2, :], wo[1][:, k - KD // 2, :], wo_high[k][:, :].bitcast(F32),
                                  ALU.subtract).then_inc(wo_low_dve, 1)

            for k in range(KD // 2, KD - 2):
                wo_second_half_low(k)
            dve.wait_ge(bias_ready, HEADS)
            dve.wait_ge(pooled_ready, NA)
            for u in range(NU + PV_LAG):
                if u < NU:
                    b, hh = units[u]
                    dve.wait_ge(qk_ps, u + 1)
                    add = bias8[:, hh, SEQ - keys(b):]
                    if b:
                        add = bm[u % 4][:, 0:keys(b)]
                        if hh % 2:
                            link(dve.tensor_tensor(add, bias8[:, hh, SEQ - keys(b):], keep[b][:, :], ALU.add))
                        else:
                            dve.wait_ge(bm_ready, (u - HEADS) // 2 + 1)
                    if u >= LG:
                        dve.wait_ge(pT_ps, u - LG + 1)
                    dve.tensor_tensor_reduce(out=lg[u % LG][:, 0:keys(b)], in0=bank[qk_bank(u)][:, 0:keys(b)], in1=add, scale=-SCALE,
                                             scalar=3e38, op0=ALU.add, op1=ALU.min, accum_out=nmx[:, u % 8:u % 8 + 1]).then_inc(logit_ready, 1)
                late_rounds = TOPK // 8 - EARLY_ROUNDS
                if u < late_rounds:
                    topk_round(NT - 1)
                elif u == late_rounds:
                    mark_kept(NT - 1)
                if u - 2 in mixes:
                    g = mixes.index(u - 2)
                    dve.wait_ge(mixed_high, g + 1)
                    dve.scalar_tensor_tensor(out=mix_low[:, :, NA + g, :], in0=bank[3 - g % 2][:, :].rearrange("p (t c) -> p t c", t=NT),
                                             scalar=pscale[:, g:g + 1], in1=mix_high[:, NA + g, :].bitcast(F32).rearrange("p (t c) -> p t c", t=NT),
                                             op0=ALU.mult, op1=ALU.subtract).then_inc(mixed_sb, 1)
                if u in (14, 15):
                    wo_second_half_low(KD - 2 + u - 14)
                if u >= PV_LAG and units[u - PV_LAG][1] == HEADS - 1:
                    b = units[u - PV_LAG][0]
                    dve.wait_ge(attn_high, b + 1)
                    cols = slice(P * b, P * b + P)
                    dve.tensor_tensor(mix_low[:, b, 0:NA, :], bank[6 + b % 2][:, :].rearrange("p (m t) -> p m t", m=NA),
                                      mix_high[:, 0:NA, cols].bitcast(F32), ALU.subtract).then_inc(attn_sb, 1)
                if split_of_wo(u) and u % 4 == 0:
                    k, cols = split_of_wo(u)
                    dve.wait_ge(wo_high_ready, KD // 2 + u // 2 - FIRST_SPLIT // 2 + 1)
                    dve.tensor_tensor(wo_low[0][:, k, cols], wo[0][:, k, cols], wo_high[k][:, cols].bitcast(F32),
                                      ALU.subtract).then_inc(wo_low_dve, 1)
                if 1 <= u <= NU:
                    dve.wait_ge(exp_ready, u)
                    if u >= 9:
                        dve.wait_ge(prob_ready, u - 8)
                    dve.reciprocal(rinv[:, (u - 1) % 8:(u - 1) % 8 + 1], rsum[:, (u - 1) % 8:(u - 1) % 8 + 1]).then_inc(rinv_ready, 1)

            def statistics(k, rows):
                for i in range(2):
                    link(dve.bn_stats(stats[:, i, :], rows[:, 512 * i:512 * i + 512]))
                link(dve.bn_aggr(mv[:, :], stats[:, :, :]))
                dve.tensor_scalar(var_e[:, :], mv[:, 1:2], EPS, None, ALU.add).then_inc(var_ready, 1)

            def factors(k):
                if k >= 1:
                    dve.wait_ge(norm_ready, k)
                dve.wait_ge(std_ready, k + 1)
                link(dve.reciprocal(rstd[:, :], std[:, :]))
                dve.tensor_scalar(nmr[:, :], mv[:, 0:1], rstd[:, 0:1], -1.0, ALU.mult, ALU.mult).then_inc(scale_ready, 1)

            def apply_gain(k, rows, gain):
                dve.wait_ge(norm_ready, k + 1)
                link(dve.tensor_tensor(rows, rows, gain, ALU.mult))
                dve.sem_inc(gain_ready, 1)

            def transposed_h(t):
                dve.wait_ge(hT_ps, t + 1)
                if t >= 2:
                    dve.wait_ge(router_ps, t - 1)
                for k in range(KD // 2, KD):
                    ins = dve.tensor_scalar(hT[t % 2][:, k, :], bank[5][:, P * (k - KD // 2):P * (k - KD // 2) + P],
                                            gT[:, k:k + 1], bT[:, k:k + 1], ALU.mult, ALU.add)
                ins.then_inc(hT_ready_dve, 1)

            def route(t):
                dve.wait_ge(router_ps, t + 1)
                ps = bank[6 + t % 2][:, 0:GROUPS + NE]
                link(dve.tensor_tensor(gl[:, t, 0:GROUPS], ps[:, 0:GROUPS], br[:, 0:GROUPS], ALU.add))
                dve.tensor_tensor(lf[:, :], ps[:, GROUPS:], br[:, GROUPS:], ALU.add).then_inc(router_sb, 1)
                dve.wait_ge(router_sb, t + 1)
                link(dve.max(gm8[:, :], gl[:, t, :]))
                link(dve.max_index(gi8[:, :], gm8[:, :], gl[:, t, :]))
                link(dve.tensor_copy(gidx[:, :], gi8[:, 0:1]))
                link(dve.tensor_scalar(pen[:, :], gid[:, :, :].rearrange("p g e -> p (g e)"), gidx[:, 0:1], -BIG, ALU.not_equal, ALU.mult))
                link(dve.tensor_tensor(lf[:, :], lf[:, :], pen[:, :], ALU.add))
                link(dve.max(em8[:, t, :], lf[:, :]))
                link(dve.max_index(ei8[:, :], em8[:, t, :], lf[:, :]))
                link(dve.tensor_copy(eidx[:, t, :], ei8[:, 0:2]))
                link(dve.tensor_tensor(hot[:, t, :, :], iota_e[:, :].unsqueeze(1).to_broadcast([P, 2, NE]),
                                       eidx[:, t, :].unsqueeze(2).to_broadcast([P, 2, NE]), ALU.is_equal))
                link(dve.tensor_tensor(hsum[:, t, :], hot[:, t, 0, :], hot[:, t, 1, :], ALU.add))
                dve.sem_inc(hot_ready, 1)
                dve.tensor_tensor(earlier[:, t + 1, :], hsum[:, t, :], earlier[:, t, :], ALU.add).then_inc(earlier_ready, 1)
                dve.wait_ge(earlier_ready, t + 1)
                dve.tensor_scalar(hot_tok[:, t, :, :], hot[:, t, :, :], tok[:, t:t + 1], None, ALU.mult).then_inc(hot_tok_ready, 1)
                link(dve.tensor_scalar(neg[:, t, 0:1], gm8[:, 0:1], -1.0, None, ALU.mult))
                link(dve.tensor_scalar(neg[:, t, 1:2], em8[:, t, 0:1], -1.0, None, ALU.mult))
                dve.sem_inc(top_ready, 1)

            dve.wait_ge(small_in, 16 * SMALLS)
            dve.wait_ge(consts_ready, 2)
            for t in range(NT):
                if t >= 1:
                    transposed_h(t - 1)
                dve.wait_ge(out_ps, t + 1)
                dve.wait_ge(x_again_in[t % 2], 32 * (t // 2 + 1))
                for i in range(2):
                    hv = h[:, t, 512 * i:512 * i + 512]
                    link(dve.scalar_tensor_tensor(out=hv, in0=x_again[t % 2][i][:, :], scalar=ALPHA, in1=bank[(2 if t % 2 == 0 else 0) + i][:, :],
                                                  op0=ALU.mult, op1=ALU.add))
                dve.sem_inc(res_ready, 1)
                statistics(t, h[:, t, :])
                factors(t)
                if t >= 1:
                    route(t - 1)

            def place(t0, t1, ps):
                ranks_ps = ps.rearrange("p (t e) -> p t e", e=NE)
                for c in range(2):
                    ins = dve.scalar_tensor_tensor(out=hot_rank[:, t0:t1, c, :], in0=ranks_ps, scalar=1.0, in1=hot[:, t0:t1, c, :],
                                                   op0=ALU.add, op1=ALU.mult)
                link(ins)
                link(dve.tensor_reduce(out=rk[:, t0:t1, :], in_=hot_rank[:, t0:t1, :, :], axis=AX.X, op=ALU.add))
                for t in range(t0, t1):
                    ins = dve.tensor_tensor(at_rank[:, t, :, :], iota_r[:, :].unsqueeze(1).to_broadcast([P, 2, CAP]),
                                            rk[:, t, :].unsqueeze(2).to_broadcast([P, 2, CAP]), ALU.is_equal)
                link(ins)
                dve.sem_inc(at_rank_ready, 1)
                dve.tensor_tensor(rank1[:, t0:t1, :], hot_rank[:, t0:t1, 0, :], hot_rank[:, t0:t1, 1, :], ALU.add).then_inc(rank1_ready, 1)

            dve.wait_ge(rank_ps, 1)
            place(0, NT - 1, bank[3][:, 0:NE * (NT - 1)])
            transposed_h(NT - 1)
            route(NT - 1)
            dve.wait_ge(rank_ps, 2)
            place(NT - 1, NT, bank[0][:, 0:NE])
            dve.wait_ge(list_ps, 1)
            dve.tensor_copy(lsti[0:CAP, :], bank[2][0:CAP, 0:NE]).then_inc(list_ready, 1)
            def gated(e, j, first):
                i = j % 2
                dve.wait_ge(silu_ready, e + 1)
                if not first:
                    dve.wait_ge(y_ps, e - 1)
                dve.tensor_tensor(act_e[i][:, :, :], bank[2][:, ME * CAP:2 * ME * CAP].rearrange("p (m t) -> p m t", m=ME),
                                  sil[i][:, :, :], ALU.mult).then_inc(act_ready, 1)

            def y_out(e, j, first, occurrence):
                i = j % 2
                dve.wait_ge(y_ps, e + 1)
                if not first:
                    dve.wait_ge(y_stored[i], occurrence * 16)
                dve.tensor_copy(ye[i][0:CAP, 0:512], bank[4 + 2 * i][0:CAP, :]).then_inc(y_lo, 1)

            def rows_low(e, j, first):
                i = j % 2
                dve.wait_ge(xe_high, e + 1)
                dve.tensor_tensor(xeT[i][:, :, 1, :], bank[0][:, 0:KD * CAP].rearrange("p (k t) -> p k t", k=KD),
                                  xeT[i][:, :, 0, :].bitcast(F32), ALU.subtract).then_inc(xe_low, 1)

            def weights_low(e, j):
                for c in range(CHUNKS):
                    dve.wait_ge(w_high_ready, CHUNKS * e + c + 1)
                    dve.tensor_tensor(w_low[j][:, c, :, :], piece(j, c), w_high[:, c, :, :].bitcast(F32),
                                      ALU.subtract).then_inc(w_low_ready, 1)

            weights_low(0, 0)
            rows_low(0, 0, True)
            rows_low(1, 1, True)
            dve.wait_ge(count_ps, 1)
            link(dve.max(m8[:, :], bank[3][:, 0:NE]))
            dve.tensor_copy(mosti[:, :], m8[:, 0:1]).then_inc(count_ready, 1)
            link(dve.tensor_scalar(fits[:, :, :], rk[:, :, :], float(CAP), None, ALU.is_le))
            link(dve.tensor_scalar(rk[:, :, :], rk[:, :, :], float(CAP), -1.0, ALU.min, ALU.add))
            link(dve.scalar_tensor_tensor(out=slotf[:, :, :], in0=eidx[:, :, :], scalar=float(CAP), in1=rk[:, :, :], op0=ALU.mult, op1=ALU.add))
            dve.tensor_copy(sloti[:, :, :], slotf[:, :, :]).then_inc(slot_ready, 1)
            dve.wait_ge(gate_exp, NT)
            link(dve.tensor_scalar(wt[:, :, 0], zs[:, :, 1], 1.0, None, ALU.add))
            link(dve.tensor_tensor(wt[:, :, 0], wt[:, :, 0], zs[:, :, 0], ALU.mult))
            link(dve.reciprocal(wt[:, :, 0], wt[:, :, 0]))
            link(dve.tensor_tensor(wt[:, :, 1], wt[:, :, 0], zs[:, :, 1], ALU.mult))
            link(dve.tensor_tensor(wfit[:, :, :], wt[:, :, :], fits[:, :, :], ALU.mult))
            weights_low(1, 1)
            gated(0, 0, True)
            for e in range(SLOTS):
                rows_low(e + 2, e, False)
                weights_low(e + 2, (e + 2) % SLOTS)
                y_out(e, e, e < 2, e // 2)
                gated(e + 1, e + 1, e < 1)
            with dve.Fori(1, NE // SLOTS) as g:
                for j in range(SLOTS):
                    rows_low(g * SLOTS + j + 2, j, False)
                    weights_low(g * SLOTS + j + 2, (j + 2) % SLOTS)
                    y_out(g * SLOTS + j, j, False, g * (SLOTS // 2) + j // 2)
                    gated(g * SLOTS + j + 1, j + 1, False)
            for e in range(NE // SLOTS * SLOTS, NE):
                y_out(e, e % SLOTS, False, e // 2)
                if e + 1 < NE:
                    gated(e + 1, e + 1, False)

            with dve.If(dve.value_load(mosti[0:1, 0:1], min_val=0, max_val=SEQ) > CAP):
                dve.wait_ge(rank1_ready, 2)
                for t in range(NT):
                    dve.tensor_scalar(scr[:, :], hot[:, t, 0, :], wt[:, t, 0:1], None, ALU.mult).then_inc(o_chain, 1)
                    dve.wait_ge(o_chain, 3 * t + 1)
                    dve.scalar_tensor_tensor(out=scr[:, :], in0=hot[:, t, 1, :], scalar=wt[:, t, 1:2], in1=scr[:, :],
                                             op0=ALU.mult, op1=ALU.add).then_inc(o_chain, 1)
                    dve.wait_ge(o_chain, 3 * t + 2)
                    dve.scalar_tensor_tensor(out=over[:, t, :], in0=rank1[:, t, :], scalar=float(CAP), in1=scr[:, :],
                                             op0=ALU.is_gt, op1=ALU.mult).then_inc(o_chain, 1)
                    dve.wait_ge(o_chain, 3 * t + 3)
                dve.wait_ge(res_sum, NT)
                dve.sem_inc(o_added, 1)
                dve.sem_inc(o_act_ready, 1)
                with dve.Fori(0, NE) as e:
                    dve.wait_ge(o_added, e * NT + 1)
                    dve.tensor_copy(over_e[:, :], over[:, :, bass.ds(e, 1)].rearrange("p t o -> p (t o)")).then_inc(o_weight_ready, 1)
                    dve.wait_ge(o_silu_ready, e * ME + ME)
                    dve.wait_ge(o_y_ps, e * NT + 1)
                    for m in range(ME):
                        ins = dve.tensor_tensor(o_act[:, m, :], bank[2 + m][:, :], o_sil[:, m, :], ALU.mult)
                    ins.then_inc(o_act_ready, 1)
                    dve.wait_ge(o_weight_ready, e + 1)
                    for t in range(NT):
                        dve.wait_ge(o_y_ps, e * NT + t + 2)
                        for c in range(2):
                            hv = res[:, t, 512 * c:512 * c + 512]
                            ins = dve.scalar_tensor_tensor(out=hv, in0=bank[4 + 2 * (t % 2) + c][:, :], scalar=over_e[:, t:t + 1], in1=hv,
                                                           op0=ALU.mult, op1=ALU.add)
                        ins.then_inc(o_added, 1)
            for t in range(NT):
                dve.wait_ge(y_gathered[t], 32)
                dve.wait_ge(res_sum, NT)
                for c in range(2):
                    link(dve.scalar_tensor_tensor(out=res[:, t, :], in0=yg[t][c][:, :], scalar=wfit[:, t, c:c + 1],
                                                  in1=res[:, t, :], op0=ALU.mult, op1=ALU.add))
                if t == 0:
                    dve.wait_ge(ln2_in, 32)
                statistics(NT + t, res[:, t, :])
                factors(NT + t)
            apply_gain(2 * NT - 1, res[:, NT - 1, :], g2[:, :])
            dve.tensor_tensor(res[:, NT - 1, 0:D // 2], res[:, NT - 1, 0:D // 2], b2[:, 0:D // 2], ALU.add).then_inc(out_ready, 1)

        @block.tensor
        def _(pe):
            pe.wait_ge(consts_ready, 1)
            for g in range(2 * NT):
                t, k0 = g // 2, 4 * (g % 2)
                if g % 2 == 0:
                    pe.wait_ge(x_in[t], 16)
                if g >= 2:
                    pe.wait_ge(xT_low_ready, g - 1)
                for k in range(4):
                    ins = pe.transpose(bank[g % 2][:, P * k:P * k + P], h[:, t, P * (k0 + k):P * (k0 + k) + P], ident[:, :])
                ins.then_inc(xT_ps, 1)
            pe.wait_ge(onehot_in, 32)
            for i, bk in enumerate((4, 7)):
                ins = pe.matmul(bank[bk][0:HEADS, 0:TW // 2], relb[0:BUCKETS, :], hot_c[0:BUCKETS, TW // 2 * i:TW // 2 * (i + 1)], start=True, stop=True)
            ins.then_inc(row_ps, 1)
            pe.wait_ge(xT_low_ready, 2 * NT)

            def score_unit(b, j):
                s = score_no[(b, j)]
                if s == 0:
                    pe.wait_ge(proj_sb, 5)
                if s >= 2:
                    pe.wait_ge(relu_ready, s - 1)
                pe.matmul(bank[5 + s % 2][:, 0:keys(b)], iqT[half(j), j // 2, P * b:P * b + P], ikT[half(j), 0:keys(b)],
                          start=True, stop=True).then_inc(dots_ps, 1)

            pending = []
            for item in front:
                if item[0] == "tile":
                    i = item[1]
                    kind, m = tiles[i]
                    if i >= 2:
                        pe.wait_ge(proj_sb, i - 1)
                    if (kind, m) == (V, 0):
                        pe.wait_ge(v_low_ready, 4)
                    elif kind != V:
                        pe.wait_ge(wt_high_ready, i + 1)
                    rows_out = HD + HEADS if kind == "ik" else P
                    for s, (w_part, xT_part) in enumerate((("high", xT_high), ("high", xT_low), ("low", xT_high))):
                        if s and pending:
                            score_unit(*pending.pop(0))
                        if w_part == "low" and kind != V:
                            pe.wait_ge(wt_low_ready, i + 1)
                        for k in range(KD):
                            if kind == V:
                                lhsT = xT_part[:, k, P * m:P * m + P]
                                rhs = v_high[:, k, :] if w_part == "high" else ring_low[ring_of[V]][:, k, :]
                            else:
                                raw, high, low = tile_parts(i)
                                lhsT, rhs = (high if w_part == "high" else low)[:, k, :], xT_part[:, k, :]
                            ins = pe.matmul(bank[2 + i % 2][0:rows_out, :], lhsT, rhs, start=(s, k) == (0, 0), stop=(s, k) == (2, KD - 1))
                    ins.then_inc(proj_ps, 1)
                    while pending:
                        score_unit(*pending.pop(0))
                elif item[0] == "iw":
                    pe.wait_ge(proj_sb, 1)
                    for t in range(NT):
                        ins = pe.transpose(bank[0][:, HEADS * t:HEADS * t + HEADS], iwT[0:HEADS, P * t:P * t + P], ident[0:HEADS, 0:HEADS])
                    ins.then_inc(iw_ps, 1)
                else:
                    pending.append(item[1:])

            def v_passes(i, piece):
                m = tiles[i][1]
                for s_k in range(6 * piece, 6 * piece + 6):
                    s, k = divmod(s_k, KD)
                    lhsT = (xT_high, xT_low, xT_high)[s][:, k, P * m:P * m + P]
                    rhs = (v_high[:, k, :], v_high[:, k, :], ring_low[ring_of[V]][:, k, :])[s]
                    ins = pe.matmul(bank[2 + i % 2][:, :], lhsT, rhs, start=s_k == 0, stop=s_k == 3 * KD - 1)
                if piece == 3:
                    ins.then_inc(proj_ps, 1)

            def mix_channels(g):
                if g < 2:
                    pe.wait_ge(proj_sb, LATE + g + 1)
                else:
                    pe.wait_ge(mixed_sb, g - 1)
                if g == 0:
                    pe.wait_ge(small_in, 16 * SMALLS)
                pe.wait_ge(pooled_ready, g + 1)
                pe.matmul(bank[3 - g % 2][:, :], wpool[:, g, :], uT[:, g, PAD:], start=True, stop=True).then_inc(mixed_ps, 1)

            pe.wait_ge(relu_ready, len(score_no))
            pe.wait_ge(proj_sb, LATE)
            for u in range(NU + PV_LAG):
                if u < NU:
                    b, hh = units[u]
                    if u >= 2:
                        pe.wait_ge(logit_ready, u - 1 if u < 22 else u - QKB + 1)
                    if u == 22:
                        pe.wait_ge(mixed_sb, NA)
                    pe.matmul(bank[qk_bank(u)][:, 0:keys(b)], qT[half(hh), hh // 2, P * b:P * b + P], kT[half(hh), hh // 2, 0:keys(b)],
                              start=True, stop=True).then_inc(qk_ps, 1)
                if u < 8:
                    v_passes(LATE + u // 4, u % 4)
                elif u in mixes:
                    mix_channels(mixes.index(u))
                if 0 <= u - T_LAG < NU:
                    w = u - T_LAG
                    b, hh = units[w]
                    pe.wait_ge(prob_ready, w + 1)
                    if w >= 2:
                        pe.wait_ge(pT_ready, w - 1)
                    for k in range(b + 1):
                        ins = pe.transpose(bank[4 + w % 2][:, P * k:P * k + P], lg[w % LG][:, P * k:P * k + P], ident[:, :])
                    ins.then_inc(pT_ps, 1)
                if u >= PV_LAG:
                    w = u - PV_LAG
                    b, hh = units[w]
                    pe.wait_ge(pT_ready, w + 1)
                    if hh == 0 and b >= 2:
                        pe.wait_ge(attn_sb, b - 1)
                    for k in range(b + 1):
                        ins = pe.matmul(bank[6 + b % 2][half(hh), P * (hh // 2):P * (hh // 2) + P], v_sb[:, k, HD * hh:HD * hh + HD],
                                        pT[w % 2][:, P * k:P * k + P], start=k == 0, stop=k == b)
                    ins.then_inc(pv_ps, 1)
            pe.wait_ge(mixed_sb, NA)
            pe.wait_ge(attn_sb, NT)
            pe.wait_ge(wo_low_dve, KD // 2 + KD // 2)
            pe.wait_ge(wo_low_pool, KD // 2)

            def transpose_h(t):
                pe.wait_ge(norm_ready, t + 1)
                if t >= 1:
                    pe.wait_ge(hT_ready, t)
                    pe.wait_ge(hT_ready_dve, t)
                for k in range(KD):
                    ins = pe.transpose(bank[4 + k // 4][:, P * (k % 4):P * (k % 4) + P], h[:, t, P * k:P * k + P], ident[:, :])
                ins.then_inc(hT_ps, 1)

            def router(t):
                pe.wait_ge(hT_ready, t + 1)
                pe.wait_ge(hT_ready_dve, t + 1)
                if t >= 2:
                    pe.wait_ge(router_sb, t - 1)
                for k in range(KD):
                    ins = pe.matmul(bank[6 + t % 2][:, 0:GROUPS + NE], hT[t % 2][:, k, :], wr[:, k, :], start=k == 0, stop=k == KD - 1)
                ins.then_inc(router_ps, 1)

            for t in range(NT):
                if t >= 2:
                    pe.wait_ge(res_ready, t - 1)
                for i in range(2):
                    for k in range(KD):
                        cols, cols_out = slice(P * t, P * t + P), slice(512 * i, 512 * i + 512)
                        w_low_k = wo_low[k // 4][:, k % 4, cols_out]
                        parts = ((mix_high[:, k, cols], wo_high[k][:, cols_out]), (mix_low[:, t, k, :], wo_high[k][:, cols_out]), (mix_high[:, k, cols], w_low_k))
                        if t >= 1 and (i, k) == (1, 3):
                            transpose_h(t - 1)
                        for s, (lhsT, rhs) in enumerate(parts):
                            ins = pe.matmul(bank[(2 if t % 2 == 0 else 0) + i][:, :], lhsT, rhs, start=(k, s) == (0, 0), stop=(k, s) == (KD - 1, 2))
                ins.then_inc(out_ps, 1)
                if t >= 1:
                    router(t - 1)

            def ranks(t0, t1, out):
                pe.wait_ge(hot_ready, t1)
                pe.matmul(out, tri[:, :], hsum[:, t0:t1, :], start=True, stop=False)
                return pe.matmul(out, ones[:, :], earlier[:, t0:t1, :], start=False, stop=True)

            def lists(t0, t1):
                for t in range(t0, t1):
                    for c in range(2):
                        ins = pe.matmul(bank[2][0:CAP, 0:NE], at_rank[:, t, c, :], hot_tok[:, t, c, :], start=(t, c) == (0, 0), stop=(t, c) == (NT - 1, 1))
                return ins

            transpose_h(NT - 1)
            pe.wait_ge(res_ready, NT)
            pe.wait_ge(earlier_ready, NT - 1)
            ranks(0, NT - 1, bank[3][:, 0:NE * (NT - 1)]).then_inc(rank_ps, 1)
            router(NT - 1)
            pe.wait_ge(hot_tok_ready, NT - 1)
            pe.wait_ge(at_rank_ready, 1)
            lists(0, NT - 1)
            ranks(NT - 1, NT, bank[0][:, 0:NE]).then_inc(rank_ps, 1)
            pe.wait_ge(earlier_ready, NT)
            pe.matmul(bank[3][:, 0:NE], ones[:, :], earlier[:, NT, :], start=True, stop=True).then_inc(count_ps, 1)
            pe.wait_ge(hot_tok_ready, NT)
            pe.wait_ge(at_rank_ready, 2)
            lists(NT - 1, NT).then_inc(list_ps, 1)

            def rows(e, j, first, occurrence):
                i = j % 2
                pe.wait_ge(gathered[i], occurrence * 16 + 16)
                if not first:
                    pe.wait_ge(xe_low, e)
                pe.sem_inc(rows_begun, 1)
                xv = xe[i][0:CAP, :].rearrange("t (p k) -> t k p", k=KD)
                for k in range(KD):
                    ins = pe.transpose(bank[0][:, CAP * k:CAP * k + CAP], xv[:, k, :], ident[0:CAP, 0:CAP])
                ins.then_inc(xeT_ps, 1)

            def gate_up(e, j, first):
                i = j % 2
                pe.wait_ge(xe_low, e + 1)
                if not first:
                    pe.wait_ge(gu_out, e)
                for c in range(CHUNKS):
                    pe.wait_ge(w_low_ready, CHUNKS * e + c + 1)
                    s, k0 = c * KC // KD, c * KC % KD
                    for part in (w_low[j], w_high):
                        for k in range(KC):
                            ins = pe.matmul(bank[1][0:2 * CAP, DE * s:DE * s + DE], xeT[i][:, k0 + k, :, :], part[:, c, k, :],
                                            start=k0 + k == 0 and part is not w_high, stop=k0 + k == KD - 1 and part is w_high)
                    ins.then_inc(piece_done, 1)

            def fold_gate_up(e, first):
                pe.wait_ge(gu_out, e + 1)
                if not first:
                    pe.wait_ge(act_ready, e)
                for m in range(2 * ME):
                    ins = pe.matmul(bank[2][:, CAP * m:CAP * m + CAP], gu_sb[0:2 * CAP, P * m:P * m + P], fold[0:2 * CAP, :], start=True, stop=True)
                ins.then_inc(gu_ps, 1)

            def down(e, j, first, turn):
                i = j % 2
                pe.wait_ge(down_in_slot[j], turn * 16 + 16)
                pe.wait_ge(act_ready, e + 1)
                if not first:
                    pe.wait_ge(y_lo, e - 1)
                    pe.wait_ge(y_hi, e - 1)
                for c in range(2):
                    for m in range(ME):
                        ins = pe.matmul(bank[4 + 2 * i + c][0:CAP, :], act_e[i][:, m, :], wd[j][:, m, 512 * c:512 * c + 512], start=m == 0, stop=m == ME - 1)
                ins.then_inc(y_ps, 1)

            rows(0, 0, True, 0)
            rows(1, 1, False, 0)
            gate_up(0, 0, True)
            fold_gate_up(0, True)
            for e in range(SLOTS):
                rows(e + 2, e + 2, False, (e + 2) // 2)
                gate_up(e + 1, (e + 1) % SLOTS, False)
                down(e, e, e < 2, 0)
                fold_gate_up(e + 1, False)
            with pe.Fori(1, NE // SLOTS) as g:
                for j in range(SLOTS):
                    rows(g * SLOTS + j + 2, j, False, g * (SLOTS // 2) + j // 2 + 1)
                    gate_up(g * SLOTS + j + 1, (j + 1) % SLOTS, False)
                    down(g * SLOTS + j, j, False, g)
                    fold_gate_up(g * SLOTS + j + 1, False)
            for e in range(NE // SLOTS * SLOTS, NE):
                if e + 1 < NE:
                    gate_up(e + 1, (e + 1) % SLOTS, False)
                down(e, e % SLOTS, False, e // SLOTS)
                if e + 1 < NE:
                    fold_gate_up(e + 1, False)

            pe.wait_ge(count_ready, 1)
            with pe.If(pe.value_load(mosti[0:1, 0:1], min_val=0, max_val=SEQ) > CAP):
                pe.wait_ge(o_rows_in, 16)
                pe.wait_ge(y_lo, NE)
                pe.wait_ge(y_hi, NE)
                for t in range(NT):
                    for k in range(2):
                        if t:
                            pe.wait_ge(o_rowsT_ready, 2 * t + k - 1)
                        for q in range(4):
                            ins = pe.transpose(bank[k][:, P * q:P * q + P], o_rows[:, t, :].rearrange("p (c k) -> p k c", k=KD)[:, 4 * k + q, :], ident[:, :])
                        ins.then_inc(o_rowsT_ps, 1)
                pe.wait_ge(o_rowsT_ready, 2 * NT)
                pe.sem_inc(o_y_ps, 1)
                with pe.Fori(0, NE) as e:
                    pe.wait_ge(o_w_in, e * 48 + 48)
                    pe.wait_ge(o_act_ready, e + 1)
                    pe.wait_ge(o_added, e * NT + 1)
                    for s, w in enumerate((wg, wu)):
                        for m in range(ME):
                            for k in range(KD):
                                ins = pe.matmul(bank[2 * s + m][:, :], w[OSLOT][:, k, P * m:P * m + P], o_rowsT[:, k, :], start=k == 0, stop=k == KD - 1)
                    ins.then_inc(o_gu_ps, 1)
                    pe.wait_ge(o_act_ready, e + 2)
                    for t in range(NT):
                        if t >= 2:
                            pe.wait_ge(o_added, e * NT + t)
                        for c in range(2):
                            for m in range(ME):
                                ins = pe.matmul(bank[4 + 2 * (t % 2) + c][:, :], o_act[:, m, P * t:P * t + P], wd[OSLOT][:, m, 512 * c:512 * c + 512],
                                                start=m == 0, stop=m == ME - 1)
                        ins.then_inc(o_y_ps, 1)


_INS = ['x', 'w_in', 'w_pool', 'pool_scale', 'w_out', 'rel_bias', 'ln1_g', 'ln1_b', 'w_r1', 'b_r1', 'w_r2', 'b_r2',
        'w_gate', 'w_up', 'w_down', 'ln2_g', 'ln2_b']


def kernel(**inputs):
    import numpy as _np
    import concourse.bacc as _bacc
    from concourse import mybir as _mybir
    from concourse.bass_utils import run_bass_kernel_spmd as _run

    nc = _bacc.Bacc("TRN2", target_bir_lowering=False, num_devices=1)
    arrays, args = {}, []
    given = {name: inputs[name] for name in _INS}
    given["onehot"] = bucket_onehot()
    given["headfix"] = head_counts()
    for name, a in given.items():
        a = _np.ascontiguousarray(a)
        arrays[f"in_{name}_dram"] = a
        args.append(nc.dram_tensor(f"in_{name}_dram", a.shape, _mybir.dt.from_np(a.dtype), kind="ExternalInput").ap())
    args.append(nc.dram_tensor("out_0_dram", (1, SEQ, D), _mybir.dt.float32, kind="ExternalOutput").ap())
    layer_kernel(nc, *args)
    r = _run(nc, [arrays], core_ids=[0])
    return r.results[0]["out_0_dram"]
```
